# Optimizing a Trainium2 kernel written in Bass

```python
import math
import jax, jax.numpy as jnp
from jax import lax
import numpy as np

D_MODEL = 1024
BATCH = 1
SEQ = 2048
DEPTH = 1
DEC_BATCH = 8
DEC_SEQ = 8
PAST_LEN = 16384
PAGE_SIZE = 128

HEAD_DIM = D_MODEL // 16
M_HEADS = 6
G_HEADS = 6
H_HEADS = 4
M_W = M_HEADS * HEAD_DIM
G_W = G_HEADS * HEAD_DIM
H_W = H_HEADS * HEAD_DIM
D_MIX = M_W + G_W + H_W
CONV_W = 4
D_FF = 4 * D_MODEL
CHUNK = 64
EPS = 1e-6
SPLITS = (M_W, M_W, M_W, M_W, M_HEADS, M_HEADS,
          3 * G_W, G_W, G_HEADS, G_HEADS,
          H_W, H_W, H_W, H_W)
P_IN = 4 * M_W + 2 * M_HEADS + 4 * G_W + 2 * G_HEADS + 4 * H_W

kernel_name = 'hybrid_mlstm_gdn_hgrn2_step'

F32 = jnp.float32

def rmsnorm(x, w):
    xf = x.astype(F32)
    y = xf * lax.rsqrt(jnp.mean(xf * xf, axis=-1, keepdims=True) + EPS)
    return (y * w.astype(F32)).astype(x.dtype)

def head_rmsnorm(h, w):
    y = h * lax.rsqrt(jnp.mean(h * h, axis=-1, keepdims=True) + EPS)
    return y.reshape(h.shape[:2] + (-1,)) * w.astype(F32)

def l2norm(x):
    return x * lax.rsqrt(jnp.sum(x * x, axis=-1, keepdims=True) + EPS)

def heads(a, n):
    return a.reshape(a.shape[:-1] + (n, a.shape[-1] // n))

def split_cols(z):
    idx = np.cumsum(np.array(SPLITS))[:-1].tolist()
    return jnp.split(z, idx, axis=-1)

def to_chunks(a, c):
    b, l = a.shape[:2]
    return jnp.swapaxes(a.reshape((b, l // c, c) + a.shape[2:]), 0, 1)

def from_chunks(a):
    a = jnp.swapaxes(a, 0, 1)
    return a.reshape((a.shape[0], a.shape[1] * a.shape[2]) + a.shape[3:])

def mlstm_scan(q, k, v, ig, lf, C0, n0, m0):
    L = q.shape[1]
    c = math.gcd(L, CHUNK)
    causal = jnp.tril(jnp.ones((c, c), dtype=bool))

    def step(carry, inp):
        C, n, m = carry
        qc, kc, vc, igc, lfc = inp
        b = jnp.cumsum(lfc, axis=1)
        dmat = b[:, :, None, :] - b[:, None, :, :] + igc[:, None, :, :]
        dmat = jnp.where(causal[None, :, :, None], dmat, -jnp.inf)
        inter = b + m[:, None, :]
        m_t = jnp.maximum(inter, jnp.max(dmat, axis=2))
        w = jnp.exp(dmat - m_t[:, :, None, :])
        wi = jnp.exp(inter - m_t)
        wqk = w * jnp.einsum('bthd,bshd->btsh', qc, kc)
        num = jnp.einsum('btsh,bshd->bthd', wqk, vc) + wi[..., None] * jnp.einsum('bthk,bhkv->bthv', qc, C)
        den = jnp.sum(wqk, axis=2) + wi * jnp.einsum('bthk,bhk->bth', qc, n)
        h = num / jnp.maximum(jnp.abs(den), 1.0)[..., None]
        m_new = m_t[:, -1]
        ws = jnp.exp(b[:, -1:, :] - b + igc - m_new[:, None, :])
        decay = jnp.exp(b[:, -1] + m - m_new)
        C_new = decay[..., None, None] * C + jnp.einsum('bsh,bshk,bshv->bhkv', ws, kc, vc)
        n_new = decay[..., None] * n + jnp.einsum('bsh,bshk->bhk', ws, kc)
        return (C_new, n_new, m_new), h

    xs = (to_chunks(q, c), to_chunks(k, c), to_chunks(v, c), to_chunks(ig, c), to_chunks(lf, c))
    (C1, n1, m1), h = lax.scan(step, (C0, n0, m0), xs)
    return from_chunks(h), C1, n1, m1

def gdn_scan(q, k, v, beta, lg, S0):
    L = q.shape[1]
    c = math.gcd(L, CHUNK)
    strict = jnp.tril(jnp.ones((c, c), dtype=bool), -1)
    incl = jnp.tril(jnp.ones((c, c), dtype=bool))
    eye = jnp.eye(c, dtype=F32)

    def step(S, inp):
        qc, kc, vc, bc, lgc = inp
        qh = jnp.swapaxes(qc, 1, 2)
        kh = jnp.swapaxes(kc, 1, 2)
        vh = jnp.swapaxes(vc, 1, 2)
        bh = jnp.swapaxes(bc, 1, 2)
        g = jnp.cumsum(jnp.swapaxes(lgc, 1, 2), axis=-1)
        diff = g[..., :, None] - g[..., None, :]
        kb = kh * bh[..., None]
        lmat = jnp.where(strict, jnp.einsum('bhtk,bhsk->bhts', kb, kh) * jnp.exp(jnp.where(strict, diff, 0.0)), 0.0)
        rhs = jnp.concatenate([vh * bh[..., None], kb * jnp.exp(g)[..., None]], axis=-1)
        sol = lax.linalg.triangular_solve(eye + lmat, rhs, left_side=True, lower=True, unit_diagonal=True)
        dv = vh.shape[-1]
        u = sol[..., :dv]
        wk = sol[..., dv:]
        v_new = u - jnp.einsum('bhtk,bhkv->bhtv', wk, S)
        attn = jnp.where(incl, jnp.einsum('bhtk,bhsk->bhts', qh, kh) * jnp.exp(jnp.where(incl, diff, 0.0)), 0.0)
        o = jnp.einsum('bhtk,bhkv->bhtv', qh * jnp.exp(g)[..., None], S) + jnp.einsum('bhts,bhsv->bhtv', attn, v_new)
        gl = g[..., -1]
        S_new = S * jnp.exp(gl)[..., None, None] + jnp.einsum('bhsk,bhsv->bhkv', kh * jnp.exp(gl[..., None] - g)[..., None], v_new)
        return S_new, jnp.swapaxes(o, 1, 2)

    xs = (to_chunks(q, c), to_chunks(k, c), to_chunks(v, c), to_chunks(beta, c), to_chunks(lg, c))
    S1, o = lax.scan(step, S0, xs)
    return from_chunks(o), S1

def hgrn_scan(q, k, v, lf, S0):
    L = q.shape[1]
    c = math.gcd(L, CHUNK)
    incl = jnp.tril(jnp.ones((c, c), dtype=bool))

    def step(S, inp):
        qc, kc, vc, lfc = inp
        G = jnp.cumsum(lfc, axis=1)
        diff = jnp.where(incl[None, :, :, None, None], G[:, :, None] - G[:, None, :], -jnp.inf)
        attn = jnp.einsum('bthk,bshk,btshk->bhts', qc, kc, jnp.exp(diff))
        o = jnp.einsum('bthk,bhkv->bthv', qc * jnp.exp(G), S) + jnp.einsum('bhts,bshv->bthv', attn, vc)
        Gl = G[:, -1]
        S_new = jnp.exp(Gl)[..., None] * S + jnp.einsum('bshk,bshv->bhkv', kc * jnp.exp(Gl[:, None] - G), vc)
        return S_new, o

    xs = (to_chunks(q, c), to_chunks(k, c), to_chunks(v, c), to_chunks(lf, c))
    S1, o = lax.scan(step, S0, xs)
    return from_chunks(o), S1

def mixer(h, w_in, b_in, f_bias, conv_w, A_log, dt_bias, lb, out_norm, w_out, st):
    C0, n0, m0, Sg0, buf0, Sh0 = st
    L = h.shape[1]
    z = (h @ w_in + b_in).astype(F32)
    mq, mk, mv, mo, mi, mf, gqkv, gg, gb, ga, hq, hf, hi, hg = split_cols(z)
    hm, C1, n1, m1 = mlstm_scan(heads(mq, M_HEADS), heads(mk, M_HEADS) * HEAD_DIM ** -0.5, heads(mv, M_HEADS),
                                mi, jax.nn.log_sigmoid(mf + f_bias.astype(F32)),
                                C0.astype(F32), n0.astype(F32), m0.astype(F32))
    ym = head_rmsnorm(hm, out_norm[:M_W]) * jax.nn.sigmoid(mo)
    xc = jnp.concatenate([buf0.astype(F32), gqkv], axis=1)
    cw = conv_w.astype(F32)
    conv = jax.nn.silu(sum(cw[j] * xc[:, j:j + L] for j in range(CONV_W)))
    buf1 = xc[:, L:]
    gq, gk, gv = jnp.split(conv, 3, axis=-1)
    gq = l2norm(heads(gq, G_HEADS)) * HEAD_DIM ** -0.5
    gk = l2norm(heads(gk, G_HEADS))
    beta = jax.nn.sigmoid(gb)
    lg = -jnp.exp(A_log.astype(F32)) * jax.nn.softplus(ga + dt_bias.astype(F32))
    hgd, Sg1 = gdn_scan(gq, gk, heads(gv, G_HEADS), beta, lg, Sg0.astype(F32))
    yg = head_rmsnorm(hgd, out_norm[M_W:M_W + G_W]) * jax.nn.silu(gg)
    lf = jnp.logaddexp(jnp.log(lb), jnp.log1p(-lb) + jax.nn.log_sigmoid(hf))
    kk = (1.0 - lb) * jax.nn.sigmoid(-hf)
    hh, Sh1 = hgrn_scan(heads(hq, H_HEADS), heads(kk, H_HEADS), heads(hi, H_HEADS), heads(lf, H_HEADS), Sh0.astype(F32))
    yh = head_rmsnorm(hh, out_norm[M_W + G_W:]) * jax.nn.silu(hg)
    y = jnp.concatenate([ym, yg, yh], axis=-1).astype(h.dtype) @ w_out
    return y, (C1, n1, m1, Sg1, buf1, Sh1)

def trunk(x, c, states, params):
    (w_ada, b_ada, norm_pre_mix, norm_post_mix, w_in, b_in, mlstm_f_bias, gdn_conv_w, gdn_A_log,
     gdn_dt_bias, hgrn_lb_logits, mix_out_norm, w_out, norm_pre_ffn, norm_post_ffn, w_ff1, w_ff2) = params
    lb_all = jnp.cumsum(jax.nn.softmax(hgrn_lb_logits.astype(F32), axis=0), axis=0)
    lb_all = lb_all - lb_all[0:1]
    new = ([], [], [], [], [], [])
    for l in range(DEPTH):
        st = (states[0][l], states[1][l], states[2][l], states[3][l], states[4][l], states[5][l])
        mod = (c @ w_ada[l] + b_ada[l])[:, None, :]
        sh1, sc1, g1, sh2, sc2, g2 = jnp.split(mod, 6, axis=-1)
        h = rmsnorm(x, norm_pre_mix[l]) * (1 + sc1) + sh1
        y, st1 = mixer(h, w_in[l], b_in[l], mlstm_f_bias[l], gdn_conv_w[l], gdn_A_log[l], gdn_dt_bias[l],
                       lb_all[l], mix_out_norm[l], w_out[l], st)
        x = x + g1 * rmsnorm(y, norm_post_mix[l])
        h = rmsnorm(x, norm_pre_ffn[l]) * (1 + sc2) + sh2
        f = jnp.square(jax.nn.relu(h @ w_ff1[l])) @ w_ff2[l]
        x = x + g2 * rmsnorm(f, norm_post_ffn[l])
        for lst, s in zip(new, st1):
            lst.append(s)
    return x, tuple(jnp.stack(s) for s in new)

def setup_inputs(seed: int = 0) -> dict:
    key = jax.random.key(seed)
    ks = jax.random.split(key, 32)

    def nrm(k, shape, s):
        return jax.random.normal(k, shape, F32) * s

    def gain(k, shape):
        return 1.0 + 0.02 * jax.random.normal(k, shape, F32)

    dt = jnp.exp(jax.random.uniform(ks[19], (DEPTH, G_HEADS), F32, math.log(1e-3), math.log(1e-1)))
    return {
        'x_prompt': nrm(ks[0], (BATCH, SEQ, D_MODEL), 1.0),
        'x_sample': nrm(ks[1], (DEC_BATCH, DEC_SEQ, D_MODEL), 1.0),
        'state_mlstm_C': nrm(ks[2], (DEPTH, DEC_BATCH, M_HEADS, HEAD_DIM, HEAD_DIM), 0.1),
        'state_mlstm_n': nrm(ks[3], (DEPTH, DEC_BATCH, M_HEADS, HEAD_DIM), 0.1),
        'state_mlstm_m': nrm(ks[4], (DEPTH, DEC_BATCH, M_HEADS), 1.0),
        'state_gdn_S': nrm(ks[5], (DEPTH, DEC_BATCH, G_HEADS, HEAD_DIM, HEAD_DIM), 0.1),
        'state_gdn_conv': nrm(ks[6], (DEPTH, DEC_BATCH, CONV_W - 1, 3 * G_W), 1.0),
        'state_hgrn_S': nrm(ks[7], (DEPTH, DEC_BATCH, H_HEADS, HEAD_DIM, HEAD_DIM), 0.5),
        'c_prompt': nrm(ks[8], (BATCH, D_MODEL), 1.0),
        'c_sample': nrm(ks[9], (DEC_BATCH, D_MODEL), 1.0),
        'w_ada': nrm(ks[10], (DEPTH, D_MODEL, 6 * D_MODEL), 0.5 * D_MODEL ** -0.5),
        'b_ada': nrm(ks[11], (DEPTH, 6 * D_MODEL), 0.02),
        'norm_pre_mix': gain(ks[12], (DEPTH, D_MODEL)),
        'norm_post_mix': gain(ks[13], (DEPTH, D_MODEL)),
        'w_in': nrm(ks[14], (DEPTH, D_MODEL, P_IN), D_MODEL ** -0.5),
        'b_in': nrm(ks[15], (DEPTH, P_IN), 0.02),
        'mlstm_f_bias': jnp.linspace(3.0, 6.0, M_HEADS, dtype=F32)[None, :] + nrm(ks[16], (DEPTH, M_HEADS), 0.1),
        'gdn_conv_w': nrm(ks[17], (DEPTH, CONV_W, 3 * G_W), CONV_W ** -0.5),
        'gdn_A_log': jnp.log(jax.random.uniform(ks[18], (DEPTH, G_HEADS), F32, 1.0, 16.0)),
        'gdn_dt_bias': dt + jnp.log(-jnp.expm1(-dt)),
        'hgrn_lb_logits': nrm(ks[20], (DEPTH, H_W), 0.1),
        'mix_out_norm': gain(ks[21], (DEPTH, D_MIX)),
        'w_out': nrm(ks[22], (DEPTH, D_MIX, D_MODEL), D_MIX ** -0.5),
        'norm_pre_ffn': gain(ks[23], (DEPTH, D_MODEL)),
        'norm_post_ffn': gain(ks[24], (DEPTH, D_MODEL)),
        'w_ff1': nrm(ks[25], (DEPTH, D_MODEL, D_FF), D_MODEL ** -0.5),
        'w_ff2': nrm(ks[26], (DEPTH, D_FF, D_MODEL), D_FF ** -0.5),
    }

def reference(x_prompt, x_sample, state_mlstm_C, state_mlstm_n, state_mlstm_m, state_gdn_S, state_gdn_conv,
              state_hgrn_S, c_prompt, c_sample, w_ada, b_ada, norm_pre_mix, norm_post_mix, w_in, b_in,
              mlstm_f_bias, gdn_conv_w, gdn_A_log, gdn_dt_bias, hgrn_lb_logits, mix_out_norm, w_out,
              norm_pre_ffn, norm_post_ffn, w_ff1, w_ff2):
    params = (w_ada, b_ada, norm_pre_mix, norm_post_mix, w_in, b_in, mlstm_f_bias, gdn_conv_w, gdn_A_log,
              gdn_dt_bias, hgrn_lb_logits, mix_out_norm, w_out, norm_pre_ffn, norm_post_ffn, w_ff1, w_ff2)
    bp = x_prompt.shape[0]
    init = (jnp.zeros((DEPTH, bp, M_HEADS, HEAD_DIM, HEAD_DIM), F32),
            jnp.zeros((DEPTH, bp, M_HEADS, HEAD_DIM), F32),
            jnp.zeros((DEPTH, bp, M_HEADS), F32),
            jnp.zeros((DEPTH, bp, G_HEADS, HEAD_DIM, HEAD_DIM), F32),
            jnp.zeros((DEPTH, bp, CONV_W - 1, 3 * G_W), F32),
            jnp.zeros((DEPTH, bp, H_HEADS, HEAD_DIM, HEAD_DIM), F32))
    y_prompt, (p_C, p_n, p_m, p_gS, p_conv, p_hS) = trunk(x_prompt, c_prompt, init, params)
    past = (state_mlstm_C, state_mlstm_n, state_mlstm_m, state_gdn_S, state_gdn_conv, state_hgrn_S)
    y_sample, (s_C, s_n, s_m, s_gS, s_conv, s_hS) = trunk(x_sample, c_sample, past, params)
    return (y_prompt, y_sample, p_C, p_n, p_m, p_gS, p_conv, p_hS, s_C, s_n, s_m, s_gS, s_conv, s_hS)


_drawn_inputs = setup_inputs


def setup_inputs(seed=0):
    import zlib

    import numpy as np

    out = dict(_drawn_inputs(seed))
    spreads = {}
    factors = {'norm_post_mix': 16.912,
     'mix_out_norm': 6.033,
     'norm_pre_ffn': 70.814,
     'norm_post_ffn': 88.898}
    for name, (base, spread) in spreads.items():
        noise = np.random.default_rng([zlib.crc32(name.encode()), seed]).standard_normal(out[name].shape)
        drawn = base * np.exp(spread * noise) if base else spread * noise
        out[name] = __import__('jax').numpy.asarray(drawn.astype(out[name].dtype))
    for name, factor in factors.items():
        out[name] = (out[name] * factor).astype(out[name].dtype)
    return out
```

```python
from contextlib import ExitStack

import numpy as np

import concourse.bass as bass
from concourse import mybir

F32 = mybir.dt.float32
F32R = mybir.dt.float32r
ALU = mybir.AluOpType
ACT = mybir.ActivationFunctionType
AX = mybir.AxisListType

P = 128
D = 1024
KT = D // P
SEQ, NB, NT = 2048, 8, 8
SAMP = NB * NT
TOK = SEQ + SAMP
TILES = SEQ // P
HD = 64
MH, GH, HH = 6, 6, 4
CONV = 4
EPS = 1e-6
LN_EXP = "natural_log_exp_and_others"
DFF = 4 * D
MODROWS = SAMP + 1
ADA_CHUNK = 512
ADA_CHUNKS = 6 * D // ADA_CHUNK
GROUPS = [(g * 512, 512) for g in range(SEQ // 512)] + [(SEQ, SAMP)]

C_GATE = 0
C_RAW = (1, 14)
C_OUTGATE = (14, 22)
C_CONVN = (22, 28)
C_CONVV = (28, 31)
C_FORGET = (31, 33)
NCOL = 33
HEADS = [0, 2, 4, 1, 3, 5]
R_MQ, R_MK, R_MV, R_HQ, R_HI, R_MO, R_GG, R_HG, R_GQ, R_GK, R_GV, R_HG0 = 0, 3, 6, 9, 11, 13, 16, 19, 21, 24, 27, 30
NROW = 34
NCOLS = 151


def in_order():
    mw, gw, hw = MH * HD, GH * HD, HH * HD
    at, o = {}, 0
    for name, n in (("mq", mw), ("mk", mw), ("mv", mw), ("mo", mw), ("mi", MH), ("mf", MH), ("gqkv", 3 * gw),
                    ("gg", gw), ("gb", GH), ("ga", GH), ("hq", hw), ("hf", hw), ("hi", hw), ("hg", hw)):
        at[name] = np.arange(o, o + n)
        o += n
    gates = np.concatenate([at[n][HEADS] for n in ("mi", "mf", "gb", "ga")])
    pad = np.full(P - gates.size, -1)
    q, k, v = np.split(at["gqkv"], 3)
    return np.concatenate([gates, pad, at["mq"], at["mk"], at["mv"], at["hq"], at["hi"], at["mo"], at["gg"],
                           at["hg"], q, k, v, at["hf"]])


def met(eng, sem):
    eng.wait_ge(sem, 1)


class Sems:

    def __init__(self, nc, ctx, prefix):
        self.nc, self.prefix, self.made = nc, prefix, {}
        ctx.callback(self.end)

    def end(self):
        self.nc.clear_and_free_semaphores(list(self.made.values()))
        self.nc.all_engine_barrier()

    def __call__(self, name):
        if name not in self.made:
            self.made[name] = self.nc.alloc_semaphore(self.prefix + name)
        return self.made[name]


def modulation(nc, d, keep):
    with ExitStack() as ctx:
        sb = lambda n, s, t=F32: ctx.enter_context(nc.sbuf_tensor("mod_" + n, s, t))
        S = Sems(nc, ctx, "mod_")
        cT = sb("cT", [P, KT, MODROWS])
        wa = sb("wa", [P, 3, KT, ADA_CHUNK])
        bias = sb("bias", [MODROWS, 6 * D])
        mod = sb("mod", [MODROWS, 6 * D])
        gain = sb("gain", [MODROWS, 2, D])
        pm = ctx.enter_context(nc.psum_tensor("mod_pm", [MODROWS, 2, 512], F32))
        pt = ctx.enter_context(nc.psum_tensor("mod_pt", [P, 2, 2, 512], F32))
        chunk_in = [S(f"chunk_in{b}") for b in range(3)]
        small_in, product, added, turned, scaled, gated, stored = (
            S(n) for n in ("small_in", "product", "added", "turned", "scaled", "gated", "stored"))
        sections = [(1, keep["A1"], 0), (0, keep["B1"], None), (4, keep["A2"], 1), (3, keep["B2"], None)]

        block = ctx.enter_context(nc.Block())

        @block.sync
        def _(sp):
            sp.dma_start(cT[:], d["cT"]).then_inc(small_in, 16)
            for c in range(ADA_CHUNKS):
                if c >= 3:
                    sp.wait_ge(product, c - 2)
                sp.dma_start(wa[:, c % 3], d["w_ada"][c]).then_inc(chunk_in[c % 3], 16)
            sp.wait_ge(gated, 2)
            sp.dma_start(d["gates"], gain[:, :, :]).then_inc(stored, 16)
            sp.wait_ge(stored, 16)

        @block.scalar
        def _(act):
            act.dma_start(bias[:], d["b_ada"].broadcast_to([MODROWS, 6 * D])).then_inc(small_in, 16)
            act.dma_start(gain[:, 0, :], d["norm_post_mix"].broadcast_to([MODROWS, D])).then_inc(small_in, 16)
            act.dma_start(gain[:, 1, :], d["norm_post_ffn"].broadcast_to([MODROWS, D])).then_inc(small_in, 16)
            act.dma_start(keep["cols"][:], d["cols"]).then_inc(small_in, 16)
            act.dma_start(keep["ident"][:], d["ident"]).then_inc(small_in, 16)
            act.dma_start(keep["headsum"][:], d["headsum"]).then_inc(small_in, 16)

        @block.tensor
        def _(pe):
            pe.wait_ge(small_in, 112)
            for c in range(ADA_CHUNKS):
                pe.wait_ge(chunk_in[c % 3], 16 * (c // 3 + 1))
                if c >= 2:
                    pe.wait_ge(added, c - 1)
                for k in range(KT):
                    mm = pe.matmul(pm[:, c % 2, :], cT[:, k, :], wa[:, c % 3, k, :], start=(k == 0), stop=(k == KT - 1))
                mm.then_inc(product, 1)
            pe.wait_ge(added, ADA_CHUNKS)
            for n, (section, _, _) in enumerate(sections):
                if n >= 2:
                    pe.wait_ge(scaled, n - 1)
                for k in range(KT):
                    at = section * D + k * P
                    mm = pe.transpose(pt[:, n % 2, k // 4, (k % 4) * MODROWS:(k % 4 + 1) * MODROWS],
                                      mod[:, at:at + P], keep["ident"][0:MODROWS, 0:MODROWS])
                mm.then_inc(turned, 1)

        @block.vector
        def _(dve):
            dve.wait_ge(small_in, 112)
            for c in range(ADA_CHUNKS):
                cols = slice(c * ADA_CHUNK, (c + 1) * ADA_CHUNK)
                dve.wait_ge(product, c + 1)
                dve.tensor_tensor(mod[:, cols], pm[:, c % 2, :], bias[:, cols], ALU.add).then_inc(added, 1)
            dve.wait_ge(added, ADA_CHUNKS)
            for n, section in enumerate((2, 5)):
                dve.tensor_tensor(gain[:, n, :], mod[:, section * D:(section + 1) * D], gain[:, n, :],
                                  ALU.mult).then_inc(gated, 1)
            for n, (_, dst, norm) in enumerate(sections):
                dve.wait_ge(turned, n + 1)
                for half in range(2):
                    src = pt[:, n % 2, half, 0:4 * MODROWS].rearrange("p (k r) -> p k r", k=4)
                    out = dst[:, 4 * half:4 * half + 4, :]
                    if norm is None:
                        ins = dve.tensor_copy(out, src)
                    else:
                        col = keep["cols"][:, 8 * norm + 4 * half:8 * norm + 4 * half + 4]
                        ins = dve.scalar_tensor_tensor(out, src, 1.0, col.unsqueeze(2).broadcast_to([P, 4, MODROWS]),
                                                       ALU.add, ALU.mult)
                ins.then_inc(scaled, 1)


def norm_in(nc, d, keep, hi, lo):
    with ExitStack() as ctx:
        sb = lambda n, s, t=F32: ctx.enter_context(nc.sbuf_tensor("nin_" + n, s, t))
        S = Sems(nc, ctx, "nin_")
        x = sb("x", [P, 2, D])
        junk = sb("junk", [P, D])
        stat = sb("stat", [P, 2, 4])
        h = sb("h", [P, 2, KT, P])
        pt = ctx.enter_context(nc.psum_tensor("nin_pt", [P, 2, KT, P], F32))
        x_in = [S("x_in0"), S("x_in1")]
        summed, logged, rstd, scaled, turned, modded, shifted, hi_ready, lo_ready = (
            S(n) for n in ("summed", "logged", "rstd", "scaled", "turned", "modded", "shifted", "hi", "lo"))

        def tiles(eng, body):
            body(0, 0, 0, P)
            body(1, 1, 0, P)
            with eng.Fori(0, TILES // 2 - 1) as pair:
                body(pair * 2 + 2, 0, pair + 1, P)
                body(pair * 2 + 3, 1, pair + 1, P)
            body(TILES, 0, TILES // 2, SAMP)

        def late(t):
            return not isinstance(t, int) or t >= 2

        block = ctx.enter_context(nc.Block())

        @block.sync
        def _(sp):
            def body(t, u, use, n):
                if late(t):
                    sp.wait_ge(turned, t - 1)
                src = d["x"][bass.ts(t, P), :] if n == P else d["x"][SEQ:TOK, :]
                sp.dma_start(x[0:n, u, :], src).then_inc(x_in[u], 16)
            tiles(sp, body)

        @block.scalar
        def _(act):
            act.preload_act_table_set(LN_EXP)

            def body(t, u, use, n):
                act.wait_ge(x_in[u], (use + 1) * 16)
                act.activation(junk[0:n, :], x[0:n, u, :], ACT.Square, accum_out=stat[0:n, u, 0:1]).then_inc(summed, 1)
                act.wait_ge(summed, t + 1)
                act.activation(stat[0:n, u, 1:2], stat[0:n, u, 0:1], ACT.Ln, scale=1.0 / D,
                               bias=keep["eps"][0:n, :]).then_inc(logged, 1)
                act.wait_ge(logged, t + 1)
                act.activation(stat[0:n, u, 2:3], stat[0:n, u, 1:2], ACT.Exp, scale=-0.5).then_inc(rstd, 1)
                act.wait_ge(shifted, t + 1)
                met(act, shifted)
                dst = hi[:, :, bass.ts(t, P)] if n == P else hi[:, :, SEQ:TOK]
                act.activation(dst, h[:, u, :, 0:n], ACT.Copy).then_inc(hi_ready, 1)
            tiles(act, body)

        @block.vector
        def _(dve):
            def body(t, u, use, n):
                dve.wait_ge(rstd, t + 1)
                dve.tensor_scalar(x[0:n, u, :], x[0:n, u, :], stat[0:n, u, 2:3], None, ALU.mult).then_inc(scaled, 1)
                if n == P:
                    a, b = (keep[m][:, :, SAMP:SAMP + 1].broadcast_to([P, KT, P]) for m in ("A1", "B1"))
                else:
                    a, b = (keep[m][:, :, 0:SAMP] for m in ("A1", "B1"))
                dve.wait_ge(turned, t + 1)
                if late(t):
                    dve.wait_ge(hi_ready, t - 1)
                    dve.wait_ge(lo_ready, t - 1)
                dve.tensor_tensor(h[:, u, :, 0:n], pt[:, u, :, 0:n], a, ALU.mult).then_inc(modded, 1)
                dve.wait_ge(modded, t + 1)
                dve.tensor_tensor(h[:, u, :, 0:n], h[:, u, :, 0:n], b, ALU.add).then_inc(shifted, 1)
            tiles(dve, body)

        @block.gpsimd
        def _(pool):
            def body(t, u, use, n):
                pool.wait_ge(hi_ready, t + 1)
                at = bass.ts(t, P) if n == P else slice(SEQ, TOK)
                pool.tensor_tensor(lo[:, :, at], h[:, u, :, 0:n], hi[:, :, at].bitcast(F32),
                                   ALU.subtract).then_inc(lo_ready, 1)
            tiles(pool, body)

        @block.tensor
        def _(pe):
            def body(t, u, use, n):
                pe.wait_ge(scaled, t + 1)
                if late(t):
                    pe.wait_ge(modded, t - 1)
                for k in range(KT):
                    mm = pe.transpose(pt[:, u, k, 0:n], x[0:n, u, k * P:(k + 1) * P], keep["ident"][0:n, 0:n])
                mm.then_inc(turned, 1)
            tiles(pe, body)


def project_in(nc, d, keep, hi, lo):
    with ExitStack() as ctx:
        sb = lambda n, s, t=F32: ctx.enter_context(nc.sbuf_tensor("pin_" + n, s, t))
        S = Sems(nc, ctx, "pin_")
        w = sb("w", [P, 2, KT, P])
        whi = sb("whi", [P, 2, KT, P], F32R)
        wlo = sb("wlo", [P, 2, KT, P], F32R)
        z = sb("z", [P, 2, CONV - 1 + TOK])
        hist = sb("hist", [P, NB, CONV - 1 + NT])
        ra = sb("ra", [P, TOK])
        rb = sb("rb", [P, TOK])
        zero = sb("zero", [P, P])
        pz = ctx.enter_context(nc.psum_tensor("pin_pz", [P, len(GROUPS), 512], F32))
        pn = ctx.enter_context(nc.psum_tensor("pin_pn", [P, 3, 512], F32))
        lb = sb("lb", [P, 4, 2])
        zcol = sb("zcol", [P, 2, 2])
        w_in = [S("w_in0"), S("w_in1")]
        stored = [S("stored0"), S("stored1")]
        (whi_ready, wlo_ready, product, row, kept_stored, ready, bound, hist_in, conv, silu, square, norm,
         log, rnormed, sig_ready, kept, tmp, soft, tap, affine, lf_ready, cst, lb_exp, lb_left, lb_step) = (
            S(n) for n in ("whi", "wlo", "product", "row", "kept_stored", "ready", "bound", "hist_in",
                           "conv", "silu", "square", "norm", "log", "rnormed", "sig", "kept", "tmp", "soft", "tap",
                           "affine", "lf", "cst", "lb_exp", "lb_left", "lb_step"))
        CSTS = 6
        Z0 = CONV - 1
        zr = lambda u: z[:, u, Z0:Z0 + TOK]

        def blocks(eng, lo_c, hi_c, body):
            c = lo_c
            while c < hi_c and (c % 2 or c < 2):
                body(c, c % 2, c // 2)
                c += 1
            n = (hi_c - c) // 2
            if n > 1:
                with eng.Fori(0, n) as pair:
                    body(pair * 2 + c, 0, pair + c // 2)
                    body(pair * 2 + (c + 1), 1, pair + c // 2)
            elif n:
                body(c, 0, c // 2)
                body(c + 1, 1, c // 2)
            if (hi_c - c) % 2:
                body(hi_c - 1, 0, hi_c // 2)

        def late(c):
            return not isinstance(c, int) or c >= 2

        block = ctx.enter_context(nc.Block())

        def store(eng, row, src, done):
            eng.dma_start(d["z"][:, :, row, :].rearrange("t p c -> p t c"),
                          src[:, 0:SEQ].rearrange("p (t c) -> p t c", c=P)).then_inc(done, 16)
            eng.dma_start(d["z_s"][:, row, :], src[:, SEQ:TOK]).then_inc(done, 16)

        @block.sync
        def _(sp):
            def load(c, u):
                if late(c):
                    sp.wait_ge(wlo_ready, c - 1)
                sp.dma_start(w[:, u], d["w_in"][c]).then_inc(w_in[u], 16)

            load(0, 0)
            load(1, 1)
            load(2, 0)
            sp.wait_ge(row, 5)
            sp.dma_start(d["gz"][:, 0:SEQ], zr(0)[0:4 * MH, 0:SEQ]).then_inc(stored[0], 16)
            sp.dma_start(d["gz"][:, SEQ:TOK], zr(0)[0:4 * MH, SEQ:TOK]).then_inc(stored[0], 16)

            def raw(c, u, r):
                load(c + 2, u)
                sp.wait_ge(row, (c + 1) * 5)
                store(sp, c - 1, zr(u), stored[u])
            blocks(sp, *C_RAW, raw)

            def ready_row(c, u, r):
                load(c + 2, u)
                sp.wait_ge(ready, c + 1 - C_OUTGATE[0])
                store(sp, c - 1, zr(u), stored[u])
            blocks(sp, *C_OUTGATE, ready_row)

            def conv_row(c, u, r):
                if not isinstance(c, int) or c + 2 < NCOL:
                    load(c + 2, u)
                j = c - C_CONVN[0]
                if not isinstance(c, int) or j >= 1:
                    sp.wait_ge(conv, j)
                sp.dma_start(hist[:, :, 0:CONV - 1], d["hist"][j]).then_inc(hist_in, 16)
                sp.wait_ge(row, (c + 1) * 5)
                sp.dma_start(d["p_conv"][j], z[:, u, SEQ:SEQ + CONV - 1]).then_inc(bound, 16)
                sp.dma_start(d["s_conv"][j], z[:, u, Z0 + SEQ:Z0 + TOK].rearrange("p (b t) -> p b t", t=NT)
                             [:, :, NT - CONV + 1:NT]).then_inc(bound, 16)
                sp.wait_ge(ready, c + 1 - C_OUTGATE[0])
                store(sp, c - 1, zr(u), stored[u])
            blocks(sp, C_CONVN[0], C_CONVV[1], conv_row)
            for j, c in enumerate(range(*C_FORGET)):
                sp.wait_ge(kept, j + 1)
                store(sp, R_HG0 + 2 * j + 1, ra, kept_stored)
                sp.wait_ge(ready, c + 1 - C_OUTGATE[0])
                store(sp, R_HG0 + 2 * j, zr(c % 2), stored[c % 2])
            sp.wait_ge(stored[0], 32 * ((NCOL + 1) // 2))
            sp.wait_ge(stored[1], 32 * (NCOL // 2))
            sp.wait_ge(kept_stored, 64)
            sp.wait_ge(bound, 32 * (C_CONVV[1] - C_CONVN[0]))

        @block.tensor
        def _(pe):
            def body(c, u, r):
                pe.wait_ge(whi_ready, c + 1)
                pe.wait_ge(wlo_ready, c + 1)
                for g, (at, n) in enumerate(GROUPS):
                    if not isinstance(c, int) or c >= 1:
                        pe.wait_ge(row, (c - 1) * 5 + g + 1)
                    for k in range(KT):
                        pe.matmul(pz[:, g, 0:n], whi[:, u, k], hi[:, k, at:at + n], start=(k == 0), stop=False)
                        pe.matmul(pz[:, g, 0:n], whi[:, u, k], lo[:, k, at:at + n], start=False, stop=False)
                        mm = pe.matmul(pz[:, g, 0:n], wlo[:, u, k], hi[:, k, at:at + n], start=False,
                                       stop=(k == KT - 1))
                    mm.then_inc(product, 1)

            def with_norms(c, u, r):
                body(c, u, r)
                j = c - 1 - C_CONVN[0]
                pe.wait_ge(square, j + 1)
                for g, (at, n) in enumerate(GROUPS):
                    if g >= 3:
                        pe.wait_ge(log, j * 5 + g - 2)
                    elif not isinstance(c, int) or j >= 1:
                        pe.wait_ge(log, j * 5)
                    pe.matmul(pn[:, g % 3, 0:n], keep["headsum"][:], rb[:, at:at + n], start=True,
                              stop=True).then_inc(norm, 1)

            blocks(pe, 0, C_CONVN[0] + 1, body)
            blocks(pe, C_CONVN[0] + 1, C_CONVN[1] + 1, with_norms)
            blocks(pe, C_CONVN[1] + 1, NCOL, body)

        @block.scalar
        def _(act):
            def split(c, u, r):
                act.wait_ge(w_in[u], (r + 1) * 16)
                if late(c):
                    act.wait_ge(product, (c - 1) * 5)
                act.activation(whi[:, u], w[:, u], ACT.Copy).then_inc(whi_ready, 1)

            def head(c, u, r):
                if not isinstance(c, int) or c + 1 < NCOL:
                    split(c + 1, 1 - u, r + u)
                if late(c):
                    act.wait_ge(stored[u], r * 32)
                for g, (at, n) in enumerate(GROUPS):
                    act.wait_ge(product, c * 5 + g + 1)
                    act.activation(z[:, u, Z0 + at:Z0 + at + n], pz[:, g, 0:n], ACT.Identity,
                                   scale=zcol[:, u, 0:1], bias=zcol[:, u, 1:2]).then_inc(row, 1)

            act.wait_ge(cst, CSTS)
            act.activation(lb[:, 1, :], lb[:, 0, :], ACT.Exp).then_inc(lb_exp, 1)
            act.wait_ge(lb_left, 1)
            act.activation(lb[:, 3, :], lb[:, 2, :], ACT.Ln).then_inc(lb_exp, 1)
            split(0, 0, 0)
            blocks(act, 0, C_RAW[1], head)

            def outgate(c, u, r):
                head(c, u, r)
                n = c - C_OUTGATE[0]
                if not isinstance(c, int) or n >= 1:
                    act.wait_ge(ready, n)
                act.wait_ge(row, c * 5 + 5)
                act.activation(ra[:, :], zr(u), ACT.Sigmoid).then_inc(sig_ready, 1)
            blocks(act, *C_OUTGATE, outgate)

            def rnorm(c):
                j = c - C_CONVN[0]
                act.preload_act_table_set(LN_EXP)
                for g, (at, n) in enumerate(GROUPS):
                    act.wait_ge(norm, j * 5 + g + 1)
                    act.activation(rb[:, at:at + n], pn[:, g % 3, 0:n], ACT.Ln, bias=keep["eps"][:, :]).then_inc(log, 1)
                act.wait_ge(log, j * 5 + 5)
                act.activation(rb[:, :], rb[:, :], ACT.Exp, scale=-0.5).then_inc(rnormed, 1)

            def conv_block(c, u, r, before, squared):
                head(c, u, r)
                if before:
                    rnorm(c - 1)
                act.wait_ge(conv, c + 1 - C_CONVN[0])
                act.activation(rb[:, :], ra[:, :], ACT.Sigmoid).then_inc(sig_ready, 1)
                if squared:
                    act.wait_ge(silu, c + 1 - C_CONVN[0])
                    act.activation(rb[:, :], ra[:, :], ACT.Square).then_inc(square, 1)

            conv_block(C_CONVN[0], C_CONVN[0] % 2, C_CONVN[0] // 2, False, True)
            blocks(act, C_CONVN[0] + 1, C_CONVN[1], lambda c, u, r: conv_block(c, u, r, True, True))
            conv_block(C_CONVV[0], C_CONVV[0] % 2, C_CONVV[0] // 2, True, False)
            blocks(act, C_CONVV[0] + 1, C_CONVV[1], lambda c, u, r: conv_block(c, u, r, False, False))
            for j, c in enumerate(range(*C_FORGET)):
                u = c % 2
                head(c, u, c // 2)
                act.wait_ge(row, c * 5 + 5)
                act.wait_ge(ready, c - C_OUTGATE[0])
                if j:
                    act.wait_ge(kept_stored, 32 * j)
                act.activation(ra[:, :], zr(u), ACT.Sigmoid, scale=-1.0).then_inc(sig_ready, 1)
                act.preload_act_table_set(LN_EXP)
                act.wait_ge(tmp, 2 * j + 1)
                act.activation(rb[:, :], rb[:, :], ACT.Exp).then_inc(soft, 1)
                act.wait_ge(soft, 2 * j + 1)
                act.activation(rb[:, :], rb[:, :], ACT.Ln, bias=1.0).then_inc(soft, 1)

        @block.vector
        def _(dve):
            def split(c, u, r):
                dve.wait_ge(w_in[u], (r + 1) * 16)
                dve.wait_ge(whi_ready, c + 1)
                dve.tensor_copy(zcol[:, u, :], keep["zcols"][:, :, bass.ds(c, 1)].rearrange("p a o -> p (a o)"))
                dve.tensor_tensor(wlo[:, u], w[:, u], whi[:, u].bitcast(F32), ALU.subtract).then_inc(wlo_ready, 1)

            def head(c, u, r):
                if not isinstance(c, int) or c + 1 < NCOL:
                    split(c + 1, 1 - u, r + u)

            dve.memset(z[:, :, 0:Z0], 0.0).then_inc(cst, 1)
            dve.memset(zero[:], 0.0).then_inc(cst, 1)
            dve.tensor_tensor(keep["zcols"][:, 1, :], keep["zcols"][:, 1, :], keep["zcols"][:, 0, :],
                              ALU.mult).then_inc(cst, 1)
            for n in range(2):
                dve.tensor_tensor(keep["ogate"][:, n, :], keep["ogate"][:, n, :], keep["ogate"][:, 2, :],
                                  ALU.mult).then_inc(cst, 1)
            lbl = keep["lbl"]
            dve.tensor_tensor(lb[:, 0, :], lbl[:, :], lbl[:, :], ALU.subtract).then_inc(cst, 1)
            dve.wait_ge(lb_exp, 1)
            dve.reciprocal(lb[:, 2, :], lb[:, 1, :]).then_inc(lb_step, 1)
            dve.wait_ge(lb_step, 1)
            dve.tensor_tensor(lb[:, 2, :], lb[:, 2, :], lb[:, 1, :], ALU.mult).then_inc(lb_step, 1)
            dve.wait_ge(lb_step, 2)
            dve.tensor_tensor(lb[:, 2, :], lb[:, 2, :], lb[:, 2, :], ALU.subtract).then_inc(lb_step, 1)
            dve.wait_ge(lb_step, 3)
            dve.tensor_scalar(lb[:, 2, :], lb[:, 2, :], -1.0, 1.0, ALU.mult, ALU.add).then_inc(lb_left, 1)
            split(0, 0, 0)
            blocks(dve, 0, C_RAW[1], head)

            def outgate(c, u, r):
                head(c, u, r)
                n = c - C_OUTGATE[0]
                dve.wait_ge(sig_ready, n + 1)
                dve.tensor_scalar(zr(u), zr(u), keep["ogate"][:, 0, bass.ds(n, 1)], keep["ogate"][:, 1, bass.ds(n, 1)],
                                  ALU.mult, ALU.add).then_inc(affine, 1)
                dve.wait_ge(affine, n + 1)
                dve.tensor_tensor(zr(u), zr(u), ra[:, :], ALU.mult).then_inc(ready, 1)
            blocks(dve, *C_OUTGATE, outgate)

            def scale_norm(c, u):
                j = c - C_CONVN[0]
                dve.wait_ge(rnormed, j + 1)
                dve.wait_ge(bound, (j + 1) * 32)
                dve.scalar_tensor_tensor(zr(u), ra[:, :], keep["qscale"][:, bass.ds(j, 1)], rb[:, :],
                                         ALU.mult, ALU.mult).then_inc(ready, 1)

            def conv_block(c, u, r, before, normed):
                head(c, u, r)
                n, j = c - C_OUTGATE[0], c - C_CONVN[0]
                if before:
                    scale_norm(c - 1, 1 - u)
                    dve.wait_ge(ready, n)
                elif not isinstance(c, int) or n >= 1:
                    dve.wait_ge(ready, n)
                dve.wait_ge(row, c * 5 + 5)
                dve.wait_ge(hist_in, (j + 1) * 16)
                zs = z[:, u, Z0 + SEQ:Z0 + TOK].rearrange("p (b t) -> p b t", t=NT)
                rs = ra[:, SEQ:TOK].rearrange("p (b t) -> p b t", t=NT)
                dve.tensor_copy(hist[:, :, Z0:Z0 + NT], zs).then_inc(tap, 1)
                for t in range(CONV):
                    wt = keep["convw"][:, t, bass.ds(j, 1)]
                    zp, zh = z[:, u, t:t + SEQ], hist[:, :, t:t + NT]
                    dve.wait_ge(tap, j * 7 + (1 if t == 0 else 2 * t + 1))
                    if t == 0:
                        dve.tensor_scalar(ra[:, 0:SEQ], zp, wt, None, ALU.mult).then_inc(tap, 1)
                        dve.tensor_scalar(rs, zh, wt, None, ALU.mult).then_inc(tap, 1)
                    else:
                        last = t == CONV - 1
                        a = dve.scalar_tensor_tensor(ra[:, 0:SEQ], zp, wt, ra[:, 0:SEQ], ALU.mult, ALU.add)
                        b = dve.scalar_tensor_tensor(rs, zh, wt, rs, ALU.mult, ALU.add)
                        if last:
                            b.then_inc(conv, 1)
                        else:
                            a.then_inc(tap, 1)
                            b.then_inc(tap, 1)
                dve.wait_ge(sig_ready, n + 1)
                if normed:
                    dve.tensor_tensor(ra[:, :], ra[:, :], rb[:, :], ALU.mult).then_inc(silu, 1)
                else:
                    dve.wait_ge(bound, (j + 1) * 32)
                    dve.tensor_tensor(zr(u), ra[:, :], rb[:, :], ALU.mult).then_inc(ready, 1)

            conv_block(C_CONVN[0], C_CONVN[0] % 2, C_CONVN[0] // 2, False, True)
            blocks(dve, C_CONVN[0] + 1, C_CONVN[1], lambda c, u, r: conv_block(c, u, r, True, True))
            conv_block(C_CONVV[0], C_CONVV[0] % 2, C_CONVV[0] // 2, True, False)
            blocks(dve, C_CONVV[0] + 1, C_CONVV[1], lambda c, u, r: conv_block(c, u, r, False, False))
            for j, c in enumerate(range(*C_FORGET)):
                u = c % 2
                head(c, u, c // 2)
                dve.wait_ge(row, c * 5 + 5)
                dve.wait_ge(ready, c - C_OUTGATE[0])
                dve.scalar_tensor_tensor(rb[:, :], zr(u), -1.0, zr(u), ALU.mult, ALU.min).then_inc(tmp, 1)
                dve.wait_ge(sig_ready, c + 1 - C_OUTGATE[0])
                dve.tensor_scalar(ra[:, :], ra[:, :], lb[:, 2, j:j + 1], None, ALU.mult).then_inc(kept, 1)
                dve.wait_ge(soft, 2 * j + 2)
                dve.scalar_tensor_tensor(rb[:, :], zr(u), 0.0, rb[:, :], ALU.min, ALU.subtract).then_inc(tmp, 1)
                dve.wait_ge(tmp, 2 * j + 2)
                dve.wait_ge(lb_exp, 2)
                dve.tensor_scalar(rb[:, :], rb[:, :], lb[:, 3, j:j + 1], None, ALU.add).then_inc(lf_ready, 1)
                dve.wait_ge(lf_ready, j + 1)
                with dve.Fori(0, TILES) as i:
                    dve.tensor_tensor_scan(zr(u)[:, bass.ts(i, P)], zero[:, :], rb[:, bass.ts(i, P)], 0.0,
                                           ALU.add, ALU.add)
                for b in range(NB):
                    at = slice(SEQ + b * NT, SEQ + (b + 1) * NT)
                    ins = dve.tensor_tensor_scan(zr(u)[:, at], zero[:, 0:NT], rb[:, at], 0.0, ALU.add, ALU.add)
                ins.then_inc(ready, 1)
Q_A, Q_NG, Q_BETA, Q_NBEG, Q_WI, Q_WS, Q_EGL, Q_EG = range(8)
NQ = 8
PJ = (2, 3)


def gates(nc, d, keep):
    with ExitStack() as ctx:
        sb = lambda n, s, t=F32: ctx.enter_context(nc.sbuf_tensor("gat_" + n, s, t))
        S = Sems(nc, ctx, "gat_")
        R = TILES * MH
        ends = sb("ends", [MH, 2, TILES])
        mend = sb("mend", [MH, TILES + 1])
        zero = sb("zero", [P, P])
        parts = {}
        for who, rows, n, length in (("p", R, P, P), ("s", MH, SAMP, NT)):
            v = {"rows": rows, "n": n, "seqs": n // length, "len": length}
            for name, k in (("raw", 4), ("x", 2), ("e", 2), ("q", NQ), ("row", 3), ("b", 1), ("g", 1), ("M", 1),
                            ("m0", 1), ("col", 3), ("fin", 3), ("tmp", 1)):
                width = {"m0": n // length, "col": 1, "fin": n // length}.get(name, n)
                v[name] = sb(f"{name}_{who}", [rows, k, width])
            parts[who] = v
        turned = ctx.enter_context(nc.psum_tensor("gat_turned", [P, NQ, P], F32))
        vp, vs = parts["p"], parts["s"]

        block = ctx.enter_context(nc.Block())

        @block.sync
        def _(sp):
            for k in range(4):
                sp.dma_start(vp["raw"][:, k, :], d["gz"][k * MH:(k + 1) * MH, 0:SEQ].rearrange("h (t c) -> t h c", c=P)
                             ).then_inc(S("in"), 16)
                sp.dma_start(vs["raw"][:, k, :], d["gz"][k * MH:(k + 1) * MH, SEQ:TOK]).then_inc(S("in"), 16)
            sp.dma_start(vp["col"][:, :, 0], d["gcol_p"]).then_inc(S("in"), 16)
            sp.dma_start(vs["col"][:, :, 0], d["gcol_s"]).then_inc(S("in"), 16)
            sp.dma_start(vs["m0"][:, 0, :], d["m0"]).then_inc(S("in"), 16)
            sp.wait_ge(S("ends"), 2)
            for k, src in ((0, vp["M"]), (1, vp["b"])):
                sp.dma_start(d["ends"][k].rearrange("(r o) -> r o", o=1), src[:, 0, P - 1:P]).then_inc(S("ends_out"), 16)
            sp.wait_ge(S("ends_out"), 32)
            sp.dma_start(ends[:], d["ends"].rearrange("k (t h) -> h k t", h=MH), allow_slow_non_contiguous=True).then_inc(S("ends_in"), 16)
            sp.wait_ge(S("mend"), 2)
            sp.dma_start(d["mprev"].rearrange("(t h) -> h t", h=MH), mend[:, 0:TILES],
                         allow_slow_non_contiguous=True).then_inc(S("mprev_out"), 16)
            sp.dma_start(d["p_m"], mend[:, TILES:TILES + 1]).then_inc(S("final"), 16)
            sp.wait_ge(S("mprev_out"), 16)
            sp.dma_start(vp["m0"][:, 0, :], d["mprev"].rearrange("(r o) -> r o", o=1)).then_inc(S("mprev_in"), 16)
            sp.wait_ge(S("fin"), 3)
            sp.dma_start(d["rows_p"].rearrange("t h k c -> (t h) k c"), vp["row"][:]).then_inc(S("final"), 16)
            sp.dma_start(d["dec_p"].rearrange("w (t h) -> (t h) w", h=MH), vp["fin"][:, 0:2, 0],
                         allow_slow_non_contiguous=True).then_inc(S("final"), 16)
            sp.wait_ge(S("fin"), 6)
            sp.dma_start(d["rows_s"], vs["row"][:]).then_inc(S("final"), 16)
            sp.dma_start(d["dec_s"].rearrange("w h b -> h w b"), vs["fin"][:, 0:2, :]).then_inc(S("final"), 16)
            sp.dma_start(d["s_m"], vs["fin"][:, 2, :]).then_inc(S("final"), 16)
            sp.wait_ge(S("final"), 96)

        @block.scalar
        def _(act):
            act.preload_act_table_set(LN_EXP)
            for n, v in enumerate((vp, vs)):
                if n == 0:
                    act.wait_ge(S("in"), 176)
                act.activation(v["col"][:, 1, :], v["col"][:, 1, :], ACT.Exp).then_inc(S("expA"), 1)
                act.activation(v["q"][:, Q_BETA, :], v["raw"][:, 2, :], ACT.Exp, scale=-1.0).then_inc(S("expb"), 1)
                act.wait_ge(S("nabs"), n + 1)
                act.activation(v["e"][:], v["e"][:], ACT.Exp).then_inc(S("soft"), 1)
                act.wait_ge(S("soft"), 2 * n + 1)
                act.activation(v["e"][:], v["e"][:], ACT.Ln, bias=1.0).then_inc(S("soft"), 1)
            for n, v in enumerate((vp, vs)):
                act.wait_ge(S("expo"), n + 1)
                act.activation(v["q"][:, Q_WI:Q_EG + 1, :], v["q"][:, Q_WI:Q_EG + 1, :], ACT.Exp).then_inc(S("weights"), 1)

        @block.vector
        def _(dve):
            step = [0]

            def then(ins):
                step[0] += 1
                ins.then_inc(S("step"), 1)
                dve.wait_ge(S("step"), step[0])

            def seq(v, name, k=0):
                return v[name][:, k, :].rearrange("h (b t) -> h b t", t=v["len"])

            def last(v, name, k=0):
                return seq(v, name, k)[:, :, v["len"] - 1:v["len"]].broadcast_to([v["rows"], v["seqs"], v["len"]])

            def running(v, out, src, op, initial, second):
                for b in range(v["seqs"]):
                    at = slice(b * v["len"], (b + 1) * v["len"])
                    ins = dve.tensor_tensor_scan(out[:, 0, at], second[0:v["rows"], 0:v["len"]] if second is not None
                                                 else src[:, at], src[:, at],
                                                 initial(b) if callable(initial) else initial, op, op)
                return ins

            dve.memset(mend[:, 0:1], 0.0).then_inc(S("mend"), 1)
            then(dve.memset(zero[:], 0.0))
            dve.wait_ge(S("in"), 176)
            for n, v in enumerate((vp, vs)):
                dve.tensor_scalar(v["x"][:, 0, :], v["raw"][:, 1, :], v["col"][:, 0, :], None, ALU.add)
                then(dve.tensor_scalar(v["x"][:, 1, :], v["raw"][:, 3, :], v["col"][:, 2, :], None, ALU.add))
                dve.scalar_tensor_tensor(v["e"][:], v["x"][:], -1.0, v["x"][:], ALU.mult, ALU.min).then_inc(S("nabs"), 1)
                dve.wait_ge(S("soft"), 2 * n + 2)
                dve.scalar_tensor_tensor(v["x"][:, 0, :], v["x"][:, 0, :], 0.0, v["e"][:, 0, :], ALU.min, ALU.subtract)
                then(dve.scalar_tensor_tensor(v["x"][:, 1, :], v["x"][:, 1, :], 0.0, v["e"][:, 1, :], ALU.max, ALU.add))
                dve.wait_ge(S("expA"), n + 1)
                then(dve.tensor_scalar(v["x"][:, 1, :], v["x"][:, 1, :], v["col"][:, 1, :], -1.0, ALU.mult, ALU.mult))
                running(v, v["b"], v["x"][:, 0, :], ALU.add, 0.0, zero)
                then(running(v, v["g"], v["x"][:, 1, :], ALU.add, 0.0, zero))
                then(dve.tensor_tensor(v["q"][:, Q_A, :], v["raw"][:, 0, :], v["b"][:, 0, :], ALU.subtract))
                m0 = v["m0"]
                start = -3.0e38 if n == 0 else (lambda b, m0=m0: m0[:, 0, b:b + 1])
                ins = running(v, v["M"], v["q"][:, Q_A, :], ALU.max, start, None)
                if n == 0:
                    ins.then_inc(S("ends"), 2)
                else:
                    then(ins)
                dve.wait_ge(S("expb"), n + 1)
                then(dve.tensor_scalar(v["q"][:, Q_BETA, :], v["q"][:, Q_BETA, :], 1.0, None, ALU.add))
                then(dve.reciprocal(v["q"][:, Q_BETA, :], v["q"][:, Q_BETA, :]))
                dve.tensor_copy(v["row"][:, 2, :], v["q"][:, Q_BETA, :])
                dve.tensor_copy(v["row"][:, 1, :], v["g"][:, 0, :])
                dve.tensor_scalar(v["q"][:, Q_NG, :], v["g"][:, 0, :], -1.0, None, ALU.mult)
                dve.tensor_copy(v["q"][:, Q_EG, :], v["g"][:, 0, :])
            dve.wait_ge(S("ends_in"), 16)
            dve.tensor_tensor_scan(mend[:, 1:TILES + 1], ends[:, 0, :], ends[:, 1, :], 0.0, ALU.max,
                                   ALU.add).then_inc(S("mend"), 1)
            dve.wait_ge(S("mprev_in"), 16)
            then(dve.tensor_scalar(vp["M"][:, 0, :], vp["M"][:, 0, :], vp["m0"][:, 0, :], None, ALU.max))
            for n, v in enumerate((vp, vs)):
                dve.tensor_scalar(v["row"][:, 0, :], v["M"][:, 0, :], -1.0, None, ALU.mult)
                m0 = v["m0"][:, 0, :].unsqueeze(2).broadcast_to([v["rows"], v["seqs"], v["len"]])
                dve.tensor_tensor(seq(v, "q", Q_WI), m0, seq(v, "M"), ALU.subtract)
                dve.tensor_tensor(seq(v, "q", Q_WS), seq(v, "q", Q_A), last(v, "M"), ALU.subtract)
                dve.tensor_tensor(seq(v, "q", Q_EGL), last(v, "g"), seq(v, "g"), ALU.subtract).then_inc(S("expo"), 1)
            for n, v in enumerate((vp, vs)):
                dve.wait_ge(S("weights"), n + 1)
                ends_of = lambda name, k: seq(v, name, k)[:, :, v["len"] - 1]
                dve.tensor_copy(v["fin"][:, 0, :], ends_of("q", Q_WI)).then_inc(S("fin"), 1)
                dve.tensor_copy(v["fin"][:, 1, :], ends_of("q", Q_EG)).then_inc(S("fin"), 1)
                dve.scalar_tensor_tensor(v["q"][:, Q_NBEG, :], v["q"][:, Q_BETA, :], -1.0, v["q"][:, Q_EG, :],
                                         ALU.mult, ALU.mult).then_inc(S("nbeg"), 1)
                dve.tensor_tensor(v["fin"][:, 2, :], ends_of("b", 0), ends_of("M", 0), ALU.add).then_inc(S("fin"), 1)
            for n, (v, dst) in enumerate(((vp, keep["cols_p"]), (vs, keep["cols_s"]))):
                dve.wait_ge(S("turned"), n + 1)
                dve.tensor_copy(dst[:], turned[0:v["n"], :, 0:v["rows"]]).then_inc(S("read"), 1)

        @block.tensor
        def _(pe):
            for n, v in enumerate((vp, vs)):
                pe.wait_ge(S("nbeg"), n + 1)
                if n:
                    pe.wait_ge(S("read"), n)
                for k in range(NQ):
                    mm = pe.transpose(turned[0:v["n"], k, 0:v["rows"]], v["q"][:, k, :],
                                      keep["ident"][0:v["rows"], 0:v["rows"]])
                mm.then_inc(S("turned"), 1)



LEVELS = P.bit_length() - 1
Y_M, Y_G, Y_H = 0, MH, MH + GH


def mixers(nc, d, keep, sample):
    with ExitStack() as ctx:
        pre = "smp_" if sample else "mix_"
        sb = lambda n, s, t=F32: ctx.enter_context(nc.sbuf_tensor(pre + n, s, t))
        S = Sems(nc, ctx, pre)
        halvings = 3 if sample else LEVELS
        nbuf = 1 if sample else 2
        zt = [sb(f"zt{u}", [P, NROW, P]) for u in range(nbuf)]
        rb = [sb(f"rb{u}", [P, MH, 3, P]) for u in range(nbuf)]
        yt = [sb(f"yt{u}", [P, KT, P]) for u in range(nbuf)]
        level = sb("level", [P, LEVELS + 1, P])
        late = sb("late", [P, 2, P])
        cc = [sb(f"cc{u}", [P, NQ, MH]) for u in range(nbuf)]
        ex = sb("ex", [P, MH, 2, P])
        bd = sb("bd", [P, MH, P])
        pm, at_, lt, xf, wn = (sb(n, [P, MH, P]) for n in ("pm", "attn", "lt", "xf", "wn"))
        cl = sb("cl", [P, 3, MH, P], F32R)
        x, xt, m1 = (sb(n, [P, MH, P], F32R) for n in ("x", "xt", "m1"))
        ident_r = sb("ident_r", [P, P], F32R)
        zero = sb("zero", [P, 2])
        v1 = sb("v1", [P, MH, HD + 1])
        kw, gkw, bv, vn, rv = (sb(n, [P, MH, HD]) for n in ("kw", "gkw", "bv", "vn", "rv"))
        hv, kd = (sb(n, [P, HH, HD]) for n in ("hv", "kd"))
        num = sb("num", [P, MH, HD + 1])
        den = sb("den", [P, 2, MH])
        y = sb("y", [P, 16, HD])
        sq = sb("sq", [P, 16, HD])
        ss = sb("ss", [P, 3, 16])
        e = sb("e", [P, LEVELS + 2, 2, P])
        hk, hq = (sb(n, [P, LEVELS + 1, 2, P]) for n in ("hk", "hq"))
        ph = sb("ph", [P, HH, LEVELS + 1, P])
        if sample:
            dc = sb("dc", [P, 2, 3, NB])
            cm, gs, hs = (sb(n, [P, k, NB, HD]) for n, k in (("cm", 3), ("gs", 3), ("hs", 2)))
            nm = sb("nm", [P, 3, NB])
            one_t = sb("one_t", [P, NB, P])
            one_s = sb("one_s", [P, NB])
            qx = sb("qx", [P, 3, NB, P])
            vx = sb("vx", [P, 2, NB, HD])
        else:
            dc = [sb(f"dc{u}", [P, 2, 3]) for u in range(nbuf)]
            dec = sb("dec", [P, 2, TILES, MH])
            cm, gs, hs = (sb(n, [P, k, w]) for n, k, w in (("cm", 3, HD + 1), ("gs", 3, HD), ("hs", 2, HD)))
        bank = lambda n: ctx.enter_context(nc.psum_tensor(pre + n, [P, 2, 512], F32))
        pa, pb, pc, pd = bank("pa"), bank("pb"), bank("pc"), bank("pd")
        z_in = [S(f"z_in{u}") for u in range(nbuf)]
        y_out = [S(f"y_out{u}") for u in range(nbuf)]
        groups = [(j, g) for j in range(2) for g in range((halvings + 1) // 4)]
        terms = halvings + 1
        plan = [("turn", 0)] + [("round", i) for i in range(len(groups))] + [("hgrn", 0), ("mlstm", 0)]
        fill = [[plan[i]] if i < len(plan) else [] for i in range(halvings)]
        rest = plan[halvings:]
        R = len(groups)
        CONSTS = 2
        pv = lambda b, w, at=0, n=3: b[:, :, at:at + n * w].rearrange("p r (j c) -> p r j c", c=w)
        hm = lambda a: a.rearrange("p (r j) c -> p r j c", r=2)
        ym = lambda a: a.rearrange("p (j r) c -> p r j c", r=2)
        half = lambda par: slice(par * HD, (par + 1) * HD)
        colh = lambda u, q, w: cc[u][:, q, :].rearrange("p (r j) -> p r j", r=2).unsqueeze(3).broadcast_to([P, 2, 3, w])
        tok = lambda b, at: b.rearrange("p a (j r c) -> p (a j) r c", r=2, c=HD)[:, at:at + 3].rearrange("p j r c -> p r j c")

        def tiles(eng, before, body, after):
            before(0, 0, 0)
            if sample:
                body(0, 0, 0, True, True)
                after(0, 0, 0)
                return
            body(0, 0, 0, True, False)
            body(1, 1, 0, False, False)
            with eng.Fori(0, TILES // 2 - 2) as pair:
                body(pair * 2 + 2, 0, pair + 1, False, False)
                body(pair * 2 + 3, 1, pair + 1, False, False)
            body(TILES - 2, 0, TILES // 2 - 1, False, False)
            body(TILES - 1, 1, TILES // 2 - 1, False, True)
            after(TILES - 1, 1, TILES // 2 - 1)

        block = ctx.enter_context(nc.Block())

        @block.sync
        def _(sp):
            def load(t, u):
                if sample:
                    sp.dma_start(zt[0][:, :, 0:SAMP], d["z_s"]).then_inc(z_in[0], 16)
                    sp.dma_start(rb[0][:, :, :, 0:SAMP].rearrange("p h k c -> p (h k) c"),
                                 d["rows_s"].rearrange("h k c -> (h k) c").unsqueeze(0)
                                 .broadcast_to([P, MH * 3, SAMP])).then_inc(z_in[0], 16)
                else:
                    tt = bass.ds(t, 1)
                    sp.dma_start(zt[u][:].rearrange("p r c -> p (r c)"),
                                 d["z"][tt].rearrange("o p r c -> (o p) (r c)")).then_inc(z_in[u], 16)
                    sp.dma_start(rb[u][:].rearrange("p h k c -> p (h k c)"),
                                 d["rows_p"][tt].rearrange("o h k c -> o (h k c)").broadcast_to([P, MH * 3 * P])
                                 ).then_inc(z_in[u], 16)

            def save(t, u):
                sp.wait_ge(S("gated"), t + 2)
                if sample:
                    sp.dma_start(d["yT_s"], yt[0][:, :, 0:SAMP]).then_inc(y_out[0], 16)
                else:
                    sp.dma_start(d["yT"][bass.ds(t, 1)].rearrange("o p k c -> (o p) (k c)"),
                                 yt[u][:].rearrange("p k c -> p (k c)")).then_inc(y_out[u], 16)

            sp.dma_start(level[:], d["level"]).then_inc(S("const_in"), 16)
            sp.dma_start(late[:], d["late"][int(sample)]).then_inc(S("const_in"), 16)
            if sample:
                sp.wait_ge(S("pads"), 3)
                for n, (dst, src) in enumerate(((cm, "s_cm"), (nm, "s_nm"), (gs, "s_gs"), (hs, "s_hs"),
                                                (one_t, "one_t"), (one_s, "one_s"))):
                    sp.dma_start(dst[:], d[src]).then_inc(S("const_in"), 16)
                for par in range(2):
                    for w in range(2):
                        sp.dma_start(dc[half(par), w], d["dec_s"][w, 3 * par:3 * par + 3].unsqueeze(0)
                                     .broadcast_to([HD, 3, NB])).then_inc(S("const_in"), 16)
                load(0, 0)
                save(0, 0)
            else:
                for w in range(2):
                    sp.dma_start(dec[:, w].rearrange("p t h -> p (t h)"),
                                 d["dec_p"][w:w + 1, :].broadcast_to([P, TILES * MH])).then_inc(S("const_in"), 16)
                load(0, 0)
                load(1, 1)
                with sp.Fori(0, TILES // 2 - 1) as pair:
                    for c in range(2):
                        save(pair * 2 + c, c)
                        load(pair * 2 + c + 2, c)
                for c in range(2):
                    save(TILES - 2 + c, c)
            sp.wait_ge(S("states"), 3)
            names = ("o_s_cm", "o_s_nm", "o_s_gs", "o_s_hs") if sample else ("o_p_cm", "o_p_gs", "o_p_hs")
            for n, src in zip(names, (cm, nm, gs, hs) if sample else (cm, gs, hs)):
                sp.dma_start(d[n], src[:]).then_inc(S("saved"), 16)
            sp.wait_ge(S("saved"), 16 * len(names))
            for u in range(nbuf):
                sp.wait_ge(y_out[u], 16 * (1 if sample else TILES // 2 + 1))

        const_n = 16 * (12 if sample else 4)

        @block.tensor
        def _(pe):
            pe.wait_ge(S("const_in"), const_n)
            pe.wait_ge(S("consts"), CONSTS)

            def finish(t, u, r):
                pe.wait_ge(S("yn"), t + 1)
                if not sample:
                    pe.wait_ge(S("hs"), t + 2)
                for k in range(KT):
                    mm = pe.transpose(pd[:, k // 4, (k % 4) * P:(k % 4 + 1) * P],
                                      y[:, 2 * k:2 * k + 2, :].rearrange("p h c -> p (h c)"), keep["ident"][:])
                mm.then_inc(S("y_turned"), 1)

            def body(t, u, r, first, last):
                v = lambda n, c: t * n + c
                z = zt[u]

                def turn(bank_, rows):
                    for n, row in enumerate(rows):
                        mm = pe.transpose(bank_[:, n // 4, (n % 4) * P:(n % 4 + 1) * P], z[:, row, :], keep["ident"][:])
                    mm.then_inc(S("turned"), 1)

                pe.wait_ge(z_in[u], 32 * (r + 1))
                for dst, keys, queries, done, free in ((pb, R_GK, R_GK, "kk", "vn"), (pc, R_GK, R_GQ, "qk_g", "o_gdn"),
                                                       (pa, R_MK, R_MQ, "qk_m", "state_read")):
                    pe.wait_ge(S(free), v(1, 1))
                    for par in range(2):
                        for j in range(3):
                            mm = pe.matmul(dst[:, par, j * P:(j + 1) * P], z[half(par), keys + j, :],
                                           z[half(par), queries + j, :], start=True, stop=True)
                    mm.then_inc(S(done), 1)

                def six(dst, lhs, rhs, done):
                    for h in range(MH):
                        mm = pe.matmul(dst[:, h // 3, (h % 3) * P:(h % 3 + 1) * P], lhs(h), rhs(h), start=True, stop=True)
                    mm.then_inc(S(done), 1)

                def step(what, i):
                    if what == "turn":
                        if not first:
                            finish(t - 1, 1 - u, r)
                        pe.wait_ge(S("attn"), v(1, 1))
                        pe.wait_ge(S("pm"), v(1, 1))
                        turn(pc, [R_GK, R_GK + 1, R_GK + 2, R_GV, R_GV + 1, R_GV + 2])
                        turn(pa, [R_MK, R_MK + 1, R_MK + 2, R_MV, R_MV + 1, R_MV + 2, R_HI, R_HI + 1])
                    elif what == "round":
                        j, g = groups[i]
                        if i == 0:
                            pe.wait_ge(S("hkq"), v(3, 3))
                            pe.wait_ge(S("gated"), v(1, 1))
                        else:
                            pe.wait_ge(S("masked"), v(R, i))
                        for par in range(2):
                            for n in range(4):
                                l = 4 * g + n - 1
                                if l < 0:
                                    a, b = z[half(par), R_HG0 + 2 * j + 1, :], z[half(par), R_HQ + j, :]
                                else:
                                    a, b = hk[half(par), l, j, :], hq[half(par), l, j, :]
                                mm = pe.matmul(pd[:, par, n * P:(n + 1) * P], a, b, start=True, stop=True)
                        mm.then_inc(S("round"), 1)
                    elif what == "mlstm":
                        pe.wait_ge(S("tok_a"), v(2, 2))
                        pe.wait_ge(S("tok_d"), v(3, 3))
                        if sample:
                            pe.wait_ge(S("qx"), 2)
                        else:
                            pe.wait_ge(S("cm"), v(1, 1))
                        W = HD + 1
                        for h in range(MH):
                            par, j = h // 3, h % 3
                            pe.matmul(pa[:, par, j * W:(j + 1) * W], pm[:, h, :], v1[:, h, :], start=True, stop=True)
                            o = pa[:, par, (3 + j) * W:(4 + j) * W]
                            if sample:
                                for b in range(NB):
                                    pe.matmul(o[:, 0:HD], qx[half(par), j, b, :], cm[half(par), j, b, :],
                                              start=(b == 0), stop=(b == NB - 1))
                                for b in range(NB):
                                    mm = pe.matmul(o[:, HD:W], qx[half(par), j, b, :], nm[half(par), j, b:b + 1],
                                                   start=(b == 0), stop=(b == NB - 1))
                            else:
                                mm = pe.matmul(o, z[half(par), R_MQ + j, :], cm[half(par), j, :], start=True, stop=True)
                        mm.then_inc(S("mo"), 1)
                    elif what == "hgrn":
                        pe.wait_ge(S("masked"), v(R, R))
                        pe.wait_ge(S("tok_a"), v(2, 2))
                        if sample:
                            pe.wait_ge(S("qx"), 1)
                        else:
                            pe.wait_ge(S("hs"), v(1, 1))
                        for par in range(2):
                            for j in range(2):
                                o = pd[:, par, j * HD:(j + 1) * HD]
                                for n in range(terms):
                                    pe.matmul(o, ph[:, 2 * par + j, n, :], hv[:, 2 * j + par, :], start=(n == 0), stop=False)
                                if sample:
                                    for b in range(NB):
                                        pe.matmul(o, qx[half(par), j, b, :], hs[half(par), j, b, :], start=False,
                                                  stop=(b == NB - 1))
                                else:
                                    pe.matmul(o, hq[half(par), LEVELS, j, :], hs[half(par), j, :], start=False, stop=True)
                        for j in range(2):
                            mm = pe.transpose(pd[:, 0, (j + 1) * P:(j + 2) * P], hk[:, LEVELS, j, :], keep["ident"][:])
                        mm.then_inc(S("ho"), 1)
                        if not sample:
                            pe.wait_ge(S("kd"), v(1, 1))
                            for par in range(2):
                                for j in range(2):
                                    mm = pe.matmul(pd[half(par), 1, P + j * HD:P + (j + 1) * HD], kd[:, 2 * j + par, :],
                                                   hv[:, 2 * j + par, :], start=True, stop=True)
                            mm.then_inc(S("dh"), 1)

                for l in range(halvings):
                    pe.wait_ge(S("cl"), v(halvings, l + 1))
                    if l:
                        pe.wait_ge(S("x"), v(2 * halvings, 2 * l))
                    if l == 0:
                        pe.wait_ge(S("lt"), v(1, 1))
                    six(pb, lambda h: cl[:, l % 3, h, :], lambda h: x[:, h, :] if l else ident_r[:], "m1")
                    for what, i in fill[l]:
                        step(what, i)
                    if l == 1:
                        pe.wait_ge(S("tok_d"), v(3, 2))
                    if l:
                        pe.wait_ge(S("m1_copy"), v(halvings - 1, l))
                        six(pc, lambda h: xt[:, h, :], lambda h: m1[:, h, :], "u")
                        six(pb, lambda h: m1[:, h, :], lambda h: xt[:, h, :], "u")
                for what, i in rest:
                    step(what, i)
                pe.wait_ge(S("x"), v(2 * halvings, 2 * halvings))
                six(pc, lambda h: lt[:, h, :], lambda h: x[:, h, :].bitcast(F32), "lx")
                if not sample:
                    pe.wait_ge(S("num"), v(1, 1))
                    for h in range(MH):
                        par, j = h // 3, h % 3
                        mm = pe.matmul(pa[half(par), 0, j * (HD + 1):(j + 1) * (HD + 1)], kw[:, h, :], v1[:, h, :],
                                       start=True, stop=True)
                    mm.then_inc(S("dm"), 1)
                pe.wait_ge(S("w"), v(1, 1))
                six(pb, lambda h: wn[:, h, :], lambda h: xt[:, h, :].bitcast(F32), "wx")
                if not sample:
                    pe.wait_ge(S("gs"), v(1, 1))
                pe.wait_ge(S("xf"), v(1, 1))
                for n, (dst, row) in enumerate(((pb, R_GK), (pc, R_GQ))):
                    if sample:
                        pe.wait_ge(S("qx"), 3 + n)
                    for par in range(2):
                        for j in range(3):
                            if sample:
                                for b in range(NB):
                                    mm = pe.matmul(dst[:, par, j * HD:(j + 1) * HD], qx[half(par), j, b, :],
                                                   gs[half(par), j, b, :], start=(b == 0), stop=(b == NB - 1))
                            else:
                                mm = pe.matmul(dst[:, par, j * HD:(j + 1) * HD], z[half(par), row + j, :],
                                               gs[half(par), j, :], start=True, stop=True)
                    mm.then_inc(S("ks"), 1)
                pe.wait_ge(S("rv"), v(2, 2))
                for h in range(MH):
                    mm = pe.matmul(pb[:, h // 3, (3 + h % 3) * HD:(4 + h % 3) * HD], xf[:, h, :], rv[:, h, :],
                                   start=True, stop=True)
                mm.then_inc(S("xr"), 1)
                pe.wait_ge(S("vn"), v(1, 2))
                for h in range(MH):
                    mm = pe.matmul(pc[:, h // 3, (3 + h % 3) * HD:(4 + h % 3) * HD], at_[:, h, :], vn[:, h, :],
                                   start=True, stop=True)
                mm.then_inc(S("av"), 1)
                if not sample:
                    for h in range(MH):
                        par, j = h // 3, h % 3
                        mm = pe.matmul(pa[half(par), 1, j * HD:(j + 1) * HD], gkw[:, h, :], vn[:, h, :], start=True, stop=True)
                    mm.then_inc(S("dg"), 1)
                if sample:
                    finish(0, 0, 0)
                    pe.wait_ge(S("num"), 1)
                    for h in range(MH):
                        mm = pe.matmul(pa[half(h // 3), 0, (h % 3) * NB:(h % 3 + 1) * NB], kw[:, h, :], one_s[:],
                                       start=True, stop=True)
                    mm.then_inc(S("dn"), 1)
                    pe.wait_ge(S("kd"), 1)
                    for n, (keys, at) in enumerate([(kw, j) for j in range(3)] + [(gkw, j) for j in range(3)] +
                                                   [(kd, j) for j in range(2)]):
                        pe.wait_ge(S("vx"), n + 1)
                        for par in range(2):
                            key = keys[:, 2 * at + par, :] if keys is kd else keys[:, 3 * par + at, :]
                            mm = pe.matmul(pa[half(par), 1, :], key, vx[:, par].rearrange("p b c -> p (b c)"),
                                           start=True, stop=True)
                        mm.then_inc(S("ds"), 1)
            tiles(pe, lambda *a: None, body, (lambda *a: None) if sample else finish)

        @block.scalar
        def _(act):
            act.preload_act_table_set(LN_EXP)
            act.wait_ge(S("const_in"), const_n)
            act.wait_ge(S("consts"), CONSTS)

            def before(t, u, r):
                decays(t)
                hgrn_decays(t)

            def decays(t):
                act.wait_ge(S("exa"), t + 1)
                act.activation(ex[:], ex[:], ACT.Exp).then_inc(S("ex"), 1)

            def hgrn_decays(t):
                act.wait_ge(S("nabs"), t + 1)
                act.activation(e[:], e[:], ACT.Exp).then_inc(S("e"), 1)

            def finish(t, u, r):
                act.wait_ge(S("o_gdn"), t + 2)
                act.wait_ge(S("y_h"), t + 1)
                act.activation(sq[:], y[:], ACT.Square).then_inc(S("sq"), 1)
                act.wait_ge(S("ss"), t + 1)
                act.activation(ss[:, 1, :], ss[:, 0, :], ACT.Ln, scale=1.0 / HD, bias=keep["eps"][:, :]).then_inc(S("rms"), 1)
                act.wait_ge(S("rms"), t * 2 + 1)
                act.activation(ss[:, 2, :], ss[:, 1, :], ACT.Exp, scale=-0.5).then_inc(S("rms"), 1)

            def body(t, u, r, first, last):
                v = lambda n, c: t * n + c

                def step(what, i):
                    if what == "turn":
                        act.wait_ge(S("turned"), v(2, 2))
                        act.activation(hm(v1[:])[:, :, :, 0:HD], tok(pa, 3), ACT.Copy).then_inc(S("tok_a"), 1)
                        act.activation(hv[:].rearrange("p h c -> p (h c)"), pa[:, 1, 2 * P:4 * P], ACT.Copy
                                       ).then_inc(S("tok_a"), 1)
                    elif what == "hgrn":
                        act.wait_ge(S("ho"), v(1, 1))
                        act.activation(ym(y[:, Y_H:16, :]), pv(pd, HD, n=2), ACT.Copy).then_inc(S("y_h"), 1)
                        act.activation(kd[:].rearrange("p h c -> p (h c)"), pd[:, 0, P:3 * P], ACT.Copy).then_inc(S("kd"), 1)

                if not first:
                    finish(t - 1, 1 - u, r)
                for l in range(halvings):
                    if l:
                        act.wait_ge(S("m1"), v(halvings, l + 1))
                        act.activation(hm(m1[:]), pv(pb, P), ACT.Copy).then_inc(S("m1_copy"), 1)
                    for what, i in fill[l]:
                        step(what, i)
                    if l == 4 and not last:
                        decays(t + 1)
                for what, i in rest:
                    step(what, i)
                if not last:
                    hgrn_decays(t + 1)
                act.wait_ge(S("xr"), v(1, 1))
                act.activation(hm(vn[:]), pv(pb, HD, 3 * HD), ACT.Copy).then_inc(S("vn"), 1)
            tiles(act, before, body, finish)

        @block.gpsimd
        def _(pool):
            pool.memset(zero[:], 0.0).then_inc(S("zero"), 1)
            pool.wait_ge(S("zero"), 1)
            pool.wait_ge(S("const_in"), const_n)
            pool.wait_ge(S("consts"), CONSTS)

            def decays(t, u):
                pool.wait_ge(S("ex"), t + 1)
                pool.tensor_tensor(bd[:], ex[:, :, 1, :], rb[u][:, :, 2, :], ALU.mult).then_inc(S("bd"), 1)
                pool.wait_ge(S("bd"), t * 2 + 1)
                pool.tensor_tensor(bd[:], bd[:], late[:, 1:2, :].broadcast_to([P, MH, P]), ALU.mult).then_inc(S("bd"), 1)

            def differences(t, u, r):
                g = zt[u][:, R_HG0:NROW:2, :]
                pool.wait_ge(z_in[u], 32 * (r + 1))
                if not sample:
                    pool.wait_ge(S("hs"), t + 1)
                for l in range(LEVELS + 2):
                    if l == LEVELS:
                        ins = pool.tensor_tensor(e[:, l], g, zero[:].unsqueeze(2).broadcast_to([P, 2, P]), ALU.add)
                        continue
                    size, at = (2 << l, (1 << l) - 1) if l < LEVELS else ((NT, NT - 1) if sample else (P, P - 1))
                    gv = g.rearrange("p j (n b) -> p j n b", b=size)
                    for j in range(2):
                        ins = pool.tensor_tensor(e[:, l, j].rearrange("p (n b) -> p n b", b=size), gv[:, j],
                                                 gv[:, j, :, at:at + 1].broadcast_to([P, P // size, size]), ALU.subtract)
                ins.then_inc(S("diff"), 1)

            def before(t, u, r):
                differences(t, u, r)
                decays(t, u)

            def body(t, u, r, first, last):
                v = lambda n, c: t * n + c
                pool.wait_ge(S("lt"), v(1, 1))
                for l in range(halvings):
                    if l >= 3:
                        pool.wait_ge(S("m1"), v(halvings, l - 1))
                    pool.tensor_tensor(cl[:, l % 3], lt[:], level[:, l + 1:l + 2, :].broadcast_to([P, MH, P]),
                                       ALU.mult).then_inc(S("cl"), 1)
                if not last:
                    decays(t + 1, 1 - u)
                    differences(t + 1, 1 - u, r + u)
            tiles(pool, before, body, lambda *a: None)

        @block.vector
        def _(dve):
            dve.memset(den[:, 0, 0:1], 0.0).then_inc(S("vn"), 1)
            dve.memset(den[:, 0, 1:2], 0.0).then_inc(S("o_gdn"), 1)
            dve.memset(den[:, 0, 2:3], 0.0).then_inc(S("state_read"), 1)
            dve.memset(den[:, 0, 3:4], 0.0).then_inc(S("gated"), 1)
            if sample:
                dve.memset(zt[0][:, :, SAMP:P], 0.0).then_inc(S("pads"), 1)
                dve.memset(rb[0][:, :, :, SAMP:P], 0.0).then_inc(S("pads"), 1)
                dve.memset(cc[0][:], 0.0).then_inc(S("pads"), 1)
                dve.wait_ge(S("pads"), 3)
            else:
                dve.memset(cm[:], 0.0).then_inc(S("cm"), 1)
                dve.memset(gs[:], 0.0).then_inc(S("gs"), 1)
                dve.memset(hs[:], 0.0).then_inc(S("hs"), 1)
                dve.memset(den[:, 0, 4:5], 0.0).then_inc(y_out[0], 16)
                dve.memset(den[:, 0, 5:6], 0.0).then_inc(y_out[1], 16)
            dve.memset(v1[:, :, HD:HD + 1], 1.0).then_inc(S("consts"), 1)
            dve.wait_ge(S("const_in"), const_n)
            dve.tensor_copy(ident_r[:], keep["ident"][:]).then_inc(S("consts"), 1)
            ident4 = keep["ident"][:].unsqueeze(1).unsqueeze(1).broadcast_to([P, 2, 3, P])
            STEPS = 64

            def chain(sem, base):
                count = [0]

                def then(ins):
                    count[0] += 1
                    ins.then_inc(S(sem), 1)
                    dve.wait_ge(S(sem), base + count[0])
                return then, count

            def decays(t, u, r, then):
                dve.wait_ge(z_in[u], 32 * (r + 1))
                if sample:
                    then(dve.tensor_copy(cc[0][0:SAMP], keep["cols_s"][:]))
                else:
                    dve.tensor_scalar(cc[u][:], keep["cols_p"][:, :, bass.ds(t * MH, MH)], 1.0, None, ALU.mult)
                    for par in range(2):
                        ins = dve.tensor_scalar(dc[u][half(par)], dec[half(par), :, bass.ds(t, 1), 3 * par:3 * par + 3]
                                                .rearrange("p w o j -> p w (o j)"), 1.0, None, ALU.mult)
                    then(ins)
                then(dve.tensor_tensor(ex[:], rb[u][:, :, 0:2, :], cc[u][:, Q_A:Q_NG + 1, :].rearrange("p k h -> p h k")
                                       .unsqueeze(3).broadcast_to([P, MH, 2, P]), ALU.add))
                dve.scalar_tensor_tensor(ex[:].rearrange("p h k c -> p (h k) c"), ex[:].rearrange("p h k c -> p (h k) c"),
                                         0.0, late[:, 0:1, :].broadcast_to([P, 2 * MH, P]), ALU.min,
                                         ALU.add).then_inc(S("exa"), 1)

            def distances(t):
                dve.wait_ge(S("diff"), t + 1)
                ef = e[:].rearrange("p l j c -> p (l j c)")
                dve.scalar_tensor_tensor(ef, ef, -1.0, ef, ALU.mult, ALU.min).then_inc(S("nabs"), 1)

            def hgrn_keys(t, u):
                kr = zt[u][:, R_HG0 + 1:NROW:2, :]
                dve.wait_ge(S("e"), t + 1)
                dve.tensor_tensor(hk[:, 0:LEVELS], e[:, 0:LEVELS], kr.unsqueeze(1).broadcast_to([P, LEVELS, 2, P]),
                                  ALU.mult).then_inc(S("hkq"), 1)
                dve.tensor_tensor(hk[:, LEVELS], e[:, LEVELS + 1], kr, ALU.mult).then_inc(S("hkq"), 1)

            def hgrn_queries(t, u):
                qr = zt[u][:, R_HQ:R_HQ + 2, :]
                dve.wait_ge(S("e"), t + 1)
                dve.tensor_tensor(hq[:], e[:, 0:LEVELS + 1], qr.unsqueeze(1).broadcast_to([P, LEVELS + 1, 2, P]),
                                  ALU.mult).then_inc(S("hkq"), 1)

            def before(t, u, r):
                decays(t, u, r, chain("step0", 0)[0])
                distances(t)
                hgrn_keys(t, u)
                hgrn_queries(t, u)

            def normalise(t):
                dve.wait_ge(S("sq"), t + 1)
                dve.tensor_reduce(ss[:, 0, :], sq[:], AX.X, ALU.add).then_inc(S("ss"), 1)

            def scale(t):
                dve.wait_ge(S("rms"), t * 2 + 2)
                dve.wait_ge(S("y_m"), t + 1)
                dve.tensor_tensor(y[:], y[:], ss[:, 2, :].unsqueeze(2).broadcast_to([P, 16, HD]),
                                  ALU.mult).then_inc(S("yn"), 1)

            def gate(t, u, r, then):
                if not sample:
                    dve.wait_ge(y_out[u], 16 * (r + 1))
                dve.wait_ge(S("y_turned"), t + 1)
                then(dve.tensor_tensor(yt[u][:], pd[:].rearrange("p a (k c) -> p (a k) c", c=P),
                                       zt[u][:, R_MO:R_MO + 8, :], ALU.mult))
                dve.tensor_copy(den[:, 0, 1:2], den[:, 1, 1:2]).then_inc(S("gated"), 1)

            def after(t, u, r):
                normalise(t)
                scale(t)
                gate(t, u, r, chain("step1", 0)[0])

            def body(t, u, r, first, last):
                v = lambda n, c: t * n + c
                z = zt[u]
                then, count = chain("step", t * STEPS)
                dve.wait_ge(S("bd"), v(2, 2))
                dve.wait_ge(S("kk"), v(1, 1))
                dve.tensor_tensor(hm(lt[:]), pv(pb, P), hm(bd[:]), ALU.mult).then_inc(S("lt"), 1)
                dve.wait_ge(S("qk_g"), v(1, 1))
                dve.tensor_tensor(hm(at_[:]), pv(pc, P), hm(ex[:, :, 1, :]), ALU.mult).then_inc(S("attn"), 1)
                dve.wait_ge(S("qk_m"), v(1, 1))
                dve.wait_ge(S("ex"), v(1, 1))
                dve.tensor_tensor(hm(pm[:]), pv(pa, P), hm(ex[:, :, 0, :]), ALU.mult).then_inc(S("pm"), 1)
                if not first:
                    normalise(t - 1)

                def spread(rows, pairs):
                    for j in range(pairs):
                        ins = dve.tensor_tensor(qx[:, j], rows[:, j:j + 1, :].broadcast_to([P, NB, P]), one_t[:], ALU.mult)
                    ins.then_inc(S("qx"), 1)

                def step(what, i):
                    if what == "turn":
                        dve.wait_ge(S("turned"), v(2, 1))
                        dve.tensor_tensor(hm(gkw[:]), tok(pc, 0), colh(u, Q_EGL, HD), ALU.mult).then_inc(S("tok_d"), 1)
                        dve.tensor_tensor(hm(bv[:]), tok(pc, 3), colh(u, Q_BETA, HD), ALU.mult).then_inc(S("tok_d"), 1)
                        dve.wait_ge(S("tok_a"), v(2, 2))
                        dve.tensor_tensor(hm(kw[:]), tok(pa, 0), colh(u, Q_WS, HD), ALU.mult).then_inc(S("tok_d"), 1)
                    elif what == "round":
                        j, g = groups[i]
                        dve.wait_ge(S("round"), v(R, i + 1))
                        dve.tensor_tensor(ph[:, j:HH:2, 4 * g:4 * g + 4, :], pv(pd, P, n=4),
                                          level[:, 4 * g:4 * g + 4, :].unsqueeze(1).broadcast_to([P, 2, 4, P]),
                                          ALU.mult).then_inc(S("masked"), 1)
                    elif what == "mlstm":
                        if sample:
                            dve.wait_ge(S("ho"), 1)
                            spread(z[:, R_MQ:R_MQ + 3, :], 3)
                        dve.wait_ge(S("mo"), v(1, 1))
                        W = HD + 1
                        then(dve.tensor_tensor(hm(num[:]), pv(pa, W, 3 * W), colh(u, Q_WI, W), ALU.mult))
                        ins = dve.tensor_tensor(hm(num[:]), hm(num[:]), pv(pa, W), ALU.add)
                        ins.then_inc(S("num"), 1)
                        dve.wait_ge(S("num"), v(1, 1))
                        then(dve.scalar_tensor_tensor(den[:, 0, :], num[:, :, HD], -1.0, num[:, :, HD], ALU.mult, ALU.max))
                        then(dve.tensor_scalar(den[:, 0, :], den[:, 0, :], 1.0, None, ALU.max))
                        then(dve.reciprocal(den[:, 1, :], den[:, 0, :]))
                        dve.tensor_tensor(ym(y[:, Y_M:Y_G, :]), hm(num[:])[:, :, :, 0:HD],
                                          den[:, 1, :].rearrange("p (r j) -> p r j", r=2).unsqueeze(3)
                                          .broadcast_to([P, 2, 3, HD]), ALU.mult).then_inc(S("y_m"), 1)
                        if not sample:
                            then(dve.tensor_tensor(cm[:], cm[:], dc[u][:, 0, :].unsqueeze(2).broadcast_to([P, 3, W]), ALU.mult))
                    else:
                        if sample:
                            spread(hq[:, LEVELS], 2)
                        dve.wait_ge(S("ho"), v(1, 1))
                        if not sample:
                            then(dve.tensor_tensor(hs[:], hs[:], e[:, LEVELS, :, P - 1:P].broadcast_to([P, 2, HD]), ALU.mult))
                            dve.wait_ge(S("dh"), v(1, 1))
                            dve.tensor_tensor(hs[:], hs[:], pd[:, 1, P:2 * P].rearrange("p (j c) -> p j c", j=2),
                                              ALU.add).then_inc(S("hs"), 1)

                for l in range(halvings):
                    if l:
                        for what, i in fill[l]:
                            step(what, i)
                    if l == 0:
                        dve.wait_ge(S("m1"), v(halvings, 1))
                        dve.tensor_tensor(hm(x[:]), ident4, pv(pb, P), ALU.subtract).then_inc(S("x"), 1)
                        dve.tensor_tensor(hm(xt[:]), ident4, hm(cl[:, 0].bitcast(F32)), ALU.subtract).then_inc(S("x"), 1)
                        if not first:
                            scale(t - 1)
                        for what, i in fill[0]:
                            step(what, i)
                        if not first:
                            gate(t - 1, 1 - u, r - 1 + u, then)
                    else:
                        U = 2 * (halvings - 1)
                        dve.wait_ge(S("u"), v(U, 2 * l - 1))
                        dve.wait_ge(S("x"), v(2 * halvings, 2 * l))
                        dve.tensor_tensor(hm(x[:]), hm(x[:].bitcast(F32)), pv(pc, P), ALU.subtract).then_inc(S("x"), 1)
                        dve.wait_ge(S("u"), v(U, 2 * l))
                        dve.tensor_tensor(hm(xt[:]), hm(xt[:].bitcast(F32)), pv(pb, P), ALU.subtract).then_inc(S("x"), 1)
                    if l == 4 and not last:
                        decays(t + 1, 1 - u, r + u, then)
                for what, i in rest:
                    step(what, i)
                dve.wait_ge(S("lx"), v(1, 1))
                dve.wait_ge(S("x"), v(2 * halvings, 2 * halvings))
                dve.tensor_tensor(hm(wn[:]), hm(x[:].bitcast(F32)), pv(pc, P), ALU.add).then_inc(S("w"), 1)
                if not sample:
                    dve.wait_ge(S("dm"), v(1, 1))
                    dve.tensor_tensor(cm[:], cm[:], pa[:, 0, 0:3 * (HD + 1)].rearrange("p (j c) -> p j c", j=3),
                                      ALU.add).then_inc(S("cm"), 1)
                dve.wait_ge(S("wx"), v(1, 1))
                dve.scalar_tensor_tensor(hm(xf[:]), hm(xt[:].bitcast(F32)), 2.0, pv(pb, P), ALU.mult,
                                         ALU.subtract).then_inc(S("xf"), 1)
                if not last:
                    distances(t + 1)
                if sample:
                    dve.wait_ge(S("mo"), 1)
                    spread(z[:, R_GK:R_GK + 3, :], 3)
                    dve.wait_ge(S("ks"), 1)
                    spread(z[:, R_GQ:R_GQ + 3, :], 3)
                dve.wait_ge(S("ks"), v(2, 1))
                dve.tensor_tensor(hm(rv[:]), pv(pb, HD), colh(u, Q_NBEG, HD), ALU.mult).then_inc(S("rv"), 1)
                dve.wait_ge(S("rv"), v(2, 1))
                dve.tensor_tensor(rv[:], rv[:], bv[:], ALU.add).then_inc(S("rv"), 1)
                if not last:
                    hgrn_keys(t + 1, 1 - u)
                dve.wait_ge(S("av"), v(1, 1))
                yg = ym(y[:, Y_G:Y_H, :])
                then(dve.tensor_tensor(yg, pv(pc, HD), colh(u, Q_EG, HD), ALU.mult))
                dve.tensor_tensor(yg, yg, pv(pc, HD, 3 * HD), ALU.add).then_inc(S("o_gdn"), 1)
                if not sample:
                    then(dve.tensor_tensor(gs[:], gs[:], dc[u][:, 1, :].unsqueeze(2).broadcast_to([P, 3, HD]), ALU.mult))
                    dve.wait_ge(S("dg"), v(1, 1))
                    dve.tensor_tensor(gs[:], gs[:], pa[:, 1, 0:3 * HD].rearrange("p (j c) -> p j c", j=3),
                                      ALU.add).then_inc(S("gs"), 1)
                    dve.tensor_copy(den[:, 0, 0:1], den[:, 1, 0:1]).then_inc(S("state_read"), 1)
                if not last:
                    hgrn_queries(t + 1, 1 - u)
                assert count[0] < STEPS
                dve.tensor_copy(den[:, 0, 2:3], den[:, 1, 2:3]).then_inc(S("step"), STEPS - count[0])
            tiles(dve, before, body, after)
            if not sample:
                dve.wait_ge(S("gs"), TILES + 1)
                dve.tensor_copy(den[:, 0, 3:4], den[:, 1, 3:4]).then_inc(S("states"), 3)
                return
            dve.tensor_tensor(nm[:], nm[:], dc[:, 0], ALU.mult).then_inc(S("decayed"), 1)
            by_seq = lambda a, n: a.unsqueeze(3).broadcast_to([P, n, NB, HD])
            dve.tensor_tensor(cm[:], cm[:], by_seq(dc[:, 0], 3), ALU.mult).then_inc(S("decayed"), 1)
            dve.tensor_tensor(gs[:], gs[:], by_seq(dc[:, 1], 3), ALU.mult).then_inc(S("decayed"), 1)
            dve.tensor_tensor(hs[:], hs[:], by_seq(e[:, LEVELS, :, NT - 1:SAMP:NT], 2), ALU.mult).then_inc(S("decayed"), 1)
            dve.wait_ge(S("decayed"), 4)
            dve.wait_ge(S("dn"), 1)
            dve.tensor_tensor(nm[:], nm[:], pa[:, 0, 0:3 * NB].rearrange("p (j b) -> p j b", b=NB), ALU.add
                              ).then_inc(S("states"), 1)
            for n, (state, vals, j) in enumerate([(cm, v1, j) for j in range(3)] + [(gs, vn, j) for j in range(3)] +
                                                 [(hs, hv, j) for j in range(2)]):
                val = vals[:, 2 * j:2 * j + 2, :] if vals is hv else vals[:, j:MH:3, 0:HD]
                dve.tensor_tensor(vx[:], val.unsqueeze(2).broadcast_to([P, 2, NB, HD]),
                                  one_s[:].unsqueeze(1).unsqueeze(3).broadcast_to([P, 2, NB, HD]), ALU.mult
                                  ).then_inc(S("vx"), 1)
                dve.wait_ge(S("ds"), n + 1)
                ins = dve.tensor_tensor(state[:, j], state[:, j], pa[:, 1, :].rearrange("p (b c) -> p b c", b=NB), ALU.add)
            ins.then_inc(S("states"), 2)


BLOCKS = 4
BP, BS = SEQ // BLOCKS, SAMP // BLOCKS
BT = BP + BS
UNITS = [("out", 0), ("ff1", 0), ("ff1", 1), ("ff2", 0), ("ff1", 2), ("ff2", 1), ("ff1", 3), ("ff2", 2), ("ff2", 3)]
CHUNKS = len(UNITS) * KT
ROWS = [(i * P, P) for i in range(BP // P)] + [(BP, BS)]


def feed_forward(nc, d, keep):
    with ExitStack() as ctx:
        sb = lambda n, s, t=F32: ctx.enter_context(nc.sbuf_tensor("ff_" + n, s, t))
        S = Sems(nc, ctx, "ff_")
        a_hi, a_lo = (sb(n, [P, 2, KT, BT], F32R) for n in ("a_hi", "a_lo"))
        h_hi, h_lo = (sb(n, [P, KT, BT], F32R) for n in ("h_hi", "h_lo"))
        out = sb("out", [P, KT, BT])
        x1 = sb("x1", [P, len(ROWS), D])
        w = sb("w", [P, 2, KT, P])
        w_hi, w_lo = (sb(n, [P, 2, KT, P], F32R) for n in ("w_hi", "w_lo"))
        gate_p = sb("gate_p", [P, 2, D])
        gate_s = sb("gate_s", [BS, 2, D])
        tmp, xs, junk = (sb(n, [P, D]) for n in ("tmp", "xs", "junk"))
        ht = sb("ht", [P, KT, P])
        sqf = sb("sqf", [P, 2, BT])
        stat = sb("stat", [P, 6])
        one = sb("one", [P, 1])
        const_one = S("const_one")
        refined = S("refined")
        acc = ctx.enter_context(nc.psum_tensor("ff_acc", [P, 2, 2, 512], F32))
        ty = ctx.enter_context(nc.psum_tensor("ff_ty", [P, D], F32))
        th = ctx.enter_context(nc.psum_tensor("ff_th", [P, KT, P], F32))
        w_in = [S("w_in0"), S("w_in1")]
        (const_in, x_in, y_in, stored, split_hi, split_lo, product, drained, in_hi, in_lo, squared, f_hi, f_lo,
         turned, ssum, slog, rstd, scaled, x_done, hsum, hlog, hrstd, xs_ready, h_turned, h_mod, h_shift, h_hi_ready,
         h_lo_ready, left) = (
            S(n) for n in ("const_in", "x_in", "y_in", "stored", "split_hi", "split_lo", "product", "drained",
                           "in_hi", "in_lo", "squared", "f_hi", "f_lo", "turned", "ssum", "slog", "rstd", "scaled",
                           "x_done", "hsum", "hlog", "hrstd", "xs_ready", "h_turned", "h_mod", "h_shift",
                           "h_hi_ready", "h_lo_ready", "left"))
        NR = len(ROWS)
        REFINES = 4 * 3 * NR
        G = BT // 2

        def blocks(eng, body):
            with eng.Fori(0, BLOCKS) as b:
                body(b)

        def chunks(eng, b, unit, body):
            with eng.Fori(0, KT // 2) as pair:
                for c in range(2):
                    body(b * CHUNKS + pair * 2 + (unit * KT + c), pair * 2 + c, c,
                         b * (CHUNKS // 2) + pair + unit * (KT // 2))

        block = ctx.enter_context(nc.Block())

        @block.sync
        def _(sp):
            def body(b):
                for unit, (kind, q) in enumerate(UNITS):
                    src = d["w_unit"][{"out": 0, "ff1": 1 + 2 * q, "ff2": 2 + 2 * q}[kind]]

                    def load(n, oc, u, use):
                        sp.wait_ge(split_lo, n + 1)
                        sp.dma_start(w[:, u].rearrange("p k c -> p (k c)"),
                                     src[bass.ds(oc, 1)].rearrange("o p c -> (o p) c")).then_inc(w_in[u], 16)
                    chunks(sp, b, unit, load)
            blocks(sp, body)

        @block.gpsimd
        def _(pool):
            pool.memset(one[:], 1.0).then_inc(const_one, 1)
            pool.wait_ge(const_one, 1)
            ones = one[:].unsqueeze(2).broadcast_to([P, KT, P])

            def body(b):
                for unit in range(len(UNITS)):
                    def split(n, oc, u, use):
                        pool.wait_ge(w_in[u], use * 16 + 16)
                        pool.wait_ge(product, n + 1)
                        pool.tensor_tensor(w_hi[:, u], w[:, u], ones, ALU.mult).then_inc(split_hi, 1)
                        pool.wait_ge(split_hi, n + 1)
                        pool.tensor_tensor(w_lo[:, u], w[:, u], w_hi[:, u].bitcast(F32), ALU.subtract).then_inc(split_lo, 1)
                    chunks(pool, b, unit, split)
            blocks(pool, body)

        @block.tensor
        def _(pe):

            def turn_out(b, i, second):
                at, n = ROWS[i]
                m = b * (2 * NR) + (second * NR + i)
                pe.wait_ge(scaled, m + 1)
                for k in range(KT):
                    mm = pe.transpose(ty[0:n, k * P:(k + 1) * P], out[:, k, at:at + n], keep["ident"][:])
                mm.then_inc(turned, 1)

            def turn_h(b, i):
                pe.wait_ge(xs_ready, b * NR + i + 1)
                pe.wait_ge(h_mod, b * NR + i + 1)
                for k in range(KT):
                    mm = pe.transpose(th[:, k, :], xs[:, k * P:(k + 1) * P], keep["ident"][:])
                mm.then_inc(h_turned, 1)

            def body(b):
                for unit, (kind, q) in enumerate(UNITS):
                    if kind == "out":
                        ready = (in_lo, b + 1)
                        src = lambda k: (a_hi[:, 0, k], a_lo[:, 0, k])
                    elif kind == "ff1":
                        ready = (h_lo_ready, b * NR + NR)
                        src = lambda k: (h_hi[:, k], h_lo[:, k])
                    else:
                        ready = (f_lo, b * (4 * KT) + (q + 1) * KT)
                        src = lambda k, u=q % 2: (a_hi[:, u, k], a_lo[:, u, k])

                    def products(n, oc, u, use):
                        pe.wait_ge(*ready)
                        pe.wait_ge(split_lo, n + 3)
                        pe.wait_ge(drained, n + 1)
                        for g in range(2):
                            cols = slice(g * G, (g + 1) * G)
                            for k in range(KT):
                                hi, lo = src(k)
                                dst = acc[:, u, g, 0:G]
                                pe.matmul(dst, w_hi[:, u, k], hi[:, cols], start=(k == 0), stop=False)
                                pe.matmul(dst, w_hi[:, u, k], lo[:, cols], start=False, stop=False)
                                mm = pe.matmul(dst, w_lo[:, u, k], hi[:, cols], start=False, stop=(k == KT - 1))
                        mm.then_inc(product, 1)
                    chunks(pe, b, unit, products)
                    if kind == "out":
                        pe.wait_ge(drained, b * CHUNKS + KT + 2)
                        turn_out(b, 0, 0)
                        for i in range(NR):
                            if i + 1 < NR:
                                turn_out(b, i + 1, 0)
                            turn_h(b, i)
                pe.wait_ge(drained, b * CHUNKS + CHUNKS + 2)
                for i in range(NR):
                    turn_out(b, i, 1)
            blocks(pe, body)

        @block.scalar
        def _(act):
            act.preload_act_table_set(LN_EXP)
            for i in range(2):
                act.dma_start(gate_p[:, i, :], d["gates"][SAMP:SAMP + 1, i, :].broadcast_to([P, D])).then_inc(const_in, 16)

            def rms(b, i, second, src, sums, logs, roots, count, at):
                n = ROWS[i][1]
                act.activation(junk[0:n, :], src, ACT.Square, accum_out=stat[0:n, at:at + 1]).then_inc(sums, 1)
                act.wait_ge(sums, count)
                act.activation(stat[0:n, at + 1:at + 2], stat[0:n, at:at + 1], ACT.Ln, scale=1.0 / D,
                               bias=keep["eps"][0:n, :]).then_inc(logs, 1)
                act.wait_ge(logs, count)
                act.activation(stat[0:n, at + 2:at + 3], stat[0:n, at + 1:at + 2], ACT.Exp, scale=-0.5).then_inc(roots, 1)

            def body(b):
                act.wait_ge(left, b + 1)
                met(act, left)
                for i in range(BP // P):
                    act.dma_start(out[:, :, i * P:(i + 1) * P], d["yT"][bass.ds(b * (BP // P) + i, 1)]
                                  .rearrange("o p k c -> (o p) k c")).then_inc(y_in, 16)
                act.dma_start(out[:, :, BP:BT], d["yT_s"][:, :, bass.ds(b * BS, BS)]).then_inc(y_in, 16)
                act.dma_start(gate_s[:], d["gates"][bass.ds(b * BS, BS)]).then_inc(x_in, 16)
                act.wait_ge(stored, b * 32 + 32)
                met(act, left)
                act.dma_start(x1[:, 0:BP // P, :], d["x"][bass.ds(b * BP, BP), :].rearrange("(i p) c -> p i c", p=P)
                              ).then_inc(x_in, 16)
                act.dma_start(x1[0:BS, BP // P, :], d["x"][bass.ds(b * BS + SEQ, BS), :]).then_inc(x_in, 16)
                act.wait_ge(y_in, b * 80 + 80)
                act.activation(a_hi[:, 0], out[:], ACT.Copy).then_inc(in_hi, 1)
                for i in range(NR):
                    n = ROWS[i][1]
                    act.wait_ge(turned, b * (2 * NR) + i + 1)
                    rms(b, i, 0, ty[0:n, :], ssum, slog, rstd, b * (2 * NR) + i + 1, 0)
                    act.wait_ge(x_done, b * (2 * NR) + i + 2)
                    rms(b, i, 0, x1[0:n, i, :], hsum, hlog, hrstd, b * NR + i + 1, 3)
                    act.wait_ge(refined, b * REFINES + 8 * (i + 1))
                    act.activation(xs[0:n, :], x1[0:n, i, :], ACT.Copy, scale=stat[0:n, 5:6]).then_inc(xs_ready, 1)
                    act.wait_ge(h_shift, b * NR + i + 1)
                    at = ROWS[i][0]
                    act.activation(h_hi[:, :, at:at + n], ht[:, :, 0:n], ACT.Copy).then_inc(h_hi_ready, 1)
                for unit, (kind, q) in enumerate(UNITS):
                    if kind == "ff1":
                        def part(n, oc, u, use):
                            act.wait_ge(squared, b * (4 * KT) + (q * KT) + oc + 1)
                            met(act, left)
                            act.activation(a_hi[:, q % 2, bass.ds(oc, 1), :].rearrange("p o c -> p (o c)"),
                                           sqf[:, u], ACT.Copy).then_inc(f_hi, 1)
                        chunks(act, b, unit, part)
                for i in range(NR):
                    n = ROWS[i][1]
                    act.wait_ge(turned, b * (2 * NR) + NR + i + 1)
                    rms(b, i, 1, ty[0:n, :], ssum, slog, rstd, b * (2 * NR) + NR + i + 1, 0)
                act.wait_ge(x_done, b * (2 * NR) + 2 * NR + 1)
                met(act, left)
                act.dma_start(d["y"][bass.ds(b * BP, BP), :].rearrange("(i p) c -> p i c", p=P),
                              x1[:, 0:BP // P, :]).then_inc(stored, 16)
                act.dma_start(d["y"][bass.ds(b * BS + SEQ, BS), :], x1[0:BS, BP // P, :]).then_inc(stored, 16)
            blocks(act, body)
            act.wait_ge(stored, BLOCKS * 32 + 32)

        @block.vector
        def _(dve):
            dve.memset(stat[:, 0:1], 0.0).then_inc(split_lo, 2)
            dve.memset(stat[:, 1:2], 0.0).then_inc(product, 2)
            dve.memset(stat[:, 2:3], 0.0).then_inc(drained, 2)
            dve.memset(stat[:, 3:4], 0.0).then_inc(scaled, 1)
            dve.memset(stat[:, 4:5], 0.0).then_inc(h_mod, 1)
            dve.memset(stat[:, 5:6], 0.0).then_inc(left, 1)
            dve.memset(tmp[:, 0:1], 0.0).then_inc(stored, 32)
            dve.memset(tmp[:, 1:2], 0.0).then_inc(x_done, 1)
            dve.wait_ge(const_in, 32)

            count = [0]

            def refine(b, n, at):
                ss, v, r = (stat[0:n, at + k:at + k + 1] for k in range(3))
                for ins in (lambda: dve.tensor_scalar(v, ss, 1.0 / D, EPS, ALU.mult, ALU.add),
                            lambda: dve.scalar_tensor_tensor(v, r, v, r, ALU.mult, ALU.mult),
                            lambda: dve.tensor_scalar(v, v, -0.5, 1.5, ALU.mult, ALU.add),
                            lambda: dve.tensor_tensor(r, r, v, ALU.mult)):
                    count[0] += 1
                    ins().then_inc(refined, 1)
                    dve.wait_ge(refined, b * REFINES + count[0])

            def residual(b, i, second):
                n = ROWS[i][1]
                m = b * (2 * NR) + (second * NR + i)
                gate = gate_p[:, second, :] if n == P else gate_s[:, second, :]
                dve.wait_ge(rstd, m + 1)
                refine(b, n, 0)
                dve.wait_ge(x_done, m + 1)
                dve.scalar_tensor_tensor(tmp[0:n, :], ty[0:n, :], stat[0:n, 2:3], gate, ALU.mult,
                                         ALU.mult).then_inc(scaled, 1)
                dve.wait_ge(scaled, m + 2)
                dve.tensor_tensor(x1[0:n, i, :], x1[0:n, i, :], tmp[0:n, :], ALU.add).then_inc(x_done, 1)

            def body(b):
                count[0] = 0
                dve.wait_ge(in_hi, b + 1)
                dve.tensor_tensor(a_lo[:, 0], out[:], a_hi[:, 0].bitcast(F32), ALU.subtract).then_inc(in_lo, 1)
                for unit, (kind, q) in enumerate(UNITS):
                    def drain(n, oc, u, use):
                        dve.wait_ge(product, n + 3)
                        dst = out[:, bass.ds(oc, 1), :].rearrange("p o (g c) -> p (o g) c", g=2)
                        src = acc[:, u, :, 0:G]
                        dve.wait_ge(drained, n + 2)
                        if kind == "ff1":
                            sq = sqf[:, u].rearrange("p (g c) -> p g c", g=2)
                            dve.tensor_scalar(sq, src, 0.0, None, ALU.max).then_inc(drained, 1)
                            dve.wait_ge(drained, n + 3)
                            dve.tensor_tensor(sq, sq, sq, ALU.mult).then_inc(squared, 1)
                            dve.wait_ge(f_hi, b * (4 * KT) + (q * KT) + oc + 1)
                            dve.tensor_tensor(a_lo[:, q % 2, bass.ds(oc, 1), :].rearrange("p o c -> p (o c)"), sqf[:, u],
                                              a_hi[:, q % 2, bass.ds(oc, 1), :].rearrange("p o c -> p (o c)").bitcast(F32),
                                              ALU.subtract).then_inc(f_lo, 1)
                        elif kind == "ff2" and q:
                            dve.tensor_tensor(dst, dst, src, ALU.add).then_inc(drained, 1)
                        else:
                            dve.tensor_scalar(dst, src, 1.0, None, ALU.mult).then_inc(drained, 1)
                    chunks(dve, b, unit, drain)
                    if kind == "out":
                        dve.wait_ge(x_in, b * 48 + 48)
                        for i in range(NR):
                            at, n = ROWS[i]
                            residual(b, i, 0)
                            if n == P:
                                s2, b2 = (keep[m][:, :, SAMP:SAMP + 1].broadcast_to([P, KT, P]) for m in ("A2", "B2"))
                            else:
                                s2, b2 = (keep[m][:, :, bass.ds(b * BS, BS)] for m in ("A2", "B2"))
                            dve.wait_ge(hrstd, b * NR + i + 1)
                            refine(b, n, 3)
                            dve.wait_ge(h_turned, b * NR + i + 1)
                            dve.tensor_tensor(ht[:, :, 0:n], th[:, :, 0:n], s2, ALU.mult).then_inc(h_mod, 1)
                            dve.wait_ge(h_mod, b * NR + i + 2)
                            dve.tensor_tensor(ht[:, :, 0:n], ht[:, :, 0:n], b2, ALU.add).then_inc(h_shift, 1)
                            dve.wait_ge(h_hi_ready, b * NR + i + 1)
                            dve.tensor_tensor(h_lo[:, :, at:at + n], ht[:, :, 0:n], h_hi[:, :, at:at + n].bitcast(F32),
                                              ALU.subtract).then_inc(h_lo_ready, 1)
                for i in range(NR):
                    residual(b, i, 1)
                dve.wait_ge(x_done, b * (2 * NR) + 2 * NR + 1)
                dve.tensor_copy(tmp[:, 0:1], tmp[:, 1:2]).then_inc(left, 1)
            blocks(dve, body)


def program(nc, d):
    with ExitStack() as ctx:
        sb = lambda n, s, t=F32: ctx.enter_context(nc.sbuf_tensor(n, s, t))
        keep = {n: sb(n, [P, KT, MODROWS]) for n in ("A2", "B2")}
        keep["ident"] = sb("ident", [P, P])
        cols = sb("cols", [P, NCOLS])
        keep["cols"] = cols
        v = lambda a, n, k: cols[:, a:a + n].rearrange("p (a b) -> p a b", a=k)
        keep["zcols"] = v(16, 2 * NCOL, 2)
        keep["ogate"] = v(16 + 66, 24, 3)
        keep["qscale"] = cols[:, 106:112]
        keep["convw"] = v(112, 36, 4)
        keep["eps"] = cols[:, 150:151]
        keep["lbl"] = cols[:, 148:150]
        with ExitStack() as c2:
            sb2 = lambda n, s, t=F32: c2.enter_context(nc.sbuf_tensor(n, s, t))
            keep["A1"], keep["B1"] = sb2("A1", [P, KT, MODROWS]), sb2("B1", [P, KT, MODROWS])
            keep["headsum"] = sb2("headsum", [P, P])
            modulation(nc, d, keep)
            hi, lo = sb2("hi", [P, KT, TOK], F32R), sb2("lo", [P, KT, TOK], F32R)
            norm_in(nc, d, keep, hi, lo)
            project_in(nc, d, keep, hi, lo)
        with ExitStack() as c2:
            sb2 = lambda n, s, t=F32: c2.enter_context(nc.sbuf_tensor(n, s, t))
            keep["cols_p"] = sb2("cols_p", [P, NQ, TILES * MH])
            keep["cols_s"] = sb2("cols_s", [SAMP, NQ, MH])
            gates(nc, d, keep)
            mixers(nc, d, keep, False)
            mixers(nc, d, keep, True)
        feed_forward(nc, d, keep)


def lay_out(i):
    f = np.ascontiguousarray
    a = {n: np.asarray(v) for n, v in i.items()}
    z = lambda *s: np.zeros(s, np.float32)
    square = lambda w, n: w.reshape(KT, P, n, P).transpose(2, 1, 0, 3)
    c = np.concatenate([np.repeat(a["c_sample"], NT, axis=0), a["c_prompt"]])
    order = in_order()
    w_in = np.concatenate([a["w_in"][0], z(D, 1)], axis=1)[:, order]
    b_in = np.concatenate([a["b_in"][0], z(1)])[order]
    scale = np.ones((P, NCOL), np.float32)
    scale[:, 1 + R_MK:1 + R_MV] = HD ** -0.5
    n = a["mix_out_norm"][0]
    gate = np.stack([np.tile(np.array([0] * 3 + [1] * 5, np.float32), (P, 1)),
                     np.tile(np.array([1] * 3 + [0] * 5, np.float32), (P, 1)), n.reshape(8, P).T], 1)
    convw = a["gdn_conv_w"][0].reshape(CONV, 9, P).transpose(2, 0, 1)
    qscale = np.tile(np.array([HD ** -0.5] * 3 + [1.0] * 3, np.float32), (P, 1))
    cols = np.concatenate([a["norm_pre_mix"][0].reshape(KT, P).T, a["norm_pre_ffn"][0].reshape(KT, P).T, scale,
                           b_in.reshape(NCOL, P).T, gate.reshape(P, 24), qscale, convw.reshape(P, 36),
                           a["hgrn_lb_logits"][0].reshape(2, P).T, np.full((P, 1), EPS, np.float32)], axis=1)
    hist = a["state_gdn_conv"][0].reshape(NB, CONV - 1, 9, P).transpose(2, 3, 0, 1)
    ff1 = square(a["w_ff1"][0], DFF // P).reshape(4, 8, P, KT, P)
    ff2 = a["w_ff2"][0].reshape(4, KT, P, 8, P).transpose(0, 3, 2, 1, 4)
    units = np.concatenate([square(a["w_out"][0], 8)[None], np.stack([ff1, ff2], 1).reshape(8, 8, P, KT, P)])
    gcol = np.stack([a[n][0][HEADS] for n in ("mlstm_f_bias", "gdn_A_log", "gdn_dt_bias")], 1)
    o = {
        "gcol_p": np.tile(gcol, (TILES, 1)), "gcol_s": gcol, "m0": a["state_mlstm_m"][0].T[HEADS],
        "x": np.concatenate([a["x_prompt"][0], a["x_sample"].reshape(SAMP, D)]),
        "cT": c.T.reshape(KT, P, MODROWS).transpose(1, 0, 2),
        "w_ada": a["w_ada"][0].reshape(KT, P, ADA_CHUNKS, ADA_CHUNK).transpose(2, 1, 0, 3),
        "b_ada": a["b_ada"], "norm_post_mix": a["norm_post_mix"], "norm_post_ffn": a["norm_post_ffn"],
        "cols": cols, "ident": np.eye(P, dtype=np.float32),
        "headsum": np.kron(np.eye(P // HD), np.ones((HD, HD))).astype(np.float32),
        "w_in": square(w_in, NCOL), "hist": hist, "w_unit": units.reshape(9, 8, P, D),
    }
    s, t = np.arange(P)[:, None], np.arange(P)[None, :]
    pairs = [s == t] + [(s // n == t // n) & (s % n < n // 2) & (t % n >= n // 2) for n in (2 << l for l in range(LEVELS))]
    same = (s // NT == t // NT) & (s < SAMP) & (t < SAMP)
    o["level"] = np.stack(pairs, 1).astype(np.float32)
    o["late"] = np.stack([np.stack([np.where((s <= t) & ok, 0, -1e30), (s < t) & ok], 1) for ok in (s >= 0, same)]
                         ).astype(np.float32)
    seq = (np.arange(P)[None, :] // NT == np.arange(NB)[:, None]).astype(np.float32)
    o["one_t"], o["one_s"] = np.broadcast_to(seq, (P, NB, P)), seq.T
    rows = lambda w, n: w.reshape(NB, n, 2, HD, -1).transpose(2, 3, 1, 0, 4).reshape(P, n, NB, -1)
    o["s_cm"], o["s_gs"] = rows(a["state_mlstm_C"][0], 3), rows(a["state_gdn_S"][0], 3)
    o["s_hs"], o["s_nm"] = rows(a["state_hgrn_S"][0], 2), rows(a["state_mlstm_n"][0][..., None], 3)[..., 0]
    return {k: f(v) for k, v in o.items()}


INTERNAL = {
    "gates": (MODROWS, 2, D), "z": (TILES, P, NROW, P), "z_s": (P, NROW, SAMP), "gz": (4 * MH, TOK), "ends": (2, TILES * MH),
    "mprev": (TILES * MH,), "rows_p": (TILES, MH, 3, P), "rows_s": (MH, 3, SAMP), "dec_p": (2, TILES * MH),
    "dec_s": (2, MH, NB), "yT": (TILES, P, KT, P), "yT_s": (P, KT, SAMP),
}
OUTPUTS = {
    "y": (TOK, D), "p_conv": (9, P, CONV - 1), "s_conv": (9, P, NB, CONV - 1), "p_m": (MH, 1), "s_m": (MH, NB),
    "o_p_cm": (P, 3, HD + 1), "o_p_gs": (P, 3, HD), "o_p_hs": (P, 2, HD), "o_s_cm": (P, 3, NB, HD),
    "o_s_nm": (P, 3, NB), "o_s_gs": (P, 3, NB, HD), "o_s_hs": (P, 2, NB, HD),
}


def give_back(o):
    f = np.ascontiguousarray
    where = np.argsort(HEADS)
    prompt = lambda a, n: a.reshape(2, HD, n, -1).transpose(2, 0, 1, 3).reshape(1, 1, 2 * n, HD, -1)
    sample = lambda a, n: a.reshape(2, HD, n, NB, -1).transpose(3, 2, 0, 1, 4).reshape(1, NB, 2 * n, HD, -1)
    cm = prompt(o["o_p_cm"], 3)
    return tuple(f(a) for a in (
        o["y"][:SEQ].reshape(1, SEQ, D), o["y"][SEQ:].reshape(NB, NT, D),
        cm[..., :HD], cm[..., HD], o["p_m"][where, 0].reshape(1, 1, MH), prompt(o["o_p_gs"], 3),
        o["p_conv"].transpose(2, 0, 1).reshape(1, 1, CONV - 1, 9 * P), prompt(o["o_p_hs"], 2),
        sample(o["o_s_cm"], 3), sample(o["o_s_nm"], 3)[..., 0], o["s_m"][where].T.reshape(1, NB, MH),
        sample(o["o_s_gs"], 3), o["s_conv"].transpose(2, 3, 0, 1).reshape(1, NB, CONV - 1, 9 * P),
        sample(o["o_s_hs"], 2)))


def kernel(**inputs):
    import concourse.bacc as bacc
    from concourse.bass_utils import run_bass_kernel_spmd

    arrays = {"in_" + k: v for k, v in lay_out(inputs).items()}
    nc = bacc.Bacc("TRN2", target_bir_lowering=False, num_devices=1)
    d = {k[3:]: nc.dram_tensor(k, v.shape, mybir.dt.from_np(v.dtype), kind="ExternalInput").ap()
         for k, v in arrays.items()}
    for k, shape in INTERNAL.items():
        d[k] = nc.dram_tensor("tmp_" + k, shape, F32, kind="Internal").ap()
    for k, shape in OUTPUTS.items():
        d[k] = nc.dram_tensor("out_" + k, shape, F32, kind="ExternalOutput").ap()
    program(nc, d)
    r = run_bass_kernel_spmd(nc, [arrays], core_ids=[0])
    return give_back({k: np.asarray(r.results[0]["out_" + k]) for k in OUTPUTS})
```

```python
from contextlib import ExitStack

import numpy as np

import concourse.bass as bass
from concourse import mybir

F32 = mybir.dt.float32
F32R = mybir.dt.float32r
ALU = mybir.AluOpType
ACT = mybir.ActivationFunctionType
AX = mybir.AxisListType

P = 128
D = 1024
KT = D // P
SEQ, NB, NT = 2048, 8, 8
SAMP = NB * NT
TOK = SEQ + SAMP
TILES = SEQ // P
HD = 64
MH, GH, HH = 6, 6, 4
CONV = 4
EPS = 1e-6
LN_EXP = "natural_log_exp_and_others"
DFF = 4 * D
MODROWS = SAMP + 1
ADA_CHUNK = 512
ADA_CHUNKS = 6 * D // ADA_CHUNK
GROUP = -(-TOK // 5 // 8) * 8
GROUPS = [(at, min(GROUP, TOK - at)) for at in range(0, TOK, GROUP)]

C_GATE = 0
C_RAW = (1, 14)
C_OUTGATE = (14, 22)
C_CONVN = (22, 28)
C_CONVV = (28, 31)
C_FORGET = (31, 33)
NCOL = 33
HEADS = [0, 2, 4, 1, 3, 5]
R_MQ, R_MK, R_MV, R_HQ, R_HI, R_MO, R_GG, R_HG, R_GQ, R_GK, R_GV, R_HG0 = 0, 3, 6, 9, 11, 13, 16, 19, 21, 24, 27, 30
NROW = 34
NCOLS = 151


def in_order():
    mw, gw, hw = MH * HD, GH * HD, HH * HD
    at, o = {}, 0
    for name, n in (("mq", mw), ("mk", mw), ("mv", mw), ("mo", mw), ("mi", MH), ("mf", MH), ("gqkv", 3 * gw),
                    ("gg", gw), ("gb", GH), ("ga", GH), ("hq", hw), ("hf", hw), ("hi", hw), ("hg", hw)):
        at[name] = np.arange(o, o + n)
        o += n
    gates = np.concatenate([at[n][HEADS] for n in ("mi", "mf", "gb", "ga")])
    pad = np.full(P - gates.size, -1)
    q, k, v = np.split(at["gqkv"], 3)
    return np.concatenate([gates, pad, at["mq"], at["mk"], at["mv"], at["hq"], at["hi"], at["mo"], at["gg"],
                           at["hg"], q, k, v, at["hf"]])


def met(eng, sem):
    eng.wait_ge(sem, 1)


class Sems:

    def __init__(self, nc, ctx, prefix):
        self.nc, self.prefix, self.made = nc, prefix, {}
        ctx.callback(self.end)

    def end(self):
        self.nc.clear_and_free_semaphores(list(self.made.values()))
        self.nc.all_engine_barrier()

    def __call__(self, name):
        if name not in self.made:
            self.made[name] = self.nc.alloc_semaphore(self.prefix + name)
        return self.made[name]


def modulation(nc, d, keep):
    with ExitStack() as ctx:
        sb = lambda n, s, t=F32: ctx.enter_context(nc.sbuf_tensor("mod_" + n, s, t))
        S = Sems(nc, ctx, "mod_")
        cT = sb("cT", [P, KT, MODROWS])
        wa = sb("wa", [P, 3, KT, ADA_CHUNK])
        bias = sb("bias", [MODROWS, 6 * D])
        mod = sb("mod", [MODROWS, 6 * D])
        gain = sb("gain", [MODROWS, 2, D])
        pm = ctx.enter_context(nc.psum_tensor("mod_pm", [MODROWS, 2, 512], F32))
        pt = ctx.enter_context(nc.psum_tensor("mod_pt", [P, 2, 2, 512], F32))
        chunk_in = [S(f"chunk_in{b}") for b in range(3)]
        small_in, product, added, turned, scaled, gated, stored = (
            S(n) for n in ("small_in", "product", "added", "turned", "scaled", "gated", "stored"))
        sections = [(1, keep["A1"], 0), (0, keep["B1"], None), (4, keep["A2"], 1), (3, keep["B2"], None)]

        block = ctx.enter_context(nc.Block())

        @block.sync
        def _(sp):
            sp.dma_start(cT[:], d["cT"]).then_inc(small_in, 16)
            for c in range(ADA_CHUNKS):
                if c >= 3:
                    sp.wait_ge(product, c - 2)
                sp.dma_start(wa[:, c % 3], d["w_ada"][c]).then_inc(chunk_in[c % 3], 16)
            sp.wait_ge(gated, 2)
            sp.dma_start(d["gates"], gain[:, :, :]).then_inc(stored, 16)
            sp.wait_ge(stored, 16)

        @block.scalar
        def _(act):
            act.dma_start(bias[:], d["b_ada"].broadcast_to([MODROWS, 6 * D])).then_inc(small_in, 16)
            act.dma_start(gain[:, 0, :], d["norm_post_mix"].broadcast_to([MODROWS, D])).then_inc(small_in, 16)
            act.dma_start(gain[:, 1, :], d["norm_post_ffn"].broadcast_to([MODROWS, D])).then_inc(small_in, 16)
            act.dma_start(keep["cols"][:], d["cols"]).then_inc(small_in, 16)
            act.dma_start(keep["ident"][:], d["ident"]).then_inc(small_in, 16)
            act.dma_start(keep["headsum"][:], d["headsum"]).then_inc(small_in, 16)

        @block.tensor
        def _(pe):
            pe.wait_ge(small_in, 112)
            for c in range(ADA_CHUNKS):
                pe.wait_ge(chunk_in[c % 3], 16 * (c // 3 + 1))
                if c >= 2:
                    pe.wait_ge(added, c - 1)
                for k in range(KT):
                    mm = pe.matmul(pm[:, c % 2, :], cT[:, k, :], wa[:, c % 3, k, :], start=(k == 0), stop=(k == KT - 1))
                mm.then_inc(product, 1)
            pe.wait_ge(added, ADA_CHUNKS)
            for n, (section, _, _) in enumerate(sections):
                if n >= 2:
                    pe.wait_ge(scaled, n - 1)
                for k in range(KT):
                    at = section * D + k * P
                    mm = pe.transpose(pt[:, n % 2, k // 4, (k % 4) * MODROWS:(k % 4 + 1) * MODROWS],
                                      mod[:, at:at + P], keep["ident"][0:MODROWS, 0:MODROWS])
                mm.then_inc(turned, 1)

        @block.vector
        def _(dve):
            dve.wait_ge(small_in, 112)
            for c in range(ADA_CHUNKS):
                cols = slice(c * ADA_CHUNK, (c + 1) * ADA_CHUNK)
                dve.wait_ge(product, c + 1)
                dve.tensor_tensor(mod[:, cols], pm[:, c % 2, :], bias[:, cols], ALU.add).then_inc(added, 1)
            dve.wait_ge(added, ADA_CHUNKS)
            for n, section in enumerate((2, 5)):
                dve.tensor_tensor(gain[:, n, :], mod[:, section * D:(section + 1) * D], gain[:, n, :],
                                  ALU.mult).then_inc(gated, 1)
            for n, (_, dst, norm) in enumerate(sections):
                dve.wait_ge(turned, n + 1)
                for half in range(2):
                    src = pt[:, n % 2, half, 0:4 * MODROWS].rearrange("p (k r) -> p k r", k=4)
                    out = dst[:, 4 * half:4 * half + 4, :]
                    if norm is None:
                        ins = dve.tensor_copy(out, src)
                    else:
                        col = keep["cols"][:, 8 * norm + 4 * half:8 * norm + 4 * half + 4]
                        ins = dve.scalar_tensor_tensor(out, src, 1.0, col.unsqueeze(2).broadcast_to([P, 4, MODROWS]),
                                                       ALU.add, ALU.mult)
                ins.then_inc(scaled, 1)


def norm_in(nc, d, keep, hi, lo):
    with ExitStack() as ctx:
        sb = lambda n, s, t=F32: ctx.enter_context(nc.sbuf_tensor("nin_" + n, s, t))
        S = Sems(nc, ctx, "nin_")
        x = sb("x", [P, 2, D])
        junk = sb("junk", [P, D])
        stat = sb("stat", [P, 2, 4])
        h = sb("h", [P, 2, KT, P])
        pt = ctx.enter_context(nc.psum_tensor("nin_pt", [P, 2, KT, P], F32))
        x_in = [S("x_in0"), S("x_in1")]
        summed, logged, rstd, scaled, turned, modded, shifted, hi_ready, lo_ready = (
            S(n) for n in ("summed", "logged", "rstd", "scaled", "turned", "modded", "shifted", "hi", "lo"))

        def tiles(eng, body):
            body(0, 0, 0, P)
            body(1, 1, 0, P)
            with eng.Fori(0, TILES // 2 - 1) as pair:
                body(pair * 2 + 2, 0, pair + 1, P)
                body(pair * 2 + 3, 1, pair + 1, P)
            body(TILES, 0, TILES // 2, SAMP)

        def late(t):
            return not isinstance(t, int) or t >= 2

        block = ctx.enter_context(nc.Block())

        @block.sync
        def _(sp):
            def body(t, u, use, n):
                if late(t):
                    sp.wait_ge(turned, t - 1)
                src = d["x"][bass.ts(t, P), :] if n == P else d["x"][SEQ:TOK, :]
                sp.dma_start(x[0:n, u, :], src).then_inc(x_in[u], 16)
            tiles(sp, body)

        @block.scalar
        def _(act):
            act.preload_act_table_set(LN_EXP)

            def body(t, u, use, n):
                act.wait_ge(x_in[u], (use + 1) * 16)
                act.activation(junk[0:n, :], x[0:n, u, :], ACT.Square, accum_out=stat[0:n, u, 0:1]).then_inc(summed, 1)
                act.wait_ge(summed, t + 1)
                act.activation(stat[0:n, u, 1:2], stat[0:n, u, 0:1], ACT.Ln, scale=1.0 / D,
                               bias=keep["eps"][0:n, :]).then_inc(logged, 1)
                act.wait_ge(logged, t + 1)
                act.activation(stat[0:n, u, 2:3], stat[0:n, u, 1:2], ACT.Exp, scale=-0.5).then_inc(rstd, 1)
                act.wait_ge(shifted, t + 1)
                met(act, shifted)
                dst = hi[:, :, bass.ts(t, P)] if n == P else hi[:, :, SEQ:TOK]
                act.activation(dst, h[:, u, :, 0:n], ACT.Copy).then_inc(hi_ready, 1)
            tiles(act, body)

        @block.vector
        def _(dve):
            def body(t, u, use, n):
                dve.wait_ge(rstd, t + 1)
                dve.tensor_scalar(x[0:n, u, :], x[0:n, u, :], stat[0:n, u, 2:3], None, ALU.mult).then_inc(scaled, 1)
                if n == P:
                    a, b = (keep[m][:, :, SAMP:SAMP + 1].broadcast_to([P, KT, P]) for m in ("A1", "B1"))
                else:
                    a, b = (keep[m][:, :, 0:SAMP] for m in ("A1", "B1"))
                dve.wait_ge(turned, t + 1)
                if late(t):
                    dve.wait_ge(hi_ready, t - 1)
                    dve.wait_ge(lo_ready, t - 1)
                dve.tensor_tensor(h[:, u, :, 0:n], pt[:, u, :, 0:n], a, ALU.mult).then_inc(modded, 1)
                dve.wait_ge(modded, t + 1)
                dve.tensor_tensor(h[:, u, :, 0:n], h[:, u, :, 0:n], b, ALU.add).then_inc(shifted, 1)
            tiles(dve, body)

        @block.gpsimd
        def _(pool):
            def body(t, u, use, n):
                pool.wait_ge(hi_ready, t + 1)
                at = bass.ts(t, P) if n == P else slice(SEQ, TOK)
                pool.tensor_tensor(lo[:, :, at], h[:, u, :, 0:n], hi[:, :, at].bitcast(F32),
                                   ALU.subtract).then_inc(lo_ready, 1)
            tiles(pool, body)

        @block.tensor
        def _(pe):
            def body(t, u, use, n):
                pe.wait_ge(scaled, t + 1)
                if late(t):
                    pe.wait_ge(modded, t - 1)
                for k in range(KT):
                    mm = pe.transpose(pt[:, u, k, 0:n], x[0:n, u, k * P:(k + 1) * P], keep["ident"][0:n, 0:n])
                mm.then_inc(turned, 1)
            tiles(pe, body)


def project_in(nc, d, keep, hi, lo):
    with ExitStack() as ctx:
        sb = lambda n, s, t=F32: ctx.enter_context(nc.sbuf_tensor("pin_" + n, s, t))
        S = Sems(nc, ctx, "pin_")
        w = sb("w", [P, 2, KT, P])
        whi = sb("whi", [P, 2, KT, P], F32R)
        wlo = sb("wlo", [P, 2, KT, P], F32R)
        z = sb("z", [P, 2, CONV - 1 + TOK])
        hist = sb("hist", [P, NB, CONV - 1 + NT])
        ra = sb("ra", [P, TOK])
        rb = sb("rb", [P, TOK])
        share = sb("share", [P, P])
        pz = ctx.enter_context(nc.psum_tensor("pin_pz", [P, len(GROUPS), 512], F32))
        pn = ctx.enter_context(nc.psum_tensor("pin_pn", [P, 3, 512], F32))
        lb = sb("lb", [P, 4, 2])
        zcol = sb("zcol", [P, 2, 2])
        w_in = [S("w_in0"), S("w_in1")]
        stored = [S("stored0"), S("stored1")]
        (whi_ready, wlo_ready, product, row, kept_stored, ready, bound, hist_in, conv, silu, square, norm,
         log, rnormed, sig_ready, kept, tmp, soft, tap, affine, lf_ready, cst, lb_exp, lb_left, lb_step) = (
            S(n) for n in ("whi", "wlo", "product", "row", "kept_stored", "ready", "bound", "hist_in",
                           "conv", "silu", "square", "norm", "log", "rnormed", "sig", "kept", "tmp", "soft", "tap",
                           "affine", "lf", "cst", "lb_exp", "lb_left", "lb_step"))
        CSTS = 5
        Z0 = CONV - 1
        zr = lambda u: z[:, u, Z0:Z0 + TOK]

        def blocks(eng, lo_c, hi_c, body):
            c = lo_c
            while c < hi_c and (c % 2 or c < 2):
                body(c, c % 2, c // 2)
                c += 1
            n = (hi_c - c) // 2
            if n > 1:
                with eng.Fori(0, n) as pair:
                    body(pair * 2 + c, 0, pair + c // 2)
                    body(pair * 2 + (c + 1), 1, pair + c // 2)
            elif n:
                body(c, 0, c // 2)
                body(c + 1, 1, c // 2)
            if (hi_c - c) % 2:
                body(hi_c - 1, 0, hi_c // 2)

        def late(c):
            return not isinstance(c, int) or c >= 2

        block = ctx.enter_context(nc.Block())

        def store(eng, row, src, done):
            eng.dma_start(d["z"][:, :, row, :].rearrange("t p c -> p t c"),
                          src[:, 0:SEQ].rearrange("p (t c) -> p t c", c=P)).then_inc(done, 16)
            eng.dma_start(d["z_s"][:, row, :], src[:, SEQ:TOK]).then_inc(done, 16)

        @block.sync
        def _(sp):
            def load(c, u):
                if late(c):
                    sp.wait_ge(wlo_ready, c - 1)
                sp.dma_start(w[:, u], d["w_in"][c]).then_inc(w_in[u], 16)

            load(0, 0)
            load(1, 1)
            load(2, 0)
            sp.wait_ge(row, 5)
            sp.dma_start(d["gz"][:, 0:SEQ], zr(0)[0:4 * MH, 0:SEQ]).then_inc(stored[0], 16)
            sp.dma_start(d["gz"][:, SEQ:TOK], zr(0)[0:4 * MH, SEQ:TOK]).then_inc(stored[0], 16)

            def raw(c, u, r):
                load(c + 2, u)
                sp.wait_ge(row, (c + 1) * 5)
                store(sp, c - 1, zr(u), stored[u])
            blocks(sp, *C_RAW, raw)

            def ready_row(c, u, r):
                load(c + 2, u)
                sp.wait_ge(ready, c + 2 - C_OUTGATE[0])
                store(sp, c - 1, zr(u), stored[u])
            blocks(sp, *C_OUTGATE, ready_row)

            def conv_row(c, u, r):
                if not isinstance(c, int) or c + 2 < NCOL:
                    load(c + 2, u)
                j = c - C_CONVN[0]
                if not isinstance(c, int) or j >= 1:
                    sp.wait_ge(conv, j + 1)
                sp.dma_start(hist[:, :, 0:CONV - 1], d["hist"][j]).then_inc(hist_in, 16)
                sp.wait_ge(row, (c + 1) * 5)
                sp.dma_start(d["p_conv"][j], z[:, u, SEQ:SEQ + CONV - 1]).then_inc(bound, 16)
                sp.dma_start(d["s_conv"][j], z[:, u, Z0 + SEQ:Z0 + TOK].rearrange("p (b t) -> p b t", t=NT)
                             [:, :, NT - CONV + 1:NT]).then_inc(bound, 16)
                sp.wait_ge(ready, c + 2 - C_OUTGATE[0])
                store(sp, c - 1, zr(u), stored[u])
            blocks(sp, C_CONVN[0], C_CONVV[1], conv_row)
            for j, c in enumerate(range(*C_FORGET)):
                sp.wait_ge(kept, j + 1)
                store(sp, R_HG0 + 2 * j + 1, ra, kept_stored)
                sp.wait_ge(ready, c + 2 - C_OUTGATE[0])
                store(sp, R_HG0 + 2 * j, zr(c % 2), stored[c % 2])
            sp.wait_ge(stored[0], 32 * ((NCOL + 1) // 2))
            sp.wait_ge(stored[1], 32 * (NCOL // 2))
            sp.wait_ge(kept_stored, 64)
            sp.wait_ge(bound, 32 * (C_CONVV[1] - C_CONVN[0]))

        @block.tensor
        def _(pe):
            def body(c, u, r):
                pe.wait_ge(whi_ready, c + 1)
                pe.wait_ge(wlo_ready, c + 1)
                for g, (at, n) in enumerate(GROUPS):
                    if not isinstance(c, int) or c >= 1:
                        pe.wait_ge(row, (c - 1) * 5 + g + 1)
                    for k in range(KT):
                        pe.matmul(pz[:, g, 0:n], whi[:, u, k], hi[:, k, at:at + n], start=(k == 0), stop=False)
                        pe.matmul(pz[:, g, 0:n], whi[:, u, k], lo[:, k, at:at + n], start=False, stop=False)
                        mm = pe.matmul(pz[:, g, 0:n], wlo[:, u, k], hi[:, k, at:at + n], start=False,
                                       stop=(k == KT - 1))
                    mm.then_inc(product, 1)

            def with_norms(c, u, r):
                body(c, u, r)
                j = c - 1 - C_CONVN[0]
                pe.wait_ge(square, j + 1)
                for g, (at, n) in enumerate(GROUPS):
                    if g >= 3:
                        pe.wait_ge(log, j * 5 + g - 2)
                    elif not isinstance(c, int) or j >= 1:
                        pe.wait_ge(log, j * 5)
                    pe.matmul(pn[:, g % 3, 0:n], keep["headsum"][:], rb[:, at:at + n], start=True,
                              stop=True).then_inc(norm, 1)

            blocks(pe, 0, C_CONVN[0] + 1, body)
            blocks(pe, C_CONVN[0] + 1, C_CONVN[1] + 1, with_norms)
            blocks(pe, C_CONVN[1] + 1, NCOL, body)

        @block.scalar
        def _(act):
            def split(c, u, r):
                act.wait_ge(w_in[u], (r + 1) * 16)
                if late(c):
                    act.wait_ge(product, (c - 1) * 5)
                act.activation(whi[:, u], w[:, u], ACT.Copy).then_inc(whi_ready, 1)

            def head(c, u, r):
                if not isinstance(c, int) or c + 1 < NCOL:
                    split(c + 1, 1 - u, r + u)
                if late(c):
                    act.wait_ge(stored[u], r * 32)
                for g, (at, n) in enumerate(GROUPS):
                    act.wait_ge(product, c * 5 + g + 1)
                    act.activation(z[:, u, Z0 + at:Z0 + at + n], pz[:, g, 0:n], ACT.Identity,
                                   scale=zcol[:, u, 0:1], bias=zcol[:, u, 1:2]).then_inc(row, 1)

            act.wait_ge(cst, CSTS)
            act.activation(lb[:, 1, :], lb[:, 0, :], ACT.Exp).then_inc(lb_exp, 1)
            act.wait_ge(lb_left, 1)
            act.activation(lb[:, 3, :], lb[:, 2, :], ACT.Ln).then_inc(lb_exp, 1)
            split(0, 0, 0)
            blocks(act, 0, C_RAW[1], head)

            def outgate(c, u, r):
                head(c, u, r)
                n = c - C_OUTGATE[0]
                if not isinstance(c, int) or n >= 1:
                    act.wait_ge(ready, n + 1)
                act.wait_ge(row, c * 5 + 5)
                act.activation(ra[:, :], zr(u), ACT.Sigmoid).then_inc(sig_ready, 1)
            blocks(act, *C_OUTGATE, outgate)

            def rnorm(c):
                j = c - C_CONVN[0]
                act.preload_act_table_set(LN_EXP)
                for g, (at, n) in enumerate(GROUPS):
                    act.wait_ge(norm, j * 5 + g + 1)
                    act.activation(rb[:, at:at + n], pn[:, g % 3, 0:n], ACT.Ln, bias=keep["eps"][:, :]).then_inc(log, 1)
                act.wait_ge(log, j * 5 + 5)
                act.activation(rb[:, :], rb[:, :], ACT.Exp, scale=-0.5).then_inc(rnormed, 1)

            def conv_block(c, u, r, before, squared):
                head(c, u, r)
                if before:
                    rnorm(c - 1)
                act.wait_ge(conv, c + 2 - C_CONVN[0])
                act.activation(rb[:, :], ra[:, :], ACT.Sigmoid).then_inc(sig_ready, 1)
                if squared:
                    act.wait_ge(silu, c + 1 - C_CONVN[0])
                    act.activation(rb[:, :], ra[:, :], ACT.Square).then_inc(square, 1)

            conv_block(C_CONVN[0], C_CONVN[0] % 2, C_CONVN[0] // 2, False, True)
            blocks(act, C_CONVN[0] + 1, C_CONVN[1], lambda c, u, r: conv_block(c, u, r, True, True))
            conv_block(C_CONVV[0], C_CONVV[0] % 2, C_CONVV[0] // 2, True, False)
            blocks(act, C_CONVV[0] + 1, C_CONVV[1], lambda c, u, r: conv_block(c, u, r, False, False))
            for j, c in enumerate(range(*C_FORGET)):
                u = c % 2
                head(c, u, c // 2)
                act.wait_ge(row, c * 5 + 5)
                act.wait_ge(ready, c + 1 - C_OUTGATE[0])
                if j:
                    act.wait_ge(kept_stored, 32 * j)
                act.activation(ra[:, :], zr(u), ACT.Sigmoid, scale=-1.0).then_inc(sig_ready, 1)
                act.preload_act_table_set(LN_EXP)
                act.wait_ge(tmp, 2 * j + 1)
                act.activation(rb[:, :], rb[:, :], ACT.Exp).then_inc(soft, 1)
                act.wait_ge(soft, 2 * j + 1)
                act.activation(rb[:, :], rb[:, :], ACT.Ln, bias=1.0).then_inc(soft, 1)

        @block.vector
        def _(dve):
            def split(c, u, r):
                dve.wait_ge(w_in[u], (r + 1) * 16)
                dve.wait_ge(whi_ready, c + 1)
                dve.tensor_copy(zcol[:, u, :], keep["zcols"][:, :, bass.ds(c, 1)].rearrange("p a o -> p (a o)"))
                dve.tensor_tensor(wlo[:, u], w[:, u], whi[:, u].bitcast(F32), ALU.subtract).then_inc(wlo_ready, 1)

            def head(c, u, r):
                if not isinstance(c, int) or c + 1 < NCOL:
                    split(c + 1, 1 - u, r + u)

            dve.memset(z[:, 0, 0:Z0], 0.0).then_inc(ready, 1)
            dve.memset(z[:, 1, 0:Z0], 0.0).then_inc(conv, 1)
            dve.memset(share[:], 0.0).then_inc(cst, 1)
            dve.tensor_tensor(keep["zcols"][:, 1, :], keep["zcols"][:, 1, :], keep["zcols"][:, 0, :],
                              ALU.mult).then_inc(cst, 1)
            for n in range(2):
                dve.tensor_tensor(keep["ogate"][:, n, :], keep["ogate"][:, n, :], keep["ogate"][:, 2, :],
                                  ALU.mult).then_inc(cst, 1)
            lbl = keep["lbl"]
            dve.tensor_tensor(lb[:, 0, :], lbl[:, :], lbl[:, :], ALU.subtract).then_inc(cst, 1)
            dve.wait_ge(lb_exp, 1)
            dve.reciprocal(lb[:, 2, :], lb[:, 1, :]).then_inc(lb_step, 1)
            dve.wait_ge(lb_step, 1)
            dve.tensor_tensor(lb[:, 2, :], lb[:, 2, :], lb[:, 1, :], ALU.mult).then_inc(lb_step, 1)
            dve.wait_ge(lb_step, 2)
            dve.tensor_tensor(lb[:, 2, :], lb[:, 2, :], lb[:, 2, :], ALU.subtract).then_inc(lb_step, 1)
            dve.wait_ge(lb_step, 3)
            dve.tensor_scalar(lb[:, 2, :], lb[:, 2, :], -1.0, 1.0, ALU.mult, ALU.add).then_inc(lb_left, 1)
            split(0, 0, 0)
            blocks(dve, 0, C_RAW[1], head)

            def outgate(c, u, r):
                head(c, u, r)
                n = c - C_OUTGATE[0]
                dve.wait_ge(sig_ready, n + 1)
                dve.tensor_scalar(zr(u), zr(u), keep["ogate"][:, 0, bass.ds(n, 1)], keep["ogate"][:, 1, bass.ds(n, 1)],
                                  ALU.mult, ALU.add).then_inc(affine, 1)
                dve.wait_ge(affine, n + 1)
                dve.tensor_tensor(zr(u), zr(u), ra[:, :], ALU.mult).then_inc(ready, 1)
            blocks(dve, *C_OUTGATE, outgate)

            def scale_norm(c, u):
                j = c - C_CONVN[0]
                dve.wait_ge(rnormed, j + 1)
                dve.wait_ge(bound, (j + 1) * 32)
                dve.scalar_tensor_tensor(zr(u), ra[:, :], keep["qscale"][:, bass.ds(j, 1)], rb[:, :],
                                         ALU.mult, ALU.mult).then_inc(ready, 1)

            def conv_block(c, u, r, before, normed):
                head(c, u, r)
                n, j = c - C_OUTGATE[0], c - C_CONVN[0]
                if before:
                    scale_norm(c - 1, 1 - u)
                    dve.wait_ge(ready, n + 1)
                elif not isinstance(c, int) or n >= 1:
                    dve.wait_ge(ready, n + 1)
                dve.wait_ge(row, c * 5 + 5)
                dve.wait_ge(hist_in, (j + 1) * 16)
                zs = z[:, u, Z0 + SEQ:Z0 + TOK].rearrange("p (b t) -> p b t", t=NT)
                rs = ra[:, SEQ:TOK].rearrange("p (b t) -> p b t", t=NT)
                dve.tensor_copy(hist[:, :, Z0:Z0 + NT], zs).then_inc(tap, 1)
                for t in range(CONV):
                    wt = keep["convw"][:, t, bass.ds(j, 1)]
                    zp, zh = z[:, u, t:t + SEQ], hist[:, :, t:t + NT]
                    dve.wait_ge(tap, j * 7 + (1 if t == 0 else 2 * t + 1))
                    if t == 0:
                        dve.tensor_scalar(ra[:, 0:SEQ], zp, wt, None, ALU.mult).then_inc(tap, 1)
                        dve.tensor_scalar(rs, zh, wt, None, ALU.mult).then_inc(tap, 1)
                    else:
                        last = t == CONV - 1
                        a = dve.scalar_tensor_tensor(ra[:, 0:SEQ], zp, wt, ra[:, 0:SEQ], ALU.mult, ALU.add)
                        b = dve.scalar_tensor_tensor(rs, zh, wt, rs, ALU.mult, ALU.add)
                        if last:
                            b.then_inc(conv, 1)
                        else:
                            a.then_inc(tap, 1)
                            b.then_inc(tap, 1)
                dve.wait_ge(sig_ready, n + 1)
                if normed:
                    dve.tensor_tensor(ra[:, :], ra[:, :], rb[:, :], ALU.mult).then_inc(silu, 1)
                else:
                    dve.wait_ge(bound, (j + 1) * 32)
                    dve.tensor_tensor(zr(u), ra[:, :], rb[:, :], ALU.mult).then_inc(ready, 1)

            conv_block(C_CONVN[0], C_CONVN[0] % 2, C_CONVN[0] // 2, False, True)
            blocks(dve, C_CONVN[0] + 1, C_CONVN[1], lambda c, u, r: conv_block(c, u, r, True, True))
            conv_block(C_CONVV[0], C_CONVV[0] % 2, C_CONVV[0] // 2, True, False)
            blocks(dve, C_CONVV[0] + 1, C_CONVV[1], lambda c, u, r: conv_block(c, u, r, False, False))
            for j, c in enumerate(range(*C_FORGET)):
                u = c % 2
                head(c, u, c // 2)
                dve.wait_ge(row, c * 5 + 5)
                dve.wait_ge(ready, c + 1 - C_OUTGATE[0])
                dve.scalar_tensor_tensor(rb[:, :], zr(u), -1.0, zr(u), ALU.mult, ALU.min).then_inc(tmp, 1)
                dve.wait_ge(sig_ready, c + 1 - C_OUTGATE[0])
                dve.tensor_scalar(ra[:, :], ra[:, :], lb[:, 2, j:j + 1], None, ALU.mult).then_inc(kept, 1)
                dve.wait_ge(lb_exp, 2)
                dve.tensor_copy(share[:, :], lb[:, 3, j:j + 1].broadcast_to([P, P])).then_inc(lf_ready, 1)
                dve.wait_ge(lf_ready, j + 1)
                dve.wait_ge(soft, 2 * j + 2)
                dve.scalar_tensor_tensor(rb[:, :], zr(u), 0.0, rb[:, :], ALU.min, ALU.subtract).then_inc(tmp, 1)
                dve.wait_ge(tmp, 2 * j + 2)
                with dve.Fori(0, TILES) as i:
                    dve.tensor_tensor_scan(zr(u)[:, bass.ts(i, P)], share[:, :], rb[:, bass.ts(i, P)], 0.0,
                                           ALU.add, ALU.add)
                for b in range(NB):
                    at = slice(SEQ + b * NT, SEQ + (b + 1) * NT)
                    ins = dve.tensor_tensor_scan(zr(u)[:, at], share[:, 0:NT], rb[:, at], 0.0, ALU.add, ALU.add)
                ins.then_inc(ready, 1)
Q_A, Q_NG, Q_BETA, Q_NBEG, Q_WI, Q_WS, Q_EGL, Q_EG = range(8)
NQ = 8
PJ = (2, 3)


def gates(nc, d, keep):
    with ExitStack() as ctx:
        sb = lambda n, s, t=F32: ctx.enter_context(nc.sbuf_tensor("gat_" + n, s, t))
        S = Sems(nc, ctx, "gat_")
        R = TILES * MH
        ends = sb("ends", [MH, 2, TILES])
        mend = sb("mend", [MH, TILES + 1])
        zero = sb("zero", [P, P])
        parts = {}
        for who, rows, n, length in (("p", R, P, P), ("s", MH, SAMP, NT)):
            v = {"rows": rows, "n": n, "seqs": n // length, "len": length}
            for name, k in (("raw", 4), ("x", 2), ("e", 2), ("q", NQ), ("row", 3), ("b", 1), ("g", 1), ("M", 1),
                            ("m0", 1), ("col", 3), ("fin", 3), ("tmp", 1)):
                width = {"m0": n // length, "col": 1, "fin": n // length}.get(name, n)
                v[name] = sb(f"{name}_{who}", [rows, k, width])
            parts[who] = v
        turned = ctx.enter_context(nc.psum_tensor("gat_turned", [P, NQ, P], F32))
        vp, vs = parts["p"], parts["s"]

        block = ctx.enter_context(nc.Block())

        @block.sync
        def _(sp):
            for k in range(4):
                sp.dma_start(vp["raw"][:, k, :], d["gz"][k * MH:(k + 1) * MH, 0:SEQ].rearrange("h (t c) -> t h c", c=P)
                             ).then_inc(S("in"), 16)
                sp.dma_start(vs["raw"][:, k, :], d["gz"][k * MH:(k + 1) * MH, SEQ:TOK]).then_inc(S("in"), 16)
            sp.dma_start(vp["col"][:, :, 0], d["gcol_p"]).then_inc(S("in"), 16)
            sp.dma_start(vs["col"][:, :, 0], d["gcol_s"]).then_inc(S("in"), 16)
            sp.dma_start(vs["m0"][:, 0, :], d["m0"]).then_inc(S("in"), 16)
            sp.wait_ge(S("ends"), 2)
            for k, src in ((0, vp["M"]), (1, vp["b"])):
                sp.dma_start(d["ends"][k].rearrange("(r o) -> r o", o=1), src[:, 0, P - 1:P]).then_inc(S("ends_out"), 16)
            sp.wait_ge(S("ends_out"), 32)
            sp.dma_start(ends[:], d["ends"].rearrange("k (t h) -> h k t", h=MH), allow_slow_non_contiguous=True).then_inc(S("ends_in"), 16)
            sp.wait_ge(S("mend"), 2)
            sp.dma_start(d["mprev"].rearrange("(t h) -> h t", h=MH), mend[:, 0:TILES],
                         allow_slow_non_contiguous=True).then_inc(S("mprev_out"), 16)
            sp.dma_start(d["p_m"], mend[:, TILES:TILES + 1]).then_inc(S("final"), 16)
            sp.wait_ge(S("mprev_out"), 16)
            sp.dma_start(vp["m0"][:, 0, :], d["mprev"].rearrange("(r o) -> r o", o=1)).then_inc(S("mprev_in"), 16)
            sp.wait_ge(S("fin"), 3)
            sp.dma_start(d["rows_p"].rearrange("t h k c -> (t h) k c"), vp["row"][:]).then_inc(S("final"), 16)
            sp.dma_start(d["dec_p"].rearrange("w (t h) -> (t h) w", h=MH), vp["fin"][:, 0:2, 0],
                         allow_slow_non_contiguous=True).then_inc(S("final"), 16)
            sp.wait_ge(S("fin"), 6)
            sp.dma_start(d["rows_s"], vs["row"][:]).then_inc(S("final"), 16)
            sp.dma_start(d["dec_s"].rearrange("w h b -> h w b"), vs["fin"][:, 0:2, :]).then_inc(S("final"), 16)
            sp.dma_start(d["s_m"], vs["fin"][:, 2, :]).then_inc(S("final"), 16)
            sp.wait_ge(S("final"), 96)

        @block.scalar
        def _(act):
            act.preload_act_table_set(LN_EXP)
            for n, v in enumerate((vp, vs)):
                if n == 0:
                    act.wait_ge(S("in"), 176)
                act.activation(v["col"][:, 1, :], v["col"][:, 1, :], ACT.Exp).then_inc(S("expA"), 1)
                act.activation(v["q"][:, Q_BETA, :], v["raw"][:, 2, :], ACT.Exp, scale=-1.0).then_inc(S("expb"), 1)
                act.wait_ge(S("nabs"), n + 1)
                act.activation(v["e"][:], v["e"][:], ACT.Exp).then_inc(S("soft"), 1)
                act.wait_ge(S("soft"), 2 * n + 1)
                act.activation(v["e"][:], v["e"][:], ACT.Ln, bias=1.0).then_inc(S("soft"), 1)
            for n, v in enumerate((vp, vs)):
                act.wait_ge(S("expo"), n + 1)
                act.activation(v["q"][:, Q_WI:Q_EG + 1, :], v["q"][:, Q_WI:Q_EG + 1, :], ACT.Exp).then_inc(S("weights"), 1)

        @block.vector
        def _(dve):
            step = [0]

            def then(ins):
                step[0] += 1
                ins.then_inc(S("step"), 1)
                dve.wait_ge(S("step"), step[0])

            def seq(v, name, k=0):
                return v[name][:, k, :].rearrange("h (b t) -> h b t", t=v["len"])

            def last(v, name, k=0):
                return seq(v, name, k)[:, :, v["len"] - 1:v["len"]].broadcast_to([v["rows"], v["seqs"], v["len"]])

            def running(v, out, src, op, initial, second):
                for b in range(v["seqs"]):
                    at = slice(b * v["len"], (b + 1) * v["len"])
                    ins = dve.tensor_tensor_scan(out[:, 0, at], second[0:v["rows"], 0:v["len"]] if second is not None
                                                 else src[:, at], src[:, at],
                                                 initial(b) if callable(initial) else initial, op, op)
                return ins

            dve.memset(mend[:, 0:1], 0.0).then_inc(S("mend"), 1)
            then(dve.memset(zero[:], 0.0))
            dve.wait_ge(S("in"), 176)
            for n, v in enumerate((vp, vs)):
                dve.tensor_scalar(v["x"][:, 0, :], v["raw"][:, 1, :], v["col"][:, 0, :], None, ALU.add)
                then(dve.tensor_scalar(v["x"][:, 1, :], v["raw"][:, 3, :], v["col"][:, 2, :], None, ALU.add))
                dve.scalar_tensor_tensor(v["e"][:], v["x"][:], -1.0, v["x"][:], ALU.mult, ALU.min).then_inc(S("nabs"), 1)
                dve.wait_ge(S("soft"), 2 * n + 2)
                dve.scalar_tensor_tensor(v["x"][:, 0, :], v["x"][:, 0, :], 0.0, v["e"][:, 0, :], ALU.min, ALU.subtract)
                then(dve.scalar_tensor_tensor(v["x"][:, 1, :], v["x"][:, 1, :], 0.0, v["e"][:, 1, :], ALU.max, ALU.add))
                dve.wait_ge(S("expA"), n + 1)
                then(dve.tensor_scalar(v["x"][:, 1, :], v["x"][:, 1, :], v["col"][:, 1, :], -1.0, ALU.mult, ALU.mult))
                running(v, v["b"], v["x"][:, 0, :], ALU.add, 0.0, zero)
                then(running(v, v["g"], v["x"][:, 1, :], ALU.add, 0.0, zero))
                then(dve.tensor_tensor(v["q"][:, Q_A, :], v["raw"][:, 0, :], v["b"][:, 0, :], ALU.subtract))
                m0 = v["m0"]
                start = -3.0e38 if n == 0 else (lambda b, m0=m0: m0[:, 0, b:b + 1])
                ins = running(v, v["M"], v["q"][:, Q_A, :], ALU.max, start, None)
                if n == 0:
                    ins.then_inc(S("ends"), 2)
                else:
                    then(ins)
                dve.wait_ge(S("expb"), n + 1)
                then(dve.tensor_scalar(v["q"][:, Q_BETA, :], v["q"][:, Q_BETA, :], 1.0, None, ALU.add))
                then(dve.reciprocal(v["q"][:, Q_BETA, :], v["q"][:, Q_BETA, :]))
                dve.tensor_copy(v["row"][:, 2, :], v["q"][:, Q_BETA, :])
                dve.tensor_copy(v["row"][:, 1, :], v["g"][:, 0, :])
                dve.tensor_scalar(v["q"][:, Q_NG, :], v["g"][:, 0, :], -1.0, None, ALU.mult)
                dve.tensor_copy(v["q"][:, Q_EG, :], v["g"][:, 0, :])
            dve.wait_ge(S("ends_in"), 16)
            dve.tensor_tensor_scan(mend[:, 1:TILES + 1], ends[:, 0, :], ends[:, 1, :], 0.0, ALU.max,
                                   ALU.add).then_inc(S("mend"), 1)
            dve.wait_ge(S("mprev_in"), 16)
            then(dve.tensor_scalar(vp["M"][:, 0, :], vp["M"][:, 0, :], vp["m0"][:, 0, :], None, ALU.max))
            for n, v in enumerate((vp, vs)):
                dve.tensor_scalar(v["row"][:, 0, :], v["M"][:, 0, :], -1.0, None, ALU.mult)
                m0 = v["m0"][:, 0, :].unsqueeze(2).broadcast_to([v["rows"], v["seqs"], v["len"]])
                dve.tensor_tensor(seq(v, "q", Q_WI), m0, seq(v, "M"), ALU.subtract)
                dve.tensor_tensor(seq(v, "q", Q_WS), seq(v, "q", Q_A), last(v, "M"), ALU.subtract)
                dve.tensor_tensor(seq(v, "q", Q_EGL), last(v, "g"), seq(v, "g"), ALU.subtract).then_inc(S("expo"), 1)
            for n, v in enumerate((vp, vs)):
                dve.wait_ge(S("weights"), n + 1)
                ends_of = lambda name, k: seq(v, name, k)[:, :, v["len"] - 1]
                dve.tensor_copy(v["fin"][:, 0, :], ends_of("q", Q_WI)).then_inc(S("fin"), 1)
                dve.tensor_copy(v["fin"][:, 1, :], ends_of("q", Q_EG)).then_inc(S("fin"), 1)
                dve.scalar_tensor_tensor(v["q"][:, Q_NBEG, :], v["q"][:, Q_BETA, :], -1.0, v["q"][:, Q_EG, :],
                                         ALU.mult, ALU.mult).then_inc(S("nbeg"), 1)
                dve.tensor_tensor(v["fin"][:, 2, :], ends_of("b", 0), ends_of("M", 0), ALU.add).then_inc(S("fin"), 1)
            for n, (v, dst) in enumerate(((vp, keep["cols_p"]), (vs, keep["cols_s"]))):
                dve.wait_ge(S("turned"), n + 1)
                dve.tensor_copy(dst[:], turned[0:v["n"], :, 0:v["rows"]]).then_inc(S("read"), 1)

        @block.tensor
        def _(pe):
            for n, v in enumerate((vp, vs)):
                pe.wait_ge(S("nbeg"), n + 1)
                if n:
                    pe.wait_ge(S("read"), n)
                for k in range(NQ):
                    mm = pe.transpose(turned[0:v["n"], k, 0:v["rows"]], v["q"][:, k, :],
                                      keep["ident"][0:v["rows"], 0:v["rows"]])
                mm.then_inc(S("turned"), 1)



LEVELS = P.bit_length() - 1
Y_M, Y_G, Y_H = 0, MH, MH + GH


def mixers(nc, d, keep, sample):
    with ExitStack() as ctx:
        pre = "smp_" if sample else "mix_"
        sb = lambda n, s, t=F32: ctx.enter_context(nc.sbuf_tensor(pre + n, s, t))
        S = Sems(nc, ctx, pre)
        halvings = 3 if sample else LEVELS
        nbuf = 1 if sample else 2
        zt = [sb(f"zt{u}", [P, NROW, P]) for u in range(nbuf)]
        rb = [sb(f"rb{u}", [P, MH, 3, P]) for u in range(nbuf)]
        yt = [sb(f"yt{u}", [P, KT, P]) for u in range(nbuf)]
        level = sb("level", [P, LEVELS + 1, P])
        late = sb("late", [P, 2, P])
        cc = [sb(f"cc{u}", [P, NQ, MH]) for u in range(nbuf)]
        ex = sb("ex", [P, MH, 2, P])
        bd = sb("bd", [P, MH, P])
        pm, at_, lt, xf, wn = (sb(n, [P, MH, P]) for n in ("pm", "attn", "lt", "xf", "wn"))
        cl = sb("cl", [P, 3, MH, P], F32R)
        x, xt, m1 = (sb(n, [P, MH + 1, P], F32R) for n in ("x", "xt", "m1"))
        ident_r = sb("ident_r", [P, 2, P], F32R)
        zero = sb("zero", [P, 2])
        v1 = sb("v1", [P, MH, HD + 1])
        kw, gkw, bv, vn, rv = (sb(n, [P, MH, HD]) for n in ("kw", "gkw", "bv", "vn", "rv"))
        hv, kd = (sb(n, [P, HH, HD]) for n in ("hv", "kd"))
        num = sb("num", [P, MH, HD + 1])
        den = sb("den", [P, 2, MH])
        eg = sb("eg", [P, 2, 1])
        y = sb("y", [P, 16, HD])
        sq = sb("sq", [P, 16, HD])
        ss = sb("ss", [P, 3, 16])
        e = sb("e", [P, LEVELS + 2, 2, P])
        hk, hq = (sb(n, [P, LEVELS + 1, 2, P]) for n in ("hk", "hq"))
        ph = sb("ph", [P, HH, LEVELS + 1, P])
        ps = sb("ps", [P, HH, P])
        if sample:
            dc = sb("dc", [P, 2, 3, NB])
            cm, gs, hs = (sb(n, [P, k, NB, HD]) for n, k in (("cm", 3), ("gs", 3), ("hs", 2)))
            nm = sb("nm", [P, 3, NB])
            one_t = sb("one_t", [P, NB, P])
            one_s = sb("one_s", [P, NB])
            qx = sb("qx", [P, 3, NB, P])
            vx = sb("vx", [P, 2, 2, NB, HD])
        else:
            dc = [sb(f"dc{u}", [P, 2, 3]) for u in range(nbuf)]
            dec = sb("dec", [P, 2, TILES, MH])
            cm, gs, hs = (sb(n, [P, k, w]) for n, k, w in (("cm", 3, HD + 1), ("gs", 3, HD), ("hs", 2, HD)))
        bank = lambda n: ctx.enter_context(nc.psum_tensor(pre + n, [P, 2, 512], F32))
        pa, pb, pc, pd = bank("pa"), bank("pb"), bank("pc"), bank("pd")
        z_in = [S(f"z_in{u}") for u in range(nbuf)]
        y_out = [S(f"y_out{u}") for u in range(nbuf)]
        groups = [(j, g) for j in range(2) for g in range((halvings + 1) // 4)]
        terms = halvings + 1
        plan = [("turn", 0), ("turn_before", 0)] + [("round", i) for i in range(len(groups))]
        fill = [[plan[i]] if i < len(plan) else [] for i in range(halvings)]
        rest = plan[halvings:] + [("mlstm", 0), ("hgrn", 0)]
        R = len(groups)
        CONSTS = 2
        pv = lambda b, w, at=0, n=3: b[:, :, at:at + n * w].rearrange("p r (j c) -> p r j c", c=w)
        hm = lambda a: a.rearrange("p (r j) c -> p r j c", r=2)
        ym = lambda a: a.rearrange("p (j r) c -> p r j c", r=2)
        pair_of = lambda a, h: a[:, h:h + 2, :].rearrange("p a c -> p (a c)")
        half = lambda par: slice(par * HD, (par + 1) * HD)
        colh = lambda u, q, w: cc[u][:, q, :].rearrange("p (r j) -> p r j", r=2).unsqueeze(3).broadcast_to([P, 2, 3, w])
        tok = lambda b, at: b.rearrange("p a (j r c) -> p (a j) r c", r=2, c=HD)[:, at:at + 3].rearrange("p j r c -> p r j c")

        def tiles(eng, before, body, after):
            before(0, 0, 0)
            if sample:
                body(0, 0, 0, True, True)
                after(0, 0, 0)
                return
            body(0, 0, 0, True, False)
            body(1, 1, 0, False, False)
            with eng.Fori(0, TILES // 2 - 2) as pair:
                body(pair * 2 + 2, 0, pair + 1, False, False)
                body(pair * 2 + 3, 1, pair + 1, False, False)
            body(TILES - 2, 0, TILES // 2 - 1, False, False)
            body(TILES - 1, 1, TILES // 2 - 1, False, True)
            after(TILES - 1, 1, TILES // 2 - 1)

        block = ctx.enter_context(nc.Block())

        @block.sync
        def _(sp):
            def load(t, u):
                if sample:
                    sp.dma_start(zt[0][:, :, 0:SAMP], d["z_s"]).then_inc(z_in[0], 16)
                    sp.dma_start(rb[0][:, :, :, 0:SAMP].rearrange("p h k c -> p (h k) c"),
                                 d["rows_s"].rearrange("h k c -> (h k) c").unsqueeze(0)
                                 .broadcast_to([P, MH * 3, SAMP])).then_inc(z_in[0], 16)
                else:
                    tt = bass.ds(t, 1)
                    sp.dma_start(zt[u][:].rearrange("p r c -> p (r c)"),
                                 d["z"][tt].rearrange("o p r c -> (o p) (r c)")).then_inc(z_in[u], 16)
                    sp.dma_start(rb[u][:].rearrange("p h k c -> p (h k c)"),
                                 d["rows_p"][tt].rearrange("o h k c -> o (h k c)").broadcast_to([P, MH * 3 * P])
                                 ).then_inc(z_in[u], 16)

            def save(t, u):
                sp.wait_ge(S("gated"), t + 2)
                if sample:
                    sp.dma_start(d["yT_s"], yt[0][:, :, 0:SAMP]).then_inc(y_out[0], 16)
                else:
                    sp.dma_start(d["yT"][bass.ds(t, 1)].rearrange("o p k c -> (o p) (k c)"),
                                 yt[u][:].rearrange("p k c -> p (k c)")).then_inc(y_out[u], 16)

            sp.dma_start(level[:], d["level"]).then_inc(S("const_in"), 16)
            sp.dma_start(late[:], d["late"][int(sample)]).then_inc(S("const_in"), 16)
            if sample:
                sp.wait_ge(S("pads"), 3)
                for n, (dst, src) in enumerate(((cm, "s_cm"), (nm, "s_nm"), (gs, "s_gs"), (hs, "s_hs"),
                                                (one_t, "one_t"), (one_s, "one_s"))):
                    sp.dma_start(dst[:], d[src]).then_inc(S("const_in"), 16)
                for par in range(2):
                    for w in range(2):
                        sp.dma_start(dc[half(par), w], d["dec_s"][w, 3 * par:3 * par + 3].unsqueeze(0)
                                     .broadcast_to([HD, 3, NB])).then_inc(S("const_in"), 16)
                load(0, 0)
                save(0, 0)
            else:
                for w in range(2):
                    sp.dma_start(dec[:, w].rearrange("p t h -> p (t h)"),
                                 d["dec_p"][w:w + 1, :].broadcast_to([P, TILES * MH])).then_inc(S("const_in"), 16)
                load(0, 0)
                load(1, 1)
                with sp.Fori(0, TILES // 2 - 1) as pair:
                    for c in range(2):
                        save(pair * 2 + c, c)
                        load(pair * 2 + c + 2, c)
                for c in range(2):
                    save(TILES - 2 + c, c)
            sp.wait_ge(S("states"), 3)
            names = ("o_s_cm", "o_s_nm", "o_s_gs", "o_s_hs") if sample else ("o_p_cm", "o_p_gs", "o_p_hs")
            for n, src in zip(names, (cm, nm, gs, hs) if sample else (cm, gs, hs)):
                sp.dma_start(d[n], src[:]).then_inc(S("saved"), 16)
            sp.wait_ge(S("saved"), 16 * len(names))
            for u in range(nbuf):
                sp.wait_ge(y_out[u], 16 * (1 if sample else TILES // 2 + 1))

        const_n = 16 * (12 if sample else 4)

        @block.tensor
        def _(pe):
            pe.wait_ge(S("const_in"), const_n)
            pe.wait_ge(S("consts"), CONSTS)

            def finish(t, u, r):
                pe.wait_ge(S("yn"), t + 1)
                if not sample:
                    pe.wait_ge(S("hs"), t + 2)
                for k in range(KT):
                    mm = pe.transpose(pd[:, k // 4, (k % 4) * P:(k % 4 + 1) * P],
                                      y[:, 2 * k:2 * k + 2, :].rearrange("p h c -> p (h c)"), keep["ident"][:])
                mm.then_inc(S("y_turned"), 1)

            def body(t, u, r, first, last):
                v = lambda n, c: t * n + c
                z = zt[u]

                def turn(bank_, rows):
                    for n, row in enumerate(rows):
                        mm = pe.transpose(bank_[:, n // 4, (n % 4) * P:(n % 4 + 1) * P], z[:, row, :], keep["ident"][:])
                    mm.then_inc(S("turned"), 1)

                pe.wait_ge(z_in[u], 32 * (r + 1))
                for dst, keys, queries, done, free in ((pb, R_GK, R_GK, "kk", "vn"), (pc, R_GK, R_GQ, "qk_g", "o_gdn"),
                                                       (pa, R_MK, R_MQ, "qk_m", "state_read")):
                    pe.wait_ge(S(free), v(1, 1))
                    for par in range(2):
                        for j in range(3):
                            mm = pe.matmul(dst[:, par, j * P:(j + 1) * P], z[half(par), keys + j, :],
                                           z[half(par), queries + j, :], start=True, stop=True)
                    mm.then_inc(S(done), 1)

                def six(dst, lhs, rhs, done, n=2 * P):
                    for h in range(MH):
                        mm = pe.matmul(dst[:, h // 3, (h % 3) * P:(h % 3) * P + n], lhs(h), rhs(h), start=True, stop=True)
                    mm.then_inc(S(done), 1)

                def step(what, i):
                    if what == "turn":
                        pe.wait_ge(S("attn"), v(1, 1))
                        pe.wait_ge(S("pm"), v(1, 1))
                        turn(pc, [R_GK, R_GK + 1, R_GK + 2, R_GV, R_GV + 1, R_GV + 2])
                        turn(pa, [R_MK, R_MK + 1, R_MK + 2, R_MV, R_MV + 1, R_MV + 2, R_HI, R_HI + 1])
                    elif what == "turn_before":
                        if not first:
                            finish(t - 1, 1 - u, r)
                    elif what == "round":
                        j, g = groups[i]
                        if i == 0:
                            pe.wait_ge(S("hk"), v(2, 2))
                            pe.wait_ge(S("hq"), v(1, 1))
                            pe.wait_ge(S("gated"), v(1, 1))
                        else:
                            pe.wait_ge(S("masked"), v(R, i))
                        for par in range(2):
                            for n in range(4):
                                l = 4 * g + n - 1
                                if l < 0:
                                    a, b = z[half(par), R_HG0 + 2 * j + 1, :], z[half(par), R_HQ + j, :]
                                else:
                                    a, b = hk[half(par), l, j, :], hq[half(par), l, j, :]
                                mm = pe.matmul(pd[:, par, n * P:(n + 1) * P], a, b, start=True, stop=True)
                        mm.then_inc(S("round"), 1)
                    elif what == "mlstm":
                        pe.wait_ge(S("x"), v(2 * halvings, 2 * halvings))
                        if sample:
                            pe.wait_ge(S("qx"), 1)
                        else:
                            pe.wait_ge(S("cm"), v(1, 1))
                        W = HD + 1
                        for h in range(MH):
                            par, j = h // 3, h % 3
                            pe.matmul(pa[:, par, j * W:(j + 1) * W], pm[:, h, :], v1[:, h, :], start=True, stop=True)
                            o = pa[:, par, (3 + j) * W:(4 + j) * W]
                            if sample:
                                for b in range(NB):
                                    pe.matmul(o[:, 0:HD], qx[half(par), j, b, :], cm[half(par), j, b, :],
                                              start=(b == 0), stop=(b == NB - 1))
                                for b in range(NB):
                                    mm = pe.matmul(o[:, HD:W], qx[half(par), j, b, :], nm[half(par), j, b:b + 1],
                                                   start=(b == 0), stop=(b == NB - 1))
                            else:
                                mm = pe.matmul(o, z[half(par), R_MQ + j, :], cm[half(par), j, :], start=True, stop=True)
                        mm.then_inc(S("mo"), 1)
                    elif what == "hgrn":
                        pe.wait_ge(S("summed"), v(2, 2))
                        pe.wait_ge(S("tok_a"), v(2, 2))
                        if sample:
                            pe.wait_ge(S("qx"), 2)
                        else:
                            pe.wait_ge(S("hs"), v(1, 1))
                        for par in range(2):
                            for j in range(2):
                                o = pd[:, par, j * HD:(j + 1) * HD]
                                pe.matmul(o, ps[:, 2 * par + j, :], hv[:, 2 * j + par, :], start=True, stop=False)
                                if sample:
                                    for b in range(NB):
                                        pe.matmul(o, qx[half(par), j, b, :], hs[half(par), j, b, :], start=False,
                                                  stop=(b == NB - 1))
                                else:
                                    pe.matmul(o, hq[half(par), LEVELS, j, :], hs[half(par), j, :], start=False, stop=True)
                        for j in range(2):
                            mm = pe.transpose(pd[:, 0, (j + 1) * P:(j + 2) * P], hk[:, LEVELS, j, :], keep["ident"][:])
                        mm.then_inc(S("ho"), 1)
                    elif what == "hgrn_state":
                        pe.wait_ge(S("kd"), v(1, 1))
                        for par in range(2):
                            for j in range(2):
                                mm = pe.matmul(pd[half(par), 1, P + j * HD:P + (j + 1) * HD], kd[:, 2 * j + par, :],
                                               hv[:, 2 * j + par, :], start=True, stop=True)
                        mm.then_inc(S("dh"), 1)

                for l in range(halvings):
                    pe.wait_ge(S("cl"), v(halvings, l + 1))
                    if l:
                        pe.wait_ge(S("x"), v(2 * halvings, 2 * l - 1))
                    if l == 0:
                        pe.wait_ge(S("lt"), v(1, 1))
                    six(pb, lambda h: cl[:, l % 3, h, :], lambda h: pair_of(x, h) if l else pair_of(ident_r, 0), "m1")
                    for what, i in fill[l]:
                        step(what, i)
                    if l == 1:
                        pe.wait_ge(S("tok_d"), v(3, 2))
                    if l == 1:
                        pe.wait_ge(S("tok_a"), v(2, 2))
                        pe.wait_ge(S("tok_d"), v(3, 3))
                    if l:
                        pe.wait_ge(S("m1_copy"), v(halvings - 1, l))
                        pe.wait_ge(S("x"), v(2 * halvings, 2 * l))
                        six(pc, lambda h: xt[:, h, :], lambda h: pair_of(m1, h), "u")
                        six(pa, lambda h: m1[:, h, :], lambda h: pair_of(xt, h), "u")
                for what, i in rest:
                    step(what, i)
                pe.wait_ge(S("x"), v(2 * halvings, 2 * halvings - 1))
                six(pc, lambda h: lt[:, h, :], lambda h: x[:, h, :].bitcast(F32), "lx", P)
                if not sample:
                    step("hgrn_state", 0)
                pe.wait_ge(S("w"), v(1, 1))
                six(pb, lambda h: wn[:, h, :], lambda h: xt[:, h, :].bitcast(F32), "wx", P)
                if not sample:
                    pe.wait_ge(S("gs"), v(1, 1))
                for n, row in enumerate((R_GK, R_GQ)):
                    if sample:
                        pe.wait_ge(S("qx"), 3 + n)
                    for par in range(2):
                        for j in range(3):
                            if sample:
                                for b in range(NB):
                                    mm = pe.matmul(pc[:, par, (3 * n + j) * HD:(3 * n + j + 1) * HD], qx[half(par), j, b, :],
                                                   gs[half(par), j, b, :], start=(b == 0), stop=(b == NB - 1))
                            else:
                                mm = pe.matmul(pc[:, par, (3 * n + j) * HD:(3 * n + j + 1) * HD], z[half(par), row + j, :],
                                               gs[half(par), j, :], start=True, stop=True)
                    mm.then_inc(S("ks"), 1)
                if not sample:
                    pe.wait_ge(S("num"), v(1, 1))
                    for h in range(MH):
                        par, j = h // 3, h % 3
                        mm = pe.matmul(pa[half(par), 0, j * (HD + 1):(j + 1) * (HD + 1)], kw[:, h, :], v1[:, h, :],
                                       start=True, stop=True)
                    mm.then_inc(S("dm"), 1)
                pe.wait_ge(S("rv"), v(2, 2))
                for h in range(MH):
                    mm = pe.matmul(pb[:, h // 3, (h % 3) * HD:(h % 3 + 1) * HD], xf[:, h, :], rv[:, h, :],
                                   start=True, stop=True)
                mm.then_inc(S("xr"), 1)
                pe.wait_ge(S("vn"), v(1, 2))
                pe.wait_ge(S("qs_read"), v(1, 1))
                for h in range(MH):
                    mm = pe.matmul(pc[:, h // 3, (h % 3) * HD:(h % 3 + 1) * HD], at_[:, h, :], vn[:, h, :],
                                   start=True, stop=True)
                mm.then_inc(S("av"), 1)
                if not sample:
                    for h in range(MH):
                        par, j = h // 3, h % 3
                        mm = pe.matmul(pa[half(par), 1, j * HD:(j + 1) * HD], gkw[:, h, :], vn[:, h, :], start=True, stop=True)
                    mm.then_inc(S("dg"), 1)
                if sample:
                    finish(0, 0, 0)
                    pe.wait_ge(S("num"), 1)
                    for h in range(MH):
                        mm = pe.matmul(pa[half(h // 3), 0, (h % 3) * NB:(h % 3 + 1) * NB], kw[:, h, :], one_s[:],
                                       start=True, stop=True)
                    mm.then_inc(S("dn"), 1)
                    pe.wait_ge(S("kd"), 1)
                    for n, (keys, at) in enumerate([(kw, j) for j in range(3)] + [(gkw, j) for j in range(3)] +
                                                   [(kd, j) for j in range(2)]):
                        pe.wait_ge(S("vx"), n + 1)
                        for par in range(2):
                            key = keys[:, 2 * at + par, :] if keys is kd else keys[:, 3 * par + at, :]
                            mm = pe.matmul((pa, pb)[n % 2][half(par), 1, :], key, vx[:, n % 2, par].rearrange("p b c -> p (b c)"),
                                           start=True, stop=True)
                        mm.then_inc(S("ds"), 1)
            tiles(pe, lambda *a: None, body, (lambda *a: None) if sample else finish)

        @block.scalar
        def _(act):
            act.preload_act_table_set(LN_EXP)
            act.wait_ge(S("const_in"), const_n)
            act.wait_ge(S("consts"), CONSTS)

            def before(t, u, r):
                decays(t)
                hgrn_decays(t)

            def decays(t):
                act.wait_ge(S("exa"), t + 1)
                act.activation(ex[:], ex[:], ACT.Exp).then_inc(S("ex"), 1)

            def hgrn_decays(t):
                act.wait_ge(S("nabs"), t + 1)
                act.activation(e[:], e[:], ACT.Exp).then_inc(S("e"), 1)

            def finish(t, u, r):
                act.wait_ge(S("o_gdn"), t + 2)
                act.wait_ge(S("y_h"), t + 1)
                act.activation(sq[:], y[:], ACT.Square).then_inc(S("sq"), 1)
                act.wait_ge(S("ss"), t + 1)
                act.activation(ss[:, 1, :], ss[:, 0, :], ACT.Ln, scale=1.0 / HD, bias=keep["eps"][:, :]).then_inc(S("rms"), 1)
                act.wait_ge(S("rms"), t * 2 + 1)
                act.activation(ss[:, 2, :], ss[:, 1, :], ACT.Exp, scale=-0.5).then_inc(S("rms"), 1)

            def body(t, u, r, first, last):
                v = lambda n, c: t * n + c

                def step(what, i):
                    if what == "turn":
                        act.wait_ge(S("turned"), v(2, 2))
                        act.activation(hm(v1[:])[:, :, :, 0:HD], tok(pa, 3), ACT.Copy).then_inc(S("tok_a"), 1)
                        act.activation(hv[:].rearrange("p h c -> p (h c)"), pa[:, 1, 2 * P:4 * P], ACT.Copy
                                       ).then_inc(S("tok_a"), 1)
                    elif what == "hgrn":
                        act.wait_ge(S("ho"), v(1, 1))
                        act.activation(ym(y[:, Y_H:16, :]), pv(pd, HD, n=2), ACT.Copy).then_inc(S("y_h"), 1)
                        act.activation(kd[:].rearrange("p h c -> p (h c)"), pd[:, 0, P:3 * P], ACT.Copy).then_inc(S("kd"), 1)

                if not first:
                    finish(t - 1, 1 - u, r)
                for l in range(halvings):
                    if l:
                        act.wait_ge(S("m1"), v(halvings, l + 1))
                        act.activation(hm(m1[:, 0:MH]), pv(pb, P), ACT.Copy).then_inc(S("m1_copy"), 1)
                    for what, i in fill[l]:
                        step(what, i)
                if not last:
                    hgrn_decays(t + 1)
                for what, i in rest:
                    step(what, i)
                if not last:
                    decays(t + 1)
                act.wait_ge(S("xr"), v(1, 1))
                act.activation(hm(vn[:]), pv(pb, HD), ACT.Copy).then_inc(S("vn"), 1)
            tiles(act, before, body, finish)

        @block.gpsimd
        def _(pool):
            pool.memset(zero[:], 0.0).then_inc(S("zero"), 1)
            pool.wait_ge(S("zero"), 1)
            pool.wait_ge(S("const_in"), const_n)
            pool.wait_ge(S("consts"), CONSTS)

            def decays(t, u):
                pool.wait_ge(S("ex"), t + 1)
                pool.tensor_tensor(bd[:], ex[:, :, 1, :], rb[u][:, :, 2, :], ALU.mult).then_inc(S("bd"), 1)
                pool.wait_ge(S("bd"), t * 2 + 1)
                pool.tensor_tensor(bd[:], bd[:], late[:, 1:2, :].broadcast_to([P, MH, P]), ALU.mult).then_inc(S("bd"), 1)

            def differences(t, u, r, levels, only=False):
                g = zt[u][:, R_HG0:NROW:2, :]
                pool.wait_ge(z_in[u], 32 * (r + 1))
                if not only:
                    pool.wait_ge(S("hq"), t)
                for l in levels:
                    if l == LEVELS:
                        ins = pool.tensor_tensor(e[:, l], g, zero[:].unsqueeze(2).broadcast_to([P, 2, P]), ALU.add)
                        continue
                    size, at = (2 << l, (1 << l) - 1) if l < LEVELS else ((NT, NT - 1) if sample else (P, P - 1))
                    gv = g.rearrange("p j (n b) -> p j n b", b=size)
                    for j in range(2):
                        ins = pool.tensor_tensor(e[:, l, j].rearrange("p (n b) -> p n b", b=size), gv[:, j],
                                                 gv[:, j, :, at:at + 1].broadcast_to([P, P // size, size]), ALU.subtract)
                if levels[-1] == LEVELS + 1:
                    ins.then_inc(S("diff"), 1)

            def hgrn_keys(t, u, only=False):
                kr = zt[u][:, R_HG0 + 1:NROW:2, :]
                pool.wait_ge(S("e"), t + 1)
                if not only:
                    pool.wait_ge(S("ho"), t)
                pool.tensor_tensor(hk[:, 0:LEVELS], e[:, 0:LEVELS], kr.unsqueeze(1).broadcast_to([P, LEVELS, 2, P]),
                                   ALU.mult).then_inc(S("hk"), 1)
                pool.tensor_tensor(hk[:, LEVELS], e[:, LEVELS + 1], kr, ALU.mult).then_inc(S("hk"), 1)

            def before(t, u, r):
                differences(t, u, r, range(LEVELS + 2), only=True)
                decays(t, u)
                hgrn_keys(t, u, only=True)

            def body(t, u, r, first, last):
                v = lambda n, c: t * n + c
                width = 4

                def add_up(i):
                    j, g = groups[i]
                    pool.wait_ge(S("masked"), v(R, i + 1))
                    t4 = lambda a, n: ph[:, j:HH:2, 4 * g + a:4 * g + a + n, :]
                    pool.tensor_tensor(t4(0, 2), t4(0, 2), t4(2, 2), ALU.add).then_inc(S("half"), 1)
                    pool.wait_ge(S("half"), v(R, i + 1))
                    out = ps[:, j:HH:2, :]
                    if g == 0:
                        ins = pool.tensor_tensor(out, ph[:, j:HH:2, 0, :], ph[:, j:HH:2, 1, :], ALU.add)
                        if terms == width:
                            ins.then_inc(S("summed"), 1)
                        else:
                            ins.then_inc(S("part"), 1)
                    else:
                        pool.tensor_tensor(ph[:, j:HH:2, 4, :], ph[:, j:HH:2, 4, :], ph[:, j:HH:2, 5, :], ALU.add
                                           ).then_inc(S("part"), 1)
                        pool.wait_ge(S("part"), v(R, i + 1))
                        pool.tensor_tensor(out, out, ph[:, j:HH:2, 4, :], ALU.add).then_inc(S("summed"), 1)

                pool.wait_ge(S("lt"), v(1, 1))
                for l in range(halvings):
                    if l >= 3:
                        pool.wait_ge(S("m1"), v(halvings, l - 1))
                    if l == 3:
                        pool.wait_ge(S("x"), v(2 * halvings, 2))
                    if l >= 4:
                        add_up(l - 4)
                    pool.tensor_tensor(cl[:, l % 3], lt[:], level[:, l + 1:l + 2, :].broadcast_to([P, MH, P]),
                                       ALU.mult).then_inc(S("cl"), 1)
                    if not last and l == LEVELS - 1:
                        differences(t + 1, 1 - u, r + u, range(LEVELS + 2))
                for i in range(len(groups)) if sample else [3]:
                    add_up(i)
                if not last:
                    hgrn_keys(t + 1, 1 - u)
                    decays(t + 1, 1 - u)
            tiles(pool, before, body, lambda *a: None)

        @block.vector
        def _(dve):
            dve.memset(den[:, 0, 0:1], 0.0).then_inc(S("vn"), 1)
            dve.memset(den[:, 0, 1:2], 0.0).then_inc(S("o_gdn"), 1)
            dve.memset(den[:, 0, 2:3], 0.0).then_inc(S("state_read"), 1)
            dve.memset(den[:, 0, 3:4], 0.0).then_inc(S("gated"), 1)
            if sample:
                dve.memset(zt[0][:, :, SAMP:P], 0.0).then_inc(S("pads"), 1)
                dve.memset(rb[0][:, :, :, SAMP:P], 0.0).then_inc(S("pads"), 1)
                dve.memset(cc[0][:], 0.0).then_inc(S("pads"), 1)
                dve.wait_ge(S("pads"), 3)
            else:
                dve.memset(cm[:], 0.0).then_inc(S("cm"), 1)
                dve.memset(gs[:], 0.0).then_inc(S("gs"), 1)
                dve.memset(hs[:], 0.0).then_inc(S("hs"), 1)
                dve.memset(den[:, 0, 4:5], 0.0).then_inc(y_out[0], 16)
                dve.memset(den[:, 0, 5:6], 0.0).then_inc(y_out[1], 16)
            dve.memset(v1[:, :, HD:HD + 1], 1.0).then_inc(S("consts"), 1)
            dve.wait_ge(S("const_in"), const_n)
            for tile in (x, xt, m1):
                dve.tensor_scalar(tile[:, MH, :], keep["ident"][:], 0.0, None, ALU.mult)
            dve.tensor_copy(ident_r[:], keep["ident"][:].unsqueeze(1).broadcast_to([P, 2, P])).then_inc(S("consts"), 1)
            ident4 = keep["ident"][:].unsqueeze(1).unsqueeze(1).broadcast_to([P, 2, 3, P])
            STEPS = 64

            def chain(sem, base):
                count = [0]

                def then(ins):
                    count[0] += 1
                    ins.then_inc(S(sem), 1)
                    dve.wait_ge(S(sem), base + count[0])
                return then, count

            def decays(t, u, r, then):
                dve.wait_ge(z_in[u], 32 * (r + 1))
                if sample:
                    then(dve.tensor_copy(cc[0][0:SAMP], keep["cols_s"][:]))
                else:
                    dve.tensor_scalar(cc[u][:], keep["cols_p"][:, :, bass.ds(t * MH, MH)], 1.0, None, ALU.mult)
                    for par in range(2):
                        ins = dve.tensor_scalar(dc[u][half(par)], dec[half(par), :, bass.ds(t, 1), 3 * par:3 * par + 3]
                                                .rearrange("p w o j -> p w (o j)"), 1.0, None, ALU.mult)
                    then(ins)
                then(dve.tensor_tensor(ex[:], rb[u][:, :, 0:2, :], cc[u][:, Q_A:Q_NG + 1, :].rearrange("p k h -> p h k")
                                       .unsqueeze(3).broadcast_to([P, MH, 2, P]), ALU.add))
                dve.scalar_tensor_tensor(ex[:].rearrange("p h k c -> p (h k) c"), ex[:].rearrange("p h k c -> p (h k) c"),
                                         0.0, late[:, 0:1, :].broadcast_to([P, 2 * MH, P]), ALU.min,
                                         ALU.add).then_inc(S("exa"), 1)

            def distances(t):
                dve.wait_ge(S("diff"), t + 1)
                ef = e[:].rearrange("p l j c -> p (l j c)")
                dve.scalar_tensor_tensor(ef, ef, -1.0, ef, ALU.mult, ALU.min).then_inc(S("nabs"), 1)

            def hgrn_queries(t, u):
                qr = zt[u][:, R_HQ:R_HQ + 2, :]
                dve.wait_ge(S("e"), t + 1)
                dve.tensor_copy(eg[:], e[:, LEVELS, :, P - 1:P])
                dve.tensor_tensor(hq[:], e[:, 0:LEVELS + 1], qr.unsqueeze(1).broadcast_to([P, LEVELS + 1, 2, P]),
                                  ALU.mult).then_inc(S("hq"), 1)

            def before(t, u, r):
                decays(t, u, r, chain("step0", 0)[0])
                distances(t)
                hgrn_queries(t, u)

            def normalise(t):
                dve.wait_ge(S("sq"), t + 1)
                dve.tensor_reduce(ss[:, 0, :], sq[:], AX.X, ALU.add).then_inc(S("ss"), 1)

            def scale(t):
                dve.wait_ge(S("rms"), t * 2 + 2)
                dve.wait_ge(S("y_m"), t + 1)
                dve.tensor_tensor(y[:], y[:], ss[:, 2, :].unsqueeze(2).broadcast_to([P, 16, HD]),
                                  ALU.mult).then_inc(S("yn"), 1)

            def gate(t, u, r, then):
                if not sample:
                    dve.wait_ge(y_out[u], 16 * (r + 1))
                dve.wait_ge(S("y_turned"), t + 1)
                then(dve.tensor_tensor(yt[u][:], pd[:].rearrange("p a (k c) -> p (a k) c", c=P),
                                       zt[u][:, R_MO:R_MO + 8, :], ALU.mult))
                dve.tensor_copy(den[:, 0, 1:2], den[:, 1, 1:2]).then_inc(S("gated"), 1)

            def after(t, u, r):
                normalise(t)
                scale(t)
                gate(t, u, r, chain("step1", 0)[0])

            def body(t, u, r, first, last):
                v = lambda n, c: t * n + c
                z = zt[u]
                then, count = chain("step", t * STEPS)
                dve.wait_ge(S("bd"), v(2, 2))
                dve.wait_ge(S("kk"), v(1, 1))
                dve.tensor_tensor(hm(lt[:]), pv(pb, P), hm(bd[:]), ALU.mult).then_inc(S("lt"), 1)
                dve.wait_ge(S("qk_g"), v(1, 1))
                dve.tensor_tensor(hm(at_[:]), pv(pc, P), hm(ex[:, :, 1, :]), ALU.mult).then_inc(S("attn"), 1)
                dve.wait_ge(S("qk_m"), v(1, 1))
                dve.wait_ge(S("ex"), v(1, 1))
                dve.tensor_tensor(hm(pm[:]), pv(pa, P), hm(ex[:, :, 0, :]), ALU.mult).then_inc(S("pm"), 1)
                if not first:
                    normalise(t - 1)

                def spread(rows, pairs):
                    for j in range(pairs):
                        ins = dve.tensor_tensor(qx[:, j], rows[:, j:j + 1, :].broadcast_to([P, NB, P]), one_t[:], ALU.mult)
                    ins.then_inc(S("qx"), 1)

                def step(what, i):
                    if what == "turn":
                        dve.wait_ge(S("turned"), v(2, 1))
                        dve.tensor_tensor(hm(gkw[:]), tok(pc, 0), colh(u, Q_EGL, HD), ALU.mult).then_inc(S("tok_d"), 1)
                        dve.tensor_tensor(hm(bv[:]), tok(pc, 3), colh(u, Q_BETA, HD), ALU.mult).then_inc(S("tok_d"), 1)
                        dve.wait_ge(S("tok_a"), v(2, 2))
                        dve.tensor_tensor(hm(kw[:]), tok(pa, 0), colh(u, Q_WS, HD), ALU.mult).then_inc(S("tok_d"), 1)
                    elif what == "turn_before":
                        if not first:
                            gate(t - 1, 1 - u, r - 1 + u, then)
                    elif what == "round":
                        j, g = groups[i]
                        dve.wait_ge(S("round"), v(R, i + 1))
                        dve.tensor_tensor(ph[:, j:HH:2, 4 * g:4 * g + 4, :], pv(pd, P, n=4),
                                          level[:, 4 * g:4 * g + 4, :].unsqueeze(1).broadcast_to([P, 2, 4, P]),
                                          ALU.mult).then_inc(S("masked"), 1)
                    elif what == "mlstm":
                        if sample:
                            spread(z[:, R_MQ:R_MQ + 3, :], 3)
                        dve.wait_ge(S("mo"), v(1, 1))
                        W = HD + 1
                        then(dve.tensor_tensor(hm(num[:]), pv(pa, W, 3 * W), colh(u, Q_WI, W), ALU.mult))
                        ins = dve.tensor_tensor(hm(num[:]), hm(num[:]), pv(pa, W), ALU.add)
                        ins.then_inc(S("num"), 1)
                        dve.wait_ge(S("num"), v(1, 1))
                        then(dve.scalar_tensor_tensor(den[:, 0, :], num[:, :, HD], -1.0, num[:, :, HD], ALU.mult, ALU.max))
                        then(dve.tensor_scalar(den[:, 0, :], den[:, 0, :], 1.0, None, ALU.max))
                        then(dve.reciprocal(den[:, 1, :], den[:, 0, :]))
                        dve.tensor_tensor(ym(y[:, Y_M:Y_G, :]), hm(num[:])[:, :, :, 0:HD],
                                          den[:, 1, :].rearrange("p (r j) -> p r j", r=2).unsqueeze(3)
                                          .broadcast_to([P, 2, 3, HD]), ALU.mult).then_inc(S("y_m"), 1)
                        if not sample:
                            then(dve.tensor_tensor(cm[:], cm[:], dc[u][:, 0, :].unsqueeze(2).broadcast_to([P, 3, W]), ALU.mult))
                    elif what == "hgrn":
                        if sample:
                            dve.wait_ge(S("mo"), 1)
                            spread(hq[:, LEVELS], 2)
                        if not sample:
                            dve.wait_ge(S("ho"), v(1, 1))
                            then(dve.tensor_tensor(hs[:], hs[:], eg[:].broadcast_to([P, 2, HD]), ALU.mult))
                            dve.wait_ge(S("dh"), v(1, 1))
                            dve.tensor_tensor(hs[:], hs[:], pd[:, 1, P:2 * P].rearrange("p (j c) -> p j c", j=2),
                                              ALU.add).then_inc(S("hs"), 1)

                for l in range(halvings):
                    if l == 0:
                        dve.wait_ge(S("m1"), v(halvings, 1))
                        dve.tensor_tensor(hm(x[:, 0:MH]), ident4, pv(pb, P), ALU.subtract).then_inc(S("x"), 1)
                        dve.tensor_tensor(hm(xt[:, 0:MH]), ident4, hm(cl[:, 0].bitcast(F32)), ALU.subtract).then_inc(S("x"), 1)
                        if not first:
                            scale(t - 1)
                        for what, i in fill[0]:
                            step(what, i)
                    else:
                        U = 2 * (halvings - 1)
                        dve.wait_ge(S("u"), v(U, 2 * l - 1))
                        dve.wait_ge(S("x"), v(2 * halvings, 2 * l))
                        dve.tensor_tensor(hm(x[:, 0:MH]), hm(x[:, 0:MH].bitcast(F32)), pv(pc, P), ALU.subtract).then_inc(S("x"), 1)
                        for what, i in fill[l]:
                            step(what, i)
                        dve.wait_ge(S("u"), v(U, 2 * l))
                        dve.tensor_tensor(hm(xt[:, 0:MH]), hm(xt[:, 0:MH].bitcast(F32)), pv(pa, P), ALU.subtract).then_inc(S("x"), 1)
                if not last:
                    decays(t + 1, 1 - u, r + u, then)
                for what, i in rest:
                    if sample or what != "hgrn":
                        step(what, i)
                if not last:
                    distances(t + 1)
                dve.wait_ge(S("lx"), v(1, 1))
                dve.wait_ge(S("x"), v(2 * halvings, 2 * halvings))
                dve.tensor_tensor(hm(wn[:]), hm(x[:, 0:MH].bitcast(F32)), pv(pc, P), ALU.add).then_inc(S("w"), 1)
                if not sample:
                    step("hgrn", 0)
                dve.wait_ge(S("wx"), v(1, 1))
                dve.scalar_tensor_tensor(hm(xf[:]), hm(xt[:, 0:MH].bitcast(F32)), 2.0, pv(pb, P), ALU.mult,
                                         ALU.subtract).then_inc(S("xf"), 1)
                if sample:
                    dve.wait_ge(S("ho"), 1)
                    spread(z[:, R_GK:R_GK + 3, :], 3)
                    dve.wait_ge(S("ks"), 1)
                    spread(z[:, R_GQ:R_GQ + 3, :], 3)
                dve.wait_ge(S("ks"), v(2, 2))
                dve.tensor_tensor(hm(rv[:]), pv(pc, HD), colh(u, Q_NBEG, HD), ALU.mult).then_inc(S("rv"), 1)
                dve.wait_ge(S("rv"), v(2, 1))
                dve.tensor_tensor(rv[:], rv[:], bv[:], ALU.add).then_inc(S("rv"), 1)
                yg = ym(y[:, Y_G:Y_H, :])
                dve.tensor_tensor(yg, pv(pc, HD, 3 * HD), colh(u, Q_EG, HD), ALU.mult).then_inc(S("qs_read"), 1)
                if not sample:
                    dve.wait_ge(S("dm"), v(1, 1))
                    dve.tensor_tensor(cm[:], cm[:], pa[:, 0, 0:3 * (HD + 1)].rearrange("p (j c) -> p j c", j=3),
                                      ALU.add).then_inc(S("cm"), 1)
                if not last:
                    hgrn_queries(t + 1, 1 - u)
                dve.wait_ge(S("qs_read"), v(1, 1))
                dve.wait_ge(S("av"), v(1, 1))
                dve.tensor_tensor(yg, yg, pv(pc, HD), ALU.add).then_inc(S("o_gdn"), 1)
                if not sample:
                    then(dve.tensor_tensor(gs[:], gs[:], dc[u][:, 1, :].unsqueeze(2).broadcast_to([P, 3, HD]), ALU.mult))
                    dve.wait_ge(S("dg"), v(1, 1))
                    dve.tensor_tensor(gs[:], gs[:], pa[:, 1, 0:3 * HD].rearrange("p (j c) -> p j c", j=3),
                                      ALU.add).then_inc(S("gs"), 1)
                    dve.tensor_copy(den[:, 0, 0:1], den[:, 1, 0:1]).then_inc(S("state_read"), 1)
                assert count[0] < STEPS
                dve.tensor_copy(den[:, 0, 2:3], den[:, 1, 2:3]).then_inc(S("step"), STEPS - count[0])
            tiles(dve, before, body, after)
            if not sample:
                dve.wait_ge(S("gs"), TILES + 1)
                dve.tensor_copy(den[:, 0, 3:4], den[:, 1, 3:4]).then_inc(S("states"), 3)
                return
            dve.tensor_tensor(nm[:], nm[:], dc[:, 0], ALU.mult).then_inc(S("decayed"), 1)
            by_seq = lambda a, n: a.unsqueeze(3).broadcast_to([P, n, NB, HD])
            dve.tensor_tensor(cm[:], cm[:], by_seq(dc[:, 0], 3), ALU.mult).then_inc(S("decayed"), 1)
            dve.tensor_tensor(gs[:], gs[:], by_seq(dc[:, 1], 3), ALU.mult).then_inc(S("decayed"), 1)
            dve.tensor_tensor(hs[:], hs[:], by_seq(e[:, LEVELS, :, NT - 1:SAMP:NT], 2), ALU.mult).then_inc(S("decayed"), 1)
            dve.wait_ge(S("decayed"), 4)
            dve.wait_ge(S("dn"), 1)
            dve.tensor_tensor(nm[:], nm[:], pa[:, 0, 0:3 * NB].rearrange("p (j b) -> p j b", b=NB), ALU.add
                              ).then_inc(S("states"), 1)
            work = [(cm, v1, j) for j in range(3)] + [(gs, vn, j) for j in range(3)] + [(hs, hv, j) for j in range(2)]

            def by_sequence(n):
                _, vals, j = work[n]
                val = vals[:, 2 * j:2 * j + 2, :] if vals is hv else vals[:, j:MH:3, 0:HD]
                dve.tensor_tensor(vx[:, n % 2], val.unsqueeze(2).broadcast_to([P, 2, NB, HD]),
                                  one_s[:].unsqueeze(1).unsqueeze(3).broadcast_to([P, 2, NB, HD]), ALU.mult
                                  ).then_inc(S("vx"), 1)

            by_sequence(0)
            by_sequence(1)
            for n, (state, _, j) in enumerate(work):
                dve.wait_ge(S("ds"), n + 1)
                ins = dve.tensor_tensor(state[:, j], state[:, j], (pa, pb)[n % 2][:, 1, :]
                                        .rearrange("p (b c) -> p b c", b=NB), ALU.add)
                if n + 2 < len(work):
                    by_sequence(n + 2)
            ins.then_inc(S("states"), 2)


BLOCKS = 4
BP, BS = SEQ // BLOCKS, SAMP // BLOCKS
BT = BP + BS
UNITS = [("out", 0), ("ff1", 0), ("ff1", 1), ("ff2", 0), ("ff1", 2), ("ff2", 1), ("ff1", 3), ("ff2", 2), ("ff2", 3)]
CHUNKS = len(UNITS) * KT
ROWS = [(i * P, P) for i in range(BP // P)] + [(BP, BS)]


def feed_forward(nc, d, keep):
    with ExitStack() as ctx:
        sb = lambda n, s, t=F32: ctx.enter_context(nc.sbuf_tensor("ff_" + n, s, t))
        S = Sems(nc, ctx, "ff_")
        a_hi, a_lo = (sb(n, [P, 2, KT, BT], F32R) for n in ("a_hi", "a_lo"))
        h_hi, h_lo = (sb(n, [P, KT, BT], F32R) for n in ("h_hi", "h_lo"))
        out = sb("out", [P, KT, BT])
        x1 = sb("x1", [P, len(ROWS), D])
        w = sb("w", [P, 2, KT, P])
        w_hi, w_lo = (sb(n, [P, 2, KT, P], F32R) for n in ("w_hi", "w_lo"))
        gate_p = sb("gate_p", [P, 2, D])
        gate_s = sb("gate_s", [BS, 2, D])
        tmp, xs, junk = (sb(n, [P, D]) for n in ("tmp", "xs", "junk"))
        ht = sb("ht", [P, KT, P])
        sqf = sb("sqf", [P, 2, BT])
        stat = sb("stat", [P, 6])
        one = sb("one", [P, 1])
        const_one = S("const_one")
        refined = S("refined")
        acc = ctx.enter_context(nc.psum_tensor("ff_acc", [P, 2, 2, 512], F32))
        ty = ctx.enter_context(nc.psum_tensor("ff_ty", [P, D], F32))
        th = ctx.enter_context(nc.psum_tensor("ff_th", [P, KT, P], F32))
        w_in = [S("w_in0"), S("w_in1")]
        y_in = [S(f"y_in{i}") for i in range(len(ROWS))]
        (const_in, x_in, stored, split_hi, split_lo, product, drained, in_hi, in_lo, squared, f_hi, f_lo,
         turned, ssum, slog, rstd, scaled, x_done, hsum, hlog, hrstd, xs_ready, h_turned, h_mod, h_shift, h_hi_ready,
         h_lo_ready, left) = (
            S(n) for n in ("const_in", "x_in", "stored", "split_hi", "split_lo", "product", "drained",
                           "in_hi", "in_lo", "squared", "f_hi", "f_lo", "turned", "ssum", "slog", "rstd", "scaled",
                           "x_done", "hsum", "hlog", "hrstd", "xs_ready", "h_turned", "h_mod", "h_shift",
                           "h_hi_ready", "h_lo_ready", "left"))
        NR = len(ROWS)
        REFINES = 4 * 3 * NR
        G = BT // 2

        def blocks(eng, body):
            with eng.Fori(0, BLOCKS - 1) as b:
                body(b, False)
            body(BLOCKS - 1, True)

        def chunks(eng, b, unit, body):
            with eng.Fori(0, KT // 2) as pair:
                for c in range(2):
                    body(b * CHUNKS + pair * 2 + (unit * KT + c), pair * 2 + c, c,
                         b * (CHUNKS // 2) + pair + unit * (KT // 2))

        block = ctx.enter_context(nc.Block())

        @block.sync
        def _(sp):
            def body(b, last):
                for unit, (kind, q) in enumerate(UNITS):
                    src = d["w_unit"][{"out": 0, "ff1": 1 + 2 * q, "ff2": 2 + 2 * q}[kind]]

                    def load(n, oc, u, use):
                        sp.wait_ge(split_lo, n + 1)
                        sp.dma_start(w[:, u].rearrange("p k c -> p (k c)"),
                                     src[bass.ds(oc, 1)].rearrange("o p c -> (o p) c")).then_inc(w_in[u], 16)
                    chunks(sp, b, unit, load)
            blocks(sp, body)

        @block.gpsimd
        def _(pool):
            pool.memset(one[:], 1.0).then_inc(const_one, 1)
            pool.wait_ge(const_one, 1)
            ones = one[:].unsqueeze(2).broadcast_to([P, KT, P])

            def body(b, last):
                for unit in range(len(UNITS)):
                    def split(n, oc, u, use):
                        pool.wait_ge(w_in[u], use * 16 + 16)
                        pool.wait_ge(product, n + 1)
                        pool.tensor_tensor(w_hi[:, u], w[:, u], ones, ALU.mult).then_inc(split_hi, 1)
                        pool.wait_ge(split_hi, n + 1)
                        pool.tensor_tensor(w_lo[:, u], w[:, u], w_hi[:, u].bitcast(F32), ALU.subtract).then_inc(split_lo, 1)
                    chunks(pool, b, unit, split)
            blocks(pool, body)

        @block.tensor
        def _(pe):

            def turn_out(b, i, second):
                at, n = ROWS[i]
                m = b * (2 * NR) + (second * NR + i)
                pe.wait_ge(scaled, m + 1)
                for k in range(KT):
                    mm = pe.transpose(ty[0:n, k * P:(k + 1) * P], out[:, k, at:at + n], keep["ident"][:])
                mm.then_inc(turned, 1)

            def turn_h(b, i):
                pe.wait_ge(xs_ready, b * NR + i + 1)
                pe.wait_ge(h_mod, b * NR + i + 1)
                for k in range(KT):
                    mm = pe.transpose(th[:, k, :], xs[:, k * P:(k + 1) * P], keep["ident"][:])
                mm.then_inc(h_turned, 1)

            def body(b, last):
                for unit, (kind, q) in enumerate(UNITS):
                    if kind == "out":
                        ready = (in_lo, b * NR + NR)
                        src = lambda k: (a_hi[:, 0, k], a_lo[:, 0, k])
                    elif kind == "ff1":
                        ready = (h_lo_ready, b * NR + NR)
                        src = lambda k: (h_hi[:, k], h_lo[:, k])
                    else:
                        ready = (f_lo, b * (4 * KT) + (q + 1) * KT)
                        src = lambda k, u=q % 2: (a_hi[:, u, k], a_lo[:, u, k])

                    def products(n, oc, u, use):
                        pe.wait_ge(*ready)
                        pe.wait_ge(split_lo, n + 3)
                        pe.wait_ge(drained, n + 1)
                        for g in range(2):
                            cols = slice(g * G, (g + 1) * G)
                            for k in range(KT):
                                hi, lo = src(k)
                                dst = acc[:, u, g, 0:G]
                                pe.matmul(dst, w_hi[:, u, k], hi[:, cols], start=(k == 0), stop=False)
                                pe.matmul(dst, w_hi[:, u, k], lo[:, cols], start=False, stop=False)
                                mm = pe.matmul(dst, w_lo[:, u, k], hi[:, cols], start=False, stop=(k == KT - 1))
                        mm.then_inc(product, 1)
                    chunks(pe, b, unit, products)
                    if kind == "out":
                        pe.wait_ge(drained, b * CHUNKS + KT + 2)
                        turn_out(b, 0, 0)
                        for i in range(NR + 1):
                            if i + 1 < NR:
                                turn_out(b, i + 1, 0)
                            if i:
                                turn_h(b, i - 1)
                pe.wait_ge(drained, b * CHUNKS + CHUNKS + 2)
                for i in range(NR):
                    turn_out(b, i, 1)
            blocks(pe, body)

        @block.scalar
        def _(act):
            act.preload_act_table_set(LN_EXP)
            for i in range(2):
                act.dma_start(gate_p[:, i, :], d["gates"][SAMP:SAMP + 1, i, :].broadcast_to([P, D])).then_inc(const_in, 16)

            def load(b, i):
                at, n = ROWS[i]
                src = (d["yT"][bass.ds(b * (BP // P) + i, 1)].rearrange("o p k c -> (o p) k c") if n == P else
                       d["yT_s"][:, :, bass.ds(b * BS, BS)])
                act.dma_start(out[:, :, at:at + n], src).then_inc(y_in[i], 16)

            def split(b, i):
                at, n = ROWS[i]
                act.wait_ge(y_in[i], b * 16 + 16)
                act.activation(a_hi[:, 0, :, at:at + n], out[:, :, at:at + n], ACT.Copy).then_inc(in_hi, 1)

            def square(n, src, dst, at, done):
                act.activation(dst[0:n, :], src, ACT.Square, accum_out=stat[0:n, at:at + 1]).then_inc(done, 1)

            def log(n, at, before, count, done):
                act.wait_ge(before, count)
                act.activation(stat[0:n, at + 1:at + 2], stat[0:n, at:at + 1], ACT.Ln, scale=1.0 / D,
                               bias=keep["eps"][0:n, :]).then_inc(done, 1)

            def root(n, at, before, count, done):
                act.wait_ge(before, count)
                act.activation(stat[0:n, at + 2:at + 3], stat[0:n, at + 1:at + 2], ACT.Exp, scale=-0.5).then_inc(done, 1)

            def body(b, last):
                act.wait_ge(left, b + 1)
                met(act, left)
                act.dma_start(gate_s[:], d["gates"][bass.ds(b * BS, BS)]).then_inc(x_in, 16)
                act.wait_ge(stored, b * 32 + 32)
                met(act, left)
                act.dma_start(x1[:, 0:BP // P, :], d["x"][bass.ds(b * BP, BP), :].rearrange("(i p) c -> p i c", p=P)
                              ).then_inc(x_in, 16)
                act.dma_start(x1[0:BS, BP // P, :], d["x"][bass.ds(b * BS + SEQ, BS), :]).then_inc(x_in, 16)
                for i in range(NR + 2):
                    m, k = b * (2 * NR) + i + 1, b * NR + i
                    y, h = i < NR, 1 <= i <= NR
                    ny, nh = ROWS[min(i, NR - 1)][1], ROWS[min(max(i - 1, 0), NR - 1)][1]
                    if y:
                        act.wait_ge(turned, m)
                        square(ny, ty[0:ny, :], junk, 0, ssum)
                    if h:
                        act.wait_ge(x_done, m)
                        act.wait_ge(h_turned, k)
                        square(nh, x1[0:nh, i - 1, :], xs, 3, hsum)
                    if y:
                        log(ny, 0, ssum, m, slog)
                    if h:
                        log(nh, 3, hsum, k, hlog)
                    if y:
                        root(ny, 0, slog, m, rstd)
                    if h:
                        root(nh, 3, hlog, k, hrstd)
                    if h:
                        act.wait_ge(refined, b * REFINES + 4 * min(i + 1, NR) + 4 * i)
                        act.activation(xs[0:nh, :], x1[0:nh, i - 1, :], ACT.Copy, scale=stat[0:nh, 5:6]).then_inc(xs_ready, 1)
                    if i >= 2:
                        at, n = ROWS[i - 2]
                        act.wait_ge(h_shift, k - 1)
                        act.activation(h_hi[:, :, at:at + n], ht[:, :, 0:n], ACT.Copy).then_inc(h_hi_ready, 1)
                for unit, (kind, q) in enumerate(UNITS):
                    if kind == "ff1":
                        def part(n, oc, u, use):
                            act.wait_ge(squared, b * (4 * KT) + (q * KT) + oc + 1)
                            met(act, left)
                            act.activation(a_hi[:, q % 2, bass.ds(oc, 1), :].rearrange("p o c -> p (o c)"),
                                           sqf[:, u], ACT.Copy).then_inc(f_hi, 1)
                        chunks(act, b, unit, part)
                for i in range(NR):
                    n = ROWS[i][1]
                    m = b * (2 * NR) + (NR + i + 1)
                    act.wait_ge(turned, m)
                    square(n, ty[0:n, :], junk, 0, ssum)
                    log(n, 0, ssum, m, slog)
                    root(n, 0, slog, m, rstd)
                    if not last:
                        load(b + 1, i)
                        if i >= 2:
                            split(b + 1, i - 2)
                act.wait_ge(x_done, b * (2 * NR) + 2 * NR + 1)
                met(act, left)
                act.dma_start(d["y"][bass.ds(b * BP, BP), :].rearrange("(i p) c -> p i c", p=P),
                              x1[:, 0:BP // P, :]).then_inc(stored, 16)
                act.dma_start(d["y"][bass.ds(b * BS + SEQ, BS), :], x1[0:BS, BP // P, :]).then_inc(stored, 16)
                if not last:
                    for i in range(NR - 2, NR):
                        split(b + 1, i)
            for i in range(NR):
                load(0, i)
            for i in range(NR):
                split(0, i)
            blocks(act, body)
            act.wait_ge(stored, BLOCKS * 32 + 32)

        @block.vector
        def _(dve):
            dve.memset(stat[:, 0:1], 0.0).then_inc(split_lo, 2)
            dve.memset(stat[:, 1:2], 0.0).then_inc(product, 2)
            dve.memset(stat[:, 2:3], 0.0).then_inc(drained, 2)
            dve.memset(stat[:, 3:4], 0.0).then_inc(scaled, 1)
            dve.memset(stat[:, 4:5], 0.0).then_inc(h_mod, 1)
            dve.memset(stat[:, 5:6], 0.0).then_inc(left, 1)
            dve.memset(tmp[:, 0:1], 0.0).then_inc(stored, 32)
            dve.memset(tmp[:, 1:2], 0.0).then_inc(x_done, 1)
            dve.memset(tmp[:, 2:3], 0.0).then_inc(h_turned, 1)
            dve.wait_ge(const_in, 32)

            count = [0]

            def refine(b, n, at):
                ss, v, r = (stat[0:n, at + k:at + k + 1] for k in range(3))
                for ins in (lambda: dve.tensor_scalar(v, ss, 1.0 / D, EPS, ALU.mult, ALU.add),
                            lambda: dve.scalar_tensor_tensor(v, r, v, r, ALU.mult, ALU.mult),
                            lambda: dve.tensor_scalar(v, v, -0.5, 1.5, ALU.mult, ALU.add),
                            lambda: dve.tensor_tensor(r, r, v, ALU.mult)):
                    count[0] += 1
                    ins().then_inc(refined, 1)
                    dve.wait_ge(refined, b * REFINES + count[0])

            def residual(b, i, second):
                n = ROWS[i][1]
                m = b * (2 * NR) + (second * NR + i)
                gate = gate_p[:, second, :] if n == P else gate_s[:, second, :]
                dve.wait_ge(x_done, m + 1)
                dve.scalar_tensor_tensor(tmp[0:n, :], ty[0:n, :], stat[0:n, 2:3], gate, ALU.mult,
                                         ALU.mult).then_inc(scaled, 1)
                dve.wait_ge(scaled, m + 2)
                dve.tensor_tensor(x1[0:n, i, :], x1[0:n, i, :], tmp[0:n, :], ALU.add).then_inc(x_done, 1)

            def refine_out(b, i, second):
                dve.wait_ge(rstd, b * (2 * NR) + (second * NR + i + 1))
                refine(b, ROWS[i][1], 0)

            def split(b, i):
                at, n = ROWS[i]
                dve.wait_ge(in_hi, b * NR + i + 1)
                dve.tensor_tensor(a_lo[:, 0, :, at:at + n], out[:, :, at:at + n], a_hi[:, 0, :, at:at + n].bitcast(F32),
                                  ALU.subtract).then_inc(in_lo, 1)

            def body(b, last):
                count[0] = 0
                for unit, (kind, q) in enumerate(UNITS):
                    def drain(n, oc, u, use):
                        dve.wait_ge(product, n + 3)
                        dst = out[:, bass.ds(oc, 1), :].rearrange("p o (g c) -> p (o g) c", g=2)
                        src = acc[:, u, :, 0:G]
                        dve.wait_ge(drained, n + 2)
                        if kind == "ff1":
                            sq = sqf[:, u].rearrange("p (g c) -> p g c", g=2)
                            dve.tensor_scalar(sq, src, 0.0, None, ALU.max).then_inc(drained, 1)
                            dve.wait_ge(drained, n + 3)
                            dve.tensor_tensor(sq, sq, sq, ALU.mult).then_inc(squared, 1)
                            dve.wait_ge(f_hi, b * (4 * KT) + (q * KT) + oc + 1)
                            dve.tensor_tensor(a_lo[:, q % 2, bass.ds(oc, 1), :].rearrange("p o c -> p (o c)"), sqf[:, u],
                                              a_hi[:, q % 2, bass.ds(oc, 1), :].rearrange("p o c -> p (o c)").bitcast(F32),
                                              ALU.subtract).then_inc(f_lo, 1)
                        elif kind == "ff2" and q:
                            dve.tensor_tensor(dst, dst, src, ALU.add).then_inc(drained, 1)
                        else:
                            dve.tensor_scalar(dst, src, 1.0, None, ALU.mult).then_inc(drained, 1)
                    chunks(dve, b, unit, drain)
                    if kind == "out":
                        dve.wait_ge(x_in, b * 48 + 48)
                        for i in range(NR + 3):
                            if i < NR:
                                refine_out(b, i, 0)
                            if 1 <= i <= NR:
                                dve.wait_ge(hrstd, b * NR + i)
                                refine(b, ROWS[i - 1][1], 3)
                            if i < NR:
                                residual(b, i, 0)
                            if i >= 3:
                                at, n = ROWS[i - 3]
                                dve.wait_ge(h_hi_ready, b * NR + i - 2)
                                dve.tensor_tensor(h_lo[:, :, at:at + n], ht[:, :, 0:n], h_hi[:, :, at:at + n].bitcast(F32),
                                                  ALU.subtract).then_inc(h_lo_ready, 1)
                            if 2 <= i < NR + 2:
                                n = ROWS[i - 2][1]
                                if n == P:
                                    s2, b2 = (keep[m][:, :, SAMP:SAMP + 1].broadcast_to([P, KT, P]) for m in ("A2", "B2"))
                                else:
                                    s2, b2 = (keep[m][:, :, bass.ds(b * BS, BS)] for m in ("A2", "B2"))
                                dve.wait_ge(h_turned, b * NR + i)
                                if i >= 3:
                                    dve.wait_ge(h_lo_ready, b * NR + i - 2)
                                dve.tensor_tensor(ht[:, :, 0:n], th[:, :, 0:n], s2, ALU.mult).then_inc(h_mod, 1)
                                dve.wait_ge(h_mod, b * NR + i)
                                dve.tensor_tensor(ht[:, :, 0:n], ht[:, :, 0:n], b2, ALU.add).then_inc(h_shift, 1)
                for i in range(NR):
                    refine_out(b, i, 1)
                    residual(b, i, 1)
                    if not last and i >= 2:
                        split(b + 1, i - 2)
                dve.wait_ge(x_done, b * (2 * NR) + 2 * NR + 1)
                dve.tensor_copy(tmp[:, 0:1], tmp[:, 1:2]).then_inc(left, 1)
                if not last:
                    for i in range(NR - 2, NR):
                        split(b + 1, i)
            for i in range(NR):
                split(0, i)
            blocks(dve, body)


def program(nc, d):
    with ExitStack() as ctx:
        sb = lambda n, s, t=F32: ctx.enter_context(nc.sbuf_tensor(n, s, t))
        keep = {n: sb(n, [P, KT, MODROWS]) for n in ("A2", "B2")}
        keep["ident"] = sb("ident", [P, P])
        cols = sb("cols", [P, NCOLS])
        keep["cols"] = cols
        v = lambda a, n, k: cols[:, a:a + n].rearrange("p (a b) -> p a b", a=k)
        keep["zcols"] = v(16, 2 * NCOL, 2)
        keep["ogate"] = v(16 + 66, 24, 3)
        keep["qscale"] = cols[:, 106:112]
        keep["convw"] = v(112, 36, 4)
        keep["eps"] = cols[:, 150:151]
        keep["lbl"] = cols[:, 148:150]
        with ExitStack() as c2:
            sb2 = lambda n, s, t=F32: c2.enter_context(nc.sbuf_tensor(n, s, t))
            keep["A1"], keep["B1"] = sb2("A1", [P, KT, MODROWS]), sb2("B1", [P, KT, MODROWS])
            keep["headsum"] = sb2("headsum", [P, P])
            modulation(nc, d, keep)
            hi, lo = sb2("hi", [P, KT, TOK], F32R), sb2("lo", [P, KT, TOK], F32R)
            norm_in(nc, d, keep, hi, lo)
            project_in(nc, d, keep, hi, lo)
        with ExitStack() as c2:
            sb2 = lambda n, s, t=F32: c2.enter_context(nc.sbuf_tensor(n, s, t))
            keep["cols_p"] = sb2("cols_p", [P, NQ, TILES * MH])
            keep["cols_s"] = sb2("cols_s", [SAMP, NQ, MH])
            gates(nc, d, keep)
            mixers(nc, d, keep, False)
            mixers(nc, d, keep, True)
        feed_forward(nc, d, keep)


def lay_out(i):
    f = np.ascontiguousarray
    a = {n: np.asarray(v) for n, v in i.items()}
    z = lambda *s: np.zeros(s, np.float32)
    square = lambda w, n: w.reshape(KT, P, n, P).transpose(2, 1, 0, 3)
    c = np.concatenate([np.repeat(a["c_sample"], NT, axis=0), a["c_prompt"]])
    order = in_order()
    w_in = np.concatenate([a["w_in"][0], z(D, 1)], axis=1)[:, order]
    b_in = np.concatenate([a["b_in"][0], z(1)])[order]
    scale = np.ones((P, NCOL), np.float32)
    scale[:, 1 + R_MK:1 + R_MV] = HD ** -0.5
    n = a["mix_out_norm"][0]
    gate = np.stack([np.tile(np.array([0] * 3 + [1] * 5, np.float32), (P, 1)),
                     np.tile(np.array([1] * 3 + [0] * 5, np.float32), (P, 1)), n.reshape(8, P).T], 1)
    convw = a["gdn_conv_w"][0].reshape(CONV, 9, P).transpose(2, 0, 1)
    qscale = np.tile(np.array([HD ** -0.5] * 3 + [1.0] * 3, np.float32), (P, 1))
    cols = np.concatenate([a["norm_pre_mix"][0].reshape(KT, P).T, a["norm_pre_ffn"][0].reshape(KT, P).T, scale,
                           b_in.reshape(NCOL, P).T, gate.reshape(P, 24), qscale, convw.reshape(P, 36),
                           a["hgrn_lb_logits"][0].reshape(2, P).T, np.full((P, 1), EPS, np.float32)], axis=1)
    hist = a["state_gdn_conv"][0].reshape(NB, CONV - 1, 9, P).transpose(2, 3, 0, 1)
    ff1 = square(a["w_ff1"][0], DFF // P).reshape(4, 8, P, KT, P)
    ff2 = a["w_ff2"][0].reshape(4, KT, P, 8, P).transpose(0, 3, 2, 1, 4)
    units = np.concatenate([square(a["w_out"][0], 8)[None], np.stack([ff1, ff2], 1).reshape(8, 8, P, KT, P)])
    gcol = np.stack([a[n][0][HEADS] for n in ("mlstm_f_bias", "gdn_A_log", "gdn_dt_bias")], 1)
    o = {
        "gcol_p": np.tile(gcol, (TILES, 1)), "gcol_s": gcol, "m0": a["state_mlstm_m"][0].T[HEADS],
        "x": np.concatenate([a["x_prompt"][0], a["x_sample"].reshape(SAMP, D)]),
        "cT": c.T.reshape(KT, P, MODROWS).transpose(1, 0, 2),
        "w_ada": a["w_ada"][0].reshape(KT, P, ADA_CHUNKS, ADA_CHUNK).transpose(2, 1, 0, 3),
        "b_ada": a["b_ada"], "norm_post_mix": a["norm_post_mix"], "norm_post_ffn": a["norm_post_ffn"],
        "cols": cols, "ident": np.eye(P, dtype=np.float32),
        "headsum": np.kron(np.eye(P // HD), np.ones((HD, HD))).astype(np.float32),
        "w_in": square(w_in, NCOL), "hist": hist, "w_unit": units.reshape(9, 8, P, D),
    }
    s, t = np.arange(P)[:, None], np.arange(P)[None, :]
    pairs = [s == t] + [(s // n == t // n) & (s % n < n // 2) & (t % n >= n // 2) for n in (2 << l for l in range(LEVELS))]
    same = (s // NT == t // NT) & (s < SAMP) & (t < SAMP)
    o["level"] = np.stack(pairs, 1).astype(np.float32)
    o["late"] = np.stack([np.stack([np.where((s <= t) & ok, 0, -1e30), (s < t) & ok], 1) for ok in (s >= 0, same)]
                         ).astype(np.float32)
    seq = (np.arange(P)[None, :] // NT == np.arange(NB)[:, None]).astype(np.float32)
    o["one_t"], o["one_s"] = np.broadcast_to(seq, (P, NB, P)), seq.T
    rows = lambda w, n: w.reshape(NB, n, 2, HD, -1).transpose(2, 3, 1, 0, 4).reshape(P, n, NB, -1)
    o["s_cm"], o["s_gs"] = rows(a["state_mlstm_C"][0], 3), rows(a["state_gdn_S"][0], 3)
    o["s_hs"], o["s_nm"] = rows(a["state_hgrn_S"][0], 2), rows(a["state_mlstm_n"][0][..., None], 3)[..., 0]
    return {k: f(v) for k, v in o.items()}


INTERNAL = {
    "gates": (MODROWS, 2, D), "z": (TILES, P, NROW, P), "z_s": (P, NROW, SAMP), "gz": (4 * MH, TOK), "ends": (2, TILES * MH),
    "mprev": (TILES * MH,), "rows_p": (TILES, MH, 3, P), "rows_s": (MH, 3, SAMP), "dec_p": (2, TILES * MH),
    "dec_s": (2, MH, NB), "yT": (TILES, P, KT, P), "yT_s": (P, KT, SAMP),
}
OUTPUTS = {
    "y": (TOK, D), "p_conv": (9, P, CONV - 1), "s_conv": (9, P, NB, CONV - 1), "p_m": (MH, 1), "s_m": (MH, NB),
    "o_p_cm": (P, 3, HD + 1), "o_p_gs": (P, 3, HD), "o_p_hs": (P, 2, HD), "o_s_cm": (P, 3, NB, HD),
    "o_s_nm": (P, 3, NB), "o_s_gs": (P, 3, NB, HD), "o_s_hs": (P, 2, NB, HD),
}


def give_back(o):
    f = np.ascontiguousarray
    where = np.argsort(HEADS)
    prompt = lambda a, n: a.reshape(2, HD, n, -1).transpose(2, 0, 1, 3).reshape(1, 1, 2 * n, HD, -1)
    sample = lambda a, n: a.reshape(2, HD, n, NB, -1).transpose(3, 2, 0, 1, 4).reshape(1, NB, 2 * n, HD, -1)
    cm = prompt(o["o_p_cm"], 3)
    return tuple(f(a) for a in (
        o["y"][:SEQ].reshape(1, SEQ, D), o["y"][SEQ:].reshape(NB, NT, D),
        cm[..., :HD], cm[..., HD], o["p_m"][where, 0].reshape(1, 1, MH), prompt(o["o_p_gs"], 3),
        o["p_conv"].transpose(2, 0, 1).reshape(1, 1, CONV - 1, 9 * P), prompt(o["o_p_hs"], 2),
        sample(o["o_s_cm"], 3), sample(o["o_s_nm"], 3)[..., 0], o["s_m"][where].T.reshape(1, NB, MH),
        sample(o["o_s_gs"], 3), o["s_conv"].transpose(2, 3, 0, 1).reshape(1, NB, CONV - 1, 9 * P),
        sample(o["o_s_hs"], 2)))


def kernel(**inputs):
    import concourse.bacc as bacc
    from concourse.bass_utils import run_bass_kernel_spmd

    arrays = {"in_" + k: v for k, v in lay_out(inputs).items()}
    nc = bacc.Bacc("TRN2", target_bir_lowering=False, num_devices=1)
    d = {k[3:]: nc.dram_tensor(k, v.shape, mybir.dt.from_np(v.dtype), kind="ExternalInput").ap()
         for k, v in arrays.items()}
    for k, shape in INTERNAL.items():
        d[k] = nc.dram_tensor("tmp_" + k, shape, F32, kind="Internal").ap()
    for k, shape in OUTPUTS.items():
        d[k] = nc.dram_tensor("out_" + k, shape, F32, kind="ExternalOutput").ap()
    program(nc, d)
    r = run_bass_kernel_spmd(nc, [arrays], core_ids=[0])
    return give_back({k: np.asarray(r.results[0]["out_" + k]) for k in OUTPUTS})
```
